# Optimizing a Trainium2 kernel written in Bass

```python
import math
import jax
import jax.numpy as jnp
from jax import lax
import numpy as np

D_MODEL = 1024
BATCH = 1
SEQ = 128
DEPTH = 2
DEC_BATCH = 1
DEC_SEQ = 256
PAST_LEN = 128

GRID_W = 64
FN_WIDTH = D_MODEL // 4
FN_GROUPS = 4
FN_GROUP_DIM = FN_WIDTH // FN_GROUPS
DA_WIDTH = D_MODEL // 2
DA_HEADS = 4
DA_VDIM = DA_WIDTH // DA_HEADS
DA_HALF = DA_VDIM // 2
HG_WIDTH = D_MODEL // 4
HG_HEADS = 4
HG_DK = HG_WIDTH // HG_HEADS
HG_DV = HG_WIDTH // HG_HEADS
MIX_WIDTH = FN_WIDTH + DA_WIDTH + HG_WIDTH
PROJ_WIDTH = FN_WIDTH + 3 * DA_WIDTH + 5 * HG_WIDTH
CHUNK = 64
Q_BLOCK = 128
ROPE_THETA = 10000.0
N_EXPERTS = 64
TOP_K = 8
N_GROUPS = 8
TOPK_GROUPS = 4
D_EXPERT = 128
D_SHARED = 128
ROUTED_SCALE = 2.5
EPS = 1e-6

kernel_name = "hybrid_fnet_diffattn_hgrn2_moe_dit_step"

def _rmsnorm(x, g):
    xf = x.astype(jnp.float32)
    y = xf * lax.rsqrt(jnp.mean(xf * xf, axis=-1, keepdims=True) + EPS)
    return (y * g.astype(jnp.float32)).astype(x.dtype)

def _axial_rope(n_tokens):
    rows = n_tokens // GRID_W
    row = jnp.repeat(jnp.arange(rows, dtype=jnp.float32), GRID_W)
    col = jnp.tile(jnp.arange(GRID_W, dtype=jnp.float32), rows)
    axis_dim = DA_HALF // 2
    inv_freq = ROPE_THETA ** (-jnp.arange(0, axis_dim, 2, dtype=jnp.float32) / axis_dim)
    ang_r = row[:, None] * inv_freq[None, :]
    ang_c = col[:, None] * inv_freq[None, :]
    ang = jnp.concatenate([ang_r, ang_r, ang_c, ang_c], axis=-1)
    return jnp.cos(ang), jnp.sin(ang)

def _apply_rope(x, cos, sin):
    xf = x.astype(jnp.float32)
    x1, x2, x3, x4 = jnp.split(xf, 4, axis=-1)
    rot = jnp.concatenate([-x2, x1, -x4, x3], axis=-1)
    c = cos[None, :, None, None, :]
    s = sin[None, :, None, None, :]
    return (xf * c + rot * s).astype(x.dtype)

def _diff_attention(q, k, v, lam):
    b, lq = q.shape[0], q.shape[1]
    nb = lq // Q_BLOCK
    qb = q.reshape(b, nb, Q_BLOCK, DA_HEADS, 2, DA_HALF).swapaxes(0, 1)
    kf = k.astype(jnp.float32)
    vf = v.astype(jnp.float32)
    scale = DA_HALF ** -0.5

    def block(qblk):
        s = jnp.einsum('bqhmd,bkhmd->bmhqk', qblk.astype(jnp.float32), kf) * scale
        p = jax.nn.softmax(s, axis=-1)
        w = p[:, 0] - lam * p[:, 1]
        return jnp.einsum('bhqk,bkhd->bqhd', w, vf)

    o = lax.map(block, qb)
    return o.swapaxes(0, 1).reshape(b, lq, DA_HEADS, DA_VDIM)

def _fourier_mixer(u, w):
    b, l, _ = u.shape
    z = u.astype(jnp.float32).reshape(b, l, FN_GROUPS, FN_GROUP_DIM)
    z = jnp.fft.fft2(z, axes=(1, 3), norm='ortho').real
    return z.reshape(b, l, FN_WIDTH).astype(u.dtype) @ w

def _gla_chunk_scan(q, k, v, logf, s0):
    b, l, h, _ = q.shape
    n = l // CHUNK

    def to_chunks(t):
        return t.reshape(b, n, CHUNK, h, t.shape[-1]).transpose(1, 0, 3, 2, 4)

    causal = jnp.tril(jnp.ones((CHUNK, CHUNK), dtype=bool))[None, None, :, :, None]

    def step(s, inp):
        qc, kc, vc, gc = inp
        cum = jnp.cumsum(gc, axis=2)
        o_inter = jnp.einsum('bhtk,bhkv->bhtv', qc * jnp.exp(cum), s)
        dec = jnp.where(causal, cum[:, :, :, None, :] - cum[:, :, None, :, :], -jnp.inf)
        a = jnp.einsum('bhtk,bhsk,bhtsk->bhts', qc, kc, jnp.exp(dec))
        o = o_inter + jnp.einsum('bhts,bhsv->bhtv', a, vc)
        last = cum[:, :, -1:, :]
        s_new = jnp.exp(last[:, :, 0, :])[..., None] * s + jnp.einsum('bhsk,bhsv->bhkv', kc * jnp.exp(last - cum), vc)
        return s_new, o

    s_fin, o = lax.scan(step, s0, (to_chunks(q), to_chunks(k), to_chunks(v), to_chunks(logf)))
    o = o.transpose(1, 0, 3, 2, 4).reshape(b, l, h, v.shape[-1])
    return o, s_fin

def _hgrn2_mixer(hq, hi, hf_fwd, hf_bwd, hg, lb, norm_g, s0_fwd, s0_bwd):
    b, l, _ = hq.shape
    shp = (b, l, HG_HEADS, HG_DK)
    q = jax.nn.silu(hq.astype(jnp.float32)).reshape(shp) * (HG_DK ** -0.5)
    v = hi.astype(jnp.float32).reshape(b, l, HG_HEADS, HG_DV)
    outs = []
    finals = []
    for d, (fp, s0) in enumerate(((hf_fwd, s0_fwd), (hf_bwd, s0_bwd))):
        fpf = fp.astype(jnp.float32).reshape(shp)
        lbd = lb[d].astype(jnp.float32).reshape(HG_HEADS, HG_DK)
        logf = jnp.logaddexp(jnp.log(lbd), jnp.log1p(-lbd) + jax.nn.log_sigmoid(fpf))
        kk = (1.0 - lbd) * jax.nn.sigmoid(-fpf)
        if d == 1:
            qd, kd, vd, gd = (jnp.flip(t, axis=1) for t in (q, kk, v, logf))
        else:
            qd, kd, vd, gd = q, kk, v, logf
        o, s_fin = _gla_chunk_scan(qd, kd, vd, gd, s0.astype(jnp.float32))
        if d == 1:
            o = jnp.flip(o, axis=1)
        outs.append(o)
        finals.append(s_fin)
    o = _rmsnorm(outs[0] + outs[1], norm_g) * jax.nn.silu(hg.astype(jnp.float32).reshape(b, l, HG_HEADS, HG_DV))
    return o.reshape(b, l, HG_WIDTH).astype(hq.dtype), finals[0], finals[1]

def _moe(h, p):
    t = h.shape[0]
    scores = jax.nn.sigmoid((h @ p['w_router']).astype(jnp.float32))
    biased = scores + p['router_bias'].astype(jnp.float32)
    per_group = N_EXPERTS // N_GROUPS
    gscore = lax.top_k(biased.reshape(t, N_GROUPS, per_group), 2)[0].sum(-1)
    _, gidx = lax.top_k(gscore, TOPK_GROUPS)
    gmask = jnp.sum(jax.nn.one_hot(gidx, N_GROUPS, dtype=jnp.float32), axis=1) > 0.0
    emask = jnp.repeat(gmask, per_group, axis=1)
    _, eidx = lax.top_k(jnp.where(emask, biased, -jnp.inf), TOP_K)
    w = jnp.take_along_axis(scores, eidx, axis=1)
    w = w / jnp.sum(w, axis=-1, keepdims=True) * ROUTED_SCALE
    gates = jnp.sum(jax.nn.one_hot(eidx, N_EXPERTS, dtype=jnp.float32) * w[..., None], axis=1)
    hg = jnp.einsum('td,edf->tef', h, p['w_gate'])
    hu = jnp.einsum('td,edf->tef', h, p['w_up'])
    act = jax.nn.silu(hg) * hu * gates[:, :, None].astype(h.dtype)
    routed = jnp.einsum('tef,efd->td', act, p['w_down'])
    shared = (jax.nn.silu(h @ p['ws_gate']) * (h @ p['ws_up'])) @ p['ws_down']
    return routed + shared

def _trunk_layer(x, mod, layer_idx, p, ctx=None):
    b, l, _ = x.shape
    sh1, sc1, g1, sh2, sc2, g2 = jnp.split(mod[:, None, :], 6, axis=-1)
    h = _rmsnorm(x, p['norm_g'][0]) * (1 + sc1) + sh1
    proj = h @ p['w_in']
    widths = [FN_WIDTH, DA_WIDTH, DA_WIDTH, DA_WIDTH, HG_WIDTH, HG_WIDTH, HG_WIDTH, HG_WIDTH]
    cuts = [int(v) for v in np.cumsum(widths)]
    u_fn, u_q, u_k, u_v, hq, hi, hf_fwd, hf_bwd, hg = jnp.split(proj, cuts, axis=-1)

    fn_out = _fourier_mixer(u_fn, p['w_fourier'])

    q = u_q.reshape(b, l, DA_HEADS, 2, DA_HALF)
    k = u_k.reshape(b, l, DA_HEADS, 2, DA_HALF)
    v = u_v.reshape(b, l, DA_HEADS, DA_VDIM)
    lam_init = 0.8 - 0.6 * math.exp(-0.3 * layer_idx)
    lmb = p['lambdas'].astype(jnp.float32)
    lam = jnp.exp(jnp.sum(lmb[0] * lmb[1])) - jnp.exp(jnp.sum(lmb[2] * lmb[3])) + lam_init
    if ctx is None:
        a = _diff_attention(q, k, v, lam)
        s0_fwd = jnp.zeros((b, HG_HEADS, HG_DK, HG_DV), jnp.float32)
        s0_bwd = s0_fwd
    else:
        cos, sin, k_ctx, v_ctx, s_ctx = ctx
        q = _apply_rope(q, cos, sin)
        k_lat = _apply_rope(k, cos, sin)
        k_all = jnp.concatenate([k_lat, k_ctx.reshape(b, -1, DA_HEADS, 2, DA_HALF).astype(k.dtype)], axis=1)
        v_all = jnp.concatenate([v, v_ctx.astype(v.dtype)], axis=1)
        a = _diff_attention(q, k_all, v_all, lam)
        s0_fwd, s0_bwd = s_ctx[:, 0], s_ctx[:, 1]
    a = (_rmsnorm(a, p['attn_norm_g']) * (1.0 - lam_init)).reshape(b, l, DA_WIDTH).astype(x.dtype)

    hg_out, s_fwd, s_bwd = _hgrn2_mixer(hq, hi, hf_fwd, hf_bwd, hg, p['lb'], p['hg_norm_g'], s0_fwd, s0_bwd)

    mix = jnp.concatenate([fn_out, a, hg_out], axis=-1) @ p['w_out']
    x = x + g1 * mix
    h2 = _rmsnorm(x, p['norm_g'][1]) * (1 + sc2) + sh2
    x = x + g2 * _moe(h2.reshape(b * l, D_MODEL), p).reshape(b, l, D_MODEL)
    if ctx is None:
        new_ctx = (k.reshape(b, l, DA_HEADS, 2 * DA_HALF), v, jnp.stack([s_fwd, s_bwd], axis=1))
        return x, new_ctx
    return x, None

def setup_inputs(seed: int = 0) -> dict:
    key = jax.random.key(seed)
    ks = jax.random.split(key, 26)

    def nrm(k, shape, s):
        return jax.random.normal(k, shape, jnp.float32) * s

    return {
        'x_prompt': nrm(ks[0], (BATCH, SEQ, D_MODEL), 1.0),
        'x_sample': nrm(ks[1], (DEC_BATCH, DEC_SEQ, D_MODEL), 1.0),
        'cache_k': nrm(ks[2], (DEC_BATCH, DEPTH, PAST_LEN, DA_HEADS, 2 * DA_HALF), 1.0),
        'cache_v': nrm(ks[3], (DEC_BATCH, DEPTH, PAST_LEN, DA_HEADS, DA_VDIM), 1.0),
        'state_hgrn': nrm(ks[4], (DEC_BATCH, DEPTH, 2, HG_HEADS, HG_DK, HG_DV), 0.5),
        'c': nrm(ks[5], (DEC_BATCH, D_MODEL), 1.0),
        'c_ctx': nrm(ks[6], (D_MODEL,), 1.0),
        'w_ada': nrm(ks[7], (DEPTH, D_MODEL, 6 * D_MODEL), 0.5 * D_MODEL ** -0.5),
        'b_ada': nrm(ks[8], (DEPTH, 6 * D_MODEL), 0.02),
        'norm_g': 1.0 + nrm(ks[9], (DEPTH, 2, D_MODEL), 0.02),
        'w_in': nrm(ks[10], (DEPTH, D_MODEL, PROJ_WIDTH), D_MODEL ** -0.5),
        'w_fourier': nrm(ks[11], (DEPTH, FN_WIDTH, FN_WIDTH), FN_WIDTH ** -0.5),
        'lambdas': nrm(ks[12], (DEPTH, 4, DA_HALF), 0.1),
        'attn_norm_g': 1.0 + nrm(ks[13], (DEPTH, DA_VDIM), 0.02),
        'lower_bounds': nrm(ks[14], (DEPTH, 2, HG_WIDTH), 1.0),
        'hg_norm_g': 1.0 + nrm(ks[15], (DEPTH, HG_DV), 0.02),
        'w_out': nrm(ks[16], (DEPTH, MIX_WIDTH, D_MODEL), MIX_WIDTH ** -0.5),
        'w_router': nrm(ks[17], (DEPTH, D_MODEL, N_EXPERTS), D_MODEL ** -0.5),
        'router_bias': nrm(ks[18], (DEPTH, N_EXPERTS), 0.01),
        'w_gate': nrm(ks[19], (DEPTH, N_EXPERTS, D_MODEL, D_EXPERT), D_MODEL ** -0.5),
        'w_up': nrm(ks[20], (DEPTH, N_EXPERTS, D_MODEL, D_EXPERT), D_MODEL ** -0.5),
        'w_down': nrm(ks[21], (DEPTH, N_EXPERTS, D_EXPERT, D_MODEL), D_EXPERT ** -0.5),
        'ws_gate': nrm(ks[22], (DEPTH, D_MODEL, D_SHARED), D_MODEL ** -0.5),
        'ws_up': nrm(ks[23], (DEPTH, D_MODEL, D_SHARED), D_MODEL ** -0.5),
        'ws_down': nrm(ks[24], (DEPTH, D_SHARED, D_MODEL), D_SHARED ** -0.5),
        'final_g': 1.0 + nrm(ks[25], (D_MODEL,), 0.02),
    }

def reference(x_prompt, x_sample, cache_k, cache_v, state_hgrn, c, c_ctx, w_ada, b_ada, norm_g,
              w_in, w_fourier, lambdas, attn_norm_g, lower_bounds, hg_norm_g, w_out, w_router,
              router_bias, w_gate, w_up, w_down, ws_gate, ws_up, ws_down, final_g):
    cs = jnp.cumsum(jax.nn.softmax(lower_bounds.astype(jnp.float32), axis=0), axis=0)
    lbs = cs - cs[0:1]
    cos, sin = _axial_rope(x_sample.shape[1])
    xp, xs = x_prompt, x_sample
    new_k, new_v, new_s = [], [], []
    for l in range(DEPTH):
        p = {
            'norm_g': norm_g[l], 'w_in': w_in[l], 'w_fourier': w_fourier[l], 'lambdas': lambdas[l],
            'attn_norm_g': attn_norm_g[l], 'lb': lbs[l], 'hg_norm_g': hg_norm_g[l], 'w_out': w_out[l],
            'w_router': w_router[l], 'router_bias': router_bias[l], 'w_gate': w_gate[l], 'w_up': w_up[l],
            'w_down': w_down[l], 'ws_gate': ws_gate[l], 'ws_up': ws_up[l], 'ws_down': ws_down[l],
        }
        mod_ctx = (jax.nn.silu(c_ctx) @ w_ada[l] + b_ada[l])[None, :]
        xp, (kc, vc, sc) = _trunk_layer(xp, mod_ctx, l, p)
        new_k.append(kc)
        new_v.append(vc)
        new_s.append(sc)
        mod_lat = jax.nn.silu(c) @ w_ada[l] + b_ada[l]
        xs, _ = _trunk_layer(xs, mod_lat, l, p, (cos, sin, cache_k[:, l], cache_v[:, l], state_hgrn[:, l]))
    y_prompt = _rmsnorm(xp, final_g)
    y_sample = _rmsnorm(xs, final_g)
    new_cache_k = jnp.stack(new_k, axis=1)
    new_cache_v = jnp.stack(new_v, axis=1)
    new_state_hgrn = jnp.stack(new_s, axis=1)
    return (y_prompt, y_sample, new_cache_k, new_cache_v, new_state_hgrn)


_drawn_inputs = setup_inputs


def setup_inputs(seed=0):
    import zlib

    import numpy as np

    out = dict(_drawn_inputs(seed))
    spreads = {}
    factors = {'state_hgrn': 5.483, 'hg_norm_g': 2.892, 'final_g': 2.779}
    for name, (base, spread) in spreads.items():
        noise = np.random.default_rng([zlib.crc32(name.encode()), seed]).standard_normal(out[name].shape)
        drawn = base * np.exp(spread * noise) if base else spread * noise
        out[name] = jnp.asarray(drawn.astype(out[name].dtype))
    for name, factor in factors.items():
        out[name] = (out[name] * factor).astype(out[name].dtype)
    return out
```

```python
from contextlib import ExitStack

import concourse.bass as bass
from concourse import mybir

F32 = mybir.dt.float32
U8 = mybir.dt.uint8
ALU = mybir.AluOpType
ACT = mybir.ActivationFunctionType
AX = mybir.AxisListType

P = 128
EPS = 1e-6
ROUTED_SCALE = 2.5
TOPK_GROUPS = 4
LOG_DECAY_FLOOR = 2.0611536e-09
NEVER = 3.0e38
TAKEN = 3.3e38
HALVES = (64, 32, 16, 8)
BASE = 8
LAYER_DVE = 92
NSLOT = 4

CONST_COLS = (("ident", 128), ("tri_f", 128), ("tri_b", 128), ("past_f", 128), ("past_b", 128), ("rot", 128),
              ("c_ctx", 128), ("s_ctx", 128), ("c_chan", 128), ("s_chan", 128), ("cos", 256), ("sin", 256),
              ("c_lat", 512), ("s_lat", 512), ("tie", 64))


def const_offsets():
    out, at = {}, 0
    for name, width in CONST_COLS:
        out[name] = (at, at + width)
        at += width
    return out, at


class Signal:

    def __init__(self, sem, start=0, layer=1):
        self.sem, self.start, self.layer = sem, start, layer

    def at(self, l, n):
        return self.start + l * self.layer + n


class InOrder:

    def __init__(self, eng, sem, start, layer, depth):
        self.eng, self.sem, self.start, self.layer, self.depth = eng, sem, start, layer, depth
        self.base, self.n, self.seen = 0, 0, {}

    def enter(self, phase, l=0):
        self.seen[phase] = 0
        self.phase = phase
        self.base = {"start": 0, "layer": self.start + l * self.layer, "final": self.start + self.depth * self.layer}[phase]
        self.n = 0

    def leave(self):
        want = {"start": self.start, "layer": self.layer}.get(self.phase, self.n)
        assert self.n == want, (self.phase, self.n, want)

    def after(self, ins):
        self.n += 1
        ins.then_inc(self.sem, 1)
        self.eng.wait_ge(self.sem, self.base + self.n)


class Banks:

    def __init__(self, banks, full, empty, depth):
        self.banks, self.full_sem, self.empty_sem, self.depth = banks, full, empty, depth
        self.count = {"start": [0] * 8, "layer": [0] * 8, "final": [0] * 8}
        self.uses = {"start": {}, "layer": {}, "final": {}}
        self.turn = 0

    def plan(self, phase, stage, n, bank=None, each=1):
        for i in range(n):
            b = bank[i] if bank is not None else self.turn % 8
            if bank is None:
                self.turn += 1
            self.uses[phase][stage, i] = (b, self.count[phase][b])
            self.count[phase][b] += each

    def plan_one(self, phase, stage, i, bank):
        self.uses[phase][stage, i] = (bank, self.count[phase][bank])
        self.count[phase][bank] += 1

    def enter(self, phase, l=0):
        self.phase, self.l = phase, l

    def _at(self, stage, i, more):
        b, nth = self.uses[self.phase][stage, i]
        if self.phase != "start":
            nth = nth + self.count["start"][b]
        if self.phase == "layer":
            nth = self.l * self.count["layer"][b] + nth
        if self.phase == "final":
            nth = nth + self.depth * self.count["layer"][b]
        return b, nth + more

    def claim(self, pe, stage, i=0, more=0):
        b, v = self._at(stage, i, more)
        pe.wait_ge(self.empty_sem[b], v + 1)
        return self.banks[b]

    def filled(self, ins, stage, i=0):
        ins.then_inc(self.full_sem[self.uses[self.phase][stage, i][0]], 1)

    def read(self, eng, stage, i=0, more=0):
        b, v = self._at(stage, i, more + 1)
        eng.wait_ge(self.full_sem[b], v)
        return self.banks[b]

    def emptied(self, ins, stage, i=0):
        ins.then_inc(self.empty_sem[self.uses[self.phase][stage, i][0]], 1)

    def wait_emptied(self, eng, stage, i=0, more=0):
        b, v = self._at(stage, i, more + 1)
        eng.wait_ge(self.empty_sem[b], v + 1)


def trunk_program(nc, T, CF, CM, y_prompt, y_sample, new_k, new_v, new_state):
    DEPTH, _, _, DH, VD = T["cache_k"].shape[1], 0, 0, T["cache_k"].shape[3], T["cache_k"].shape[4]
    D = T["x_prompt"].shape[2]
    NJ = D // P
    NTILE = (T["x_prompt"].shape[1] + T["x_sample"].shape[1]) // P
    TOK = NTILE * P
    SPAN = (slice(0, P), slice(P, TOK))
    DK = VD // 2
    HH, HK = T["state_hgrn"].shape[3], T["state_hgrn"].shape[4]
    HW = HH * HK
    DA = DH * VD
    FN = T["w_fourier"].shape[1]
    E = T["w_router"].shape[2]
    NG = 8
    PG = E // NG
    PROJ = T["w_in"].shape[2]
    KEYS = TOK + T["cache_k"].shape[2]
    SCALE = DK ** -0.5
    Q0, K0, V0, HQ0, HI0, HB0 = FN, FN + DA, FN + 2 * DA, FN + 3 * DA, FN + 3 * DA + HW, FN + 3 * DA + 3 * HW
    assert PROJ == HB0 + 2 * HW and NTILE == 3 and D == 1024 and E % NSLOT == 0

    ctx = ExitStack()
    with ctx:
        def sb(name, shape, dt=F32):
            return ctx.enter_context(nc.sbuf_tensor(name, shape, dt))

        def sem(name):
            return ctx.enter_context(nc.semaphore(name))

        ring = sb("ring", [P, NSLOT, 4096])
        x = sb("x", [P, NJ, TOK])
        h = sb("h", [P, NJ, TOK])
        big = sb("big", [P, NJ * TOK])
        squares = big[:, :].rearrange("p (j t) -> p j t", j=NJ)
        mixT = squares
        rows = big[:, :].rearrange("p (i d) -> p i d", i=NTILE)
        aT = sb("aT", [P, 2, NTILE, 4 * P])
        w_shared = aT[:, :, :, :].rearrange("p d i t -> p (d i t)")
        work = sb("work", [P, 12 * TOK])

        def part(a, b, inner=TOK):
            return work[:, a * TOK:b * TOK].rearrange("p (c t) -> p c t", t=inner)

        hflat = h[:, :, :].rearrange("p j t -> p (j t)")
        rstd = sb("rstd", [P, TOK])
        rms = sb("rms", [P, TOK])
        consts = sb("consts", [P, CF.shape[1]])
        masks = sb("masks", [P, 2 * (len(HALVES) + 1), P], U8)
        masks_f = hflat[:, 0:2 * (len(HALVES) + 1) * P].rearrange("p (m t) -> p m t", t=P)
        ones = sb("ones", [P, P])
        eps_t = sb("eps_t", [P, 1])
        cond = sb("cond", [P, 2, NJ])
        scond = sb("scond", [P, NJ, 2])
        mod = sb("mod", [P, 6, NJ, 2])
        gain = sb("gain", [P, NJ, 2])
        b_ada = sb("b_ada", [P, 6, NJ])
        norm_g = sb("norm_g", [P, 2, NJ])
        attn_g = sb("attn_g", [P, VD])
        hg_g = sb("hg_g", [P, HK])
        lambdas = sb("lambdas", [P, 4, DK])
        lam_init = sb("lam_init", [P, 2])
        r_bias = sb("r_bias", [P, E])
        w_four = sb("w_four", [P, 2, FN])
        w_router = sb("w_router", [P, NJ, E])
        cache_k = sb("cache_k", [P, DA])
        cache_v = sb("cache_v", [P, DA])
        state0 = sb("state0", [P, 4, HK])
        final_g = sb("final_g", [P, NJ])
        lb_all = sb("lb_all", [P, DEPTH, 2 * HW])
        lb = sb("lb", [P, 2 * HW])
        om = sb("om", [P, 2 * HW])
        qT = sb("qT", [P, DH, TOK])
        kT = sb("kT", [P, DH, KEYS])
        val = sb("val", [P, NTILE, DA])
        k_rows = sb("k_rows", [P, DA])
        rot_t = sb("rot_t", [P, 2, 256])
        lam_p = sb("lam_p", [P, 2, DK])
        lam_s = sb("lam_s", [P, 2])
        neg_lam = sb("neg_lam", [P, 1])
        top = sb("top", [P, 2, 2])
        ntop = sb("ntop", [P, 2, 2])
        den = sb("den", [P, 2, 2])
        rden = sb("rden", [P, 2, 2])
        prob = hflat[:, 0:4 * TOK].rearrange("p (a m t) -> p a m t", a=2, m=2)
        wts = hflat[:, 4 * TOK:6 * TOK].rearrange("p (a t) -> p a t", a=2)
        wT = hflat[:, 6 * TOK:8 * TOK].rearrange("p (a t) -> p a t", a=2)
        logf = sb("logf", [P, NTILE, 2 * HW])
        att = logf
        att_r = sb("att_r", [P, 2, NTILE * DH])
        u_fn = sb("u_fn", [P, NTILE, FN])
        ho = u_fn
        four1 = part(0, 4)
        att_sq = part(0, 4, DA)
        zT = part(4, 6)
        hqT = sb("hqT", [P, 2, TOK])
        hv = sb("hv", [P, NTILE, HW])
        gate_o = sb("gate_o", [P, NTILE, HW])
        kk = part(6, 10, 2 * HW)
        kkT = hflat[:, 0:4 * TOK].rearrange("p (g t) -> p g t", g=4)
        cum = hflat[:, 4 * TOK:8 * TOK].rearrange("p (g t) -> p g t", g=4)
        qdec = big[:, 2 * TOK:6 * TOK].rearrange("p (g t) -> p g t", g=4)
        kdec = logf[:, :, :].rearrange("p i f -> p (i f)")[:, 0:4 * HW].rearrange("p (g f) -> p g f", g=4)
        diff = part(0, 2)
        fac = part(2, 4)
        fac2 = part(4, 6)
        pair = work[:, 6 * TOK:10 * TOK].rearrange("p (a c t) -> p a c t", a=2, c=2)
        pair2 = part(10, 12)
        st_out = sb("st_out", [P, 4, HK])
        st_mid = sb("st_mid", [P, 4, HK])
        ho_sq = big[:, 6 * TOK:8 * TOK].rearrange("p (i f) -> p i f", i=NTILE)
        ho_r = sb("ho_r", [P, 2, NTILE * HH])
        edge = sb("edge", [P, 4])
        tick = sb("tick", [P, 1])
        at = [0]

        def scratch(*shape):
            n = 1
            for k in shape:
                n *= k
            v = work[:, at[0]:at[0] + n]
            at[0] += n
            assert at[0] <= 8 * TOK
            return v.rearrange("p (a b) -> p a b", a=shape[0]) if len(shape) == 2 else v

        score, biased, gsel = scratch(NTILE, E), scratch(NTILE, E), scratch(NTILE, E)
        tops, gsum = scratch(NTILE * NG, 8), scratch(NTILE, NG)
        cmp_a, cmp_b = scratch(NTILE, NG * NG), scratch(NTILE, NG * NG)
        rank, gpen, best, wsum = scratch(NTILE * NG), scratch(NTILE * NG), scratch(NTILE, 8), scratch(NTILE)
        gatesT = sb("gatesT", [E, TOK])
        gate_b = work[:, 0:8 * TOK].rearrange("p (i s t) -> p i s t", i=2, s=NSLOT)
        sil = part(8, 10)
        act = part(10, 12)

        coff, _ = const_offsets()

        def const(name):
            a, b = coff[name]
            return consts[:, a:b]

        ident = const("ident")
        gates_dram = nc.dram_tensor("gates_scratch", (E, TOK), F32, kind="Internal").ap()

        banks = Banks([ctx.enter_context(nc.psum_tensor(f"bank{b}", [P, 512], F32)) for b in range(8)],
                      [sem(f"bank{b}_full") for b in range(8)], [sem(f"bank{b}_empty") for b in range(8)], DEPTH)
        LEVELS = len(HALVES) + 1
        banks.plan("start", "xT", 2 * NTILE)
        for stage, n in (("ms1", 1), ("mod", 1), ("q", DH), ("k", DH), ("v", NTILE), ("fn", NTILE), ("hq", 2),
                         ("hif", NTILE), ("hbg", NTILE), ("k_rows", 1), ("ckT", 1), ("rotq", 2), ("rotk", 2),
                         ("four1", 4), ("zT", 2), ("fnT", 2), ("kkT", 4), ("cum", 4), ("past", 2),
                         ("lev", 4 * LEVELS * NTILE), ("st", 2), ("ho", 2)):
            banks.plan("layer", stage, n)
        UNITS = [(t, hd) for t in range(NTILE) for hd in range(DH)]
        NU = len(UNITS)
        ring6 = 0
        for u in range(NU + 3):
            if u < NU:
                for m in range(2):
                    banks.plan_one("layer", "sc", 2 * u + m, ring6 % 6)
                    ring6 += 1
            if 2 <= u < NU + 2:
                banks.plan_one("layer", "wT", u - 2, ring6 % 6)
                ring6 += 1
            if u >= 3 and UNITS[u - 3][1] == 0:
                banks.plan_one("layer", "o", UNITS[u - 3][0], 6 + UNITS[u - 3][0] % 2)
        for stage, n in (("oT", NTILE), ("hgT", 2)):
            banks.plan("layer", stage, n)
        banks.turn = 0
        for stage, n in (("out", NJ), ("ms2", 1), ("router", 1), ("gT", 1)):
            banks.plan("layer", stage, n)
        banks.plan("layer", "G", 1, [6], each=E + 1)
        banks.plan("layer", "U", 1, [7], each=E + 1)
        banks.plan("layer", "y", 6, range(6))
        banks.turn = 0
        banks.plan("layer", "yT", NJ)
        banks.plan("final", "ms", 1)
        banks.plan("final", "rows", 2 * NTILE)

        waited = sem("waited")
        consts_in = sem("consts_in")
        params_in = sem("params_in")
        slot_full = [sem(f"slot{s}_full") for s in range(NSLOT)]
        slot_read = sem("slot_read")
        aT_zero = Signal(sem("aT_zero"))
        shared_in = sem("shared_in")
        gates_out = sem("gates_out")
        gate_in = [sem(f"gate{i}_in") for i in range(2)]
        results_out = sem("results_out")
        y_out = sem("y_out")
        squared = Signal(sem("squared"), 0, 2)
        h_ready = Signal(sem("h_ready"), 0, 2)
        scond_ready = sem("scond_ready")
        ones_ready = sem("ones_ready")
        rope_done = Signal(sem("rope_done"))
        fgate_ready = Signal(sem("fgate_ready"))
        logf_ready = Signal(sem("logf_ready"))
        kk_ready = Signal(sem("kk_ready"))
        lam_sum = Signal(sem("lam_sum"))
        lam_exp = Signal(sem("lam_exp"))
        ecum_ready = Signal(sem("ecum_ready"))
        qdec_ready = Signal(sem("qdec_ready"))
        kdec_ready = Signal(sem("kdec_ready"))
        NLEV = 2 * LEVELS
        diff_ready = Signal(sem("diff_ready"), 0, NLEV)
        fac_ready = Signal(sem("fac_ready"), 0, NLEV)
        pair_ready = Signal(sem("pair_ready"), 0, NLEV)
        sums_ready = Signal(sem("sums_ready"))
        roots_ready = Signal(sem("roots_ready"))
        hnorm_ready = Signal(sem("hnorm_ready"))
        ntop_ready = Signal(sem("ntop_ready"), 0, NU)
        wts_ready = Signal(sem("wts_ready"), 0, NU)
        anorm_ready = Signal(sem("anorm_ready"))
        gsel_ready = Signal(sem("gsel_ready"))
        act_ready = Signal(sem("act_ready"), 0, E + 1)
        x_ready = Signal(sem("x_ready"), 1, 2)
        final_ready = sem("final_ready")
        lb_diff = sem("lb_diff")
        lb_exp = sem("lb_exp")
        dve_order, act_order = sem("dve_order"), sem("act_order")

        w_ada_v = T["w_ada"].rearrange("l (p j) n -> l p j n", j=NJ)
        w_in_v = T["w_in"].rearrange("l (p j) n -> l p j n", j=NJ)
        w_out_v = T["w_out"].rearrange("l (c p) n -> l p c n", p=P)
        w_gate_v = T["w_gate"].rearrange("l e (p j) f -> l e p (j f)", j=NJ)
        w_up_v = T["w_up"].rearrange("l e (p j) f -> l e p (j f)", j=NJ)
        w_down_v = T["w_down"]

        def in_cols(l, c0, n):
            return w_in_v[l][:, :, c0:c0 + n]

        fixed = []
        for m in range(6):
            for half in range(2):
                fixed.append(("ada", [(4, 1024, 0, lambda l, m=m, half=half:
                                       w_ada_v[l][:, 4 * half:4 * half + 4, m * D:(m + 1) * D])]))
        for name, c0 in (("q", Q0), ("k", K0), ("v", V0)):
            fixed.append((name, [(NJ, 512, 0, lambda l, c0=c0: in_cols(l, c0, 512))]))
        fixed.append(("fn+hq", [(NJ, 256, 0, lambda l: in_cols(l, 0, 256)), (NJ, 256, 2048, lambda l: in_cols(l, HQ0, 256))]))
        fixed.append(("hif", [(NJ, 512, 0, lambda l: in_cols(l, HI0, 512))]))
        fixed.append(("hbg", [(NJ, 512, 0, lambda l: in_cols(l, HB0, 512))]))
        for half in range(2):
            fixed.append(("out", [(4, 1024, 0, lambda l, half=half: w_out_v[l][:, 4 * half:4 * half + 4, :])]))
        NFIX = len(fixed)
        NBLK = NFIX + E
        assert NFIX % NSLOT == 0
        landed, fix_sum = [], [0] * NSLOT
        for b, (_, parts) in enumerate(fixed):
            fix_sum[b % NSLOT] += 16 * len(parts)
            landed.append(fix_sum[b % NSLOT])
        slot_layer = [fix_sum[s] + 48 * (E // NSLOT) for s in range(NSLOT)]

        def block_in(eng, l, b):
            eng.wait_ge(slot_full[b % NSLOT], l * slot_layer[b % NSLOT] + landed[b])
            return ring[:, b % NSLOT, :]

        FIX_READS = 12
        READS = FIX_READS + E - 1
        SPARE = NSLOT - 1
        last_fill = {11: ("mod", 0), 12: ("q", DH - 1), 13: ("k", DH - 1), 14: ("v", NTILE - 1), 15: ("hq", 1),
                     16: ("hif", NTILE - 1), 17: ("hbg", NTILE - 1), 19: ("out", NJ - 1)}

        def slot_released(sp, l, b):
            prev = b - NSLOT
            if prev == -1:
                sp.wait_ge(x_ready.sem, x_ready.at(l, 0))
            elif prev in last_fill:
                banks.read(sp, *last_fill[prev])
            else:
                reads = prev + 2 if prev < 0 else prev + 1 if prev < 11 else FIX_READS
                sp.wait_ge(slot_read, l * READS + (reads + SPARE))
            apart(sp)

        NCONST, NPARAM = 8, 12

        def apart(eng):
            eng.sem_inc(waited, 1)

        block = ctx.enter_context(nc.Block())

        @block.sync
        def _(sp):
            sp.sem_inc(slot_read, SPARE)
            sp.dma_start(rows[:, 0, :], T["x_prompt"][0]).then_inc(consts_in, 16)
            sp.dma_start(rows[:, 1:3, :], T["x_sample"][0].rearrange("(i p) d -> p i d", p=P)).then_inc(consts_in, 16)
            sp.dma_start(consts[:, :], CF).then_inc(consts_in, 16)
            sp.dma_start(masks_f, CM.rearrange("m p t -> p m t")).then_inc(consts_in, 16)
            sp.dma_start(cond[:, 0, :], T["c_ctx"].rearrange("(p j) -> p j", j=NJ)).then_inc(consts_in, 16)
            sp.dma_start(cond[:, 1, :], T["c"][0].rearrange("(p j) -> p j", j=NJ)).then_inc(consts_in, 16)
            sp.dma_start(final_g[:, :], T["final_g"].rearrange("(p j) -> p j", j=NJ)).then_inc(consts_in, 16)
            sp.dma_start(lb_all[:, :, :], T["lower_bounds"].rearrange("l d w -> l (d w)").partition_broadcast(P))\
              .then_inc(consts_in, 16)
            with sp.Fori(0, DEPTH) as l:
                banks.enter("layer", l)
                for b, (_, parts) in enumerate(fixed):
                    slot_released(sp, l, b)
                    for j, n, at, src in parts:
                        dst = ring[:, b % NSLOT, at:at + j * n].rearrange("p (j n) -> p j n", j=j)
                        sp.dma_start(dst, src(l)).then_inc(slot_full[b % NSLOT], 16)

                def load_expert(s, e):
                    sp.dma_start(ring[:, s, 0:D], w_gate_v[l, e]).then_inc(slot_full[s], 16)
                    sp.dma_start(ring[:, s, D:2 * D], w_up_v[l, e]).then_inc(slot_full[s], 16)
                    sp.dma_start(ring[:, s, 2 * D:3 * D], w_down_v[l, e]).then_inc(slot_full[s], 16)

                for s in range(NSLOT):
                    slot_released(sp, l, NFIX + s)
                    load_expert(s, s)
                with sp.Fori(1, E // NSLOT) as turn:
                    for s in range(NSLOT):
                        sp.wait_ge(slot_read, l * READS + (turn * NSLOT) + (s + 1 + SPARE + FIX_READS - NSLOT))
                        load_expert(s, turn * NSLOT + s)
            banks.enter("final")
            for i in range(2 * NTILE):
                banks.wait_emptied(sp, "rows", i)
            sp.dma_start(y_prompt[0], rows[:, 0, :]).then_inc(y_out, 16)
            sp.dma_start(y_sample[0].rearrange("(i p) d -> p i d", p=P), rows[:, 1:3, :]).then_inc(y_out, 16)
            sp.wait_ge(y_out, 32)
            sp.wait_ge(results_out, 48 * DEPTH)

        @block.gpsimd
        def _(pool):
            def over_partitions(ap):
                return ap.partition_broadcast(P)

            with pool.Fori(0, DEPTH) as l:
                pool.wait_ge(x_ready.sem, x_ready.at(l, 0))
                apart(pool)
                for dst, src in (
                    (b_ada[:, :, :], T["b_ada"][l].rearrange("(m p j) -> p m j", p=P, j=NJ)),
                    (norm_g[:, :, :], T["norm_g"][l].rearrange("m (p j) -> p m j", j=NJ)),
                    (attn_g[:, :], over_partitions(T["attn_norm_g"][l])),
                    (hg_g[:, :], over_partitions(T["hg_norm_g"][l])),
                    (lambdas[:, :, :], over_partitions(T["lambdas"][l])),
                    (lam_init[:, :], over_partitions(T["lam_init"][l])),
                    (r_bias[:, :], over_partitions(T["router_bias"][l])),
                    (w_four[:, :, :], T["w_fourier"][l].rearrange("(c p) n -> p c n", p=P)),
                    (w_router[:, :, :], T["w_router"][l].rearrange("(p j) e -> p j e", j=NJ)),
                    (cache_k[:, :], T["cache_k"][0][l].rearrange("t h d -> t (h d)")),
                    (cache_v[:, :], T["cache_v"][0][l].rearrange("t h d -> t (h d)")),
                    (state0[:, :, :], T["state_hgrn"][0][l].rearrange("d (a b) k v -> (b k) (d a) v", b=2)),
                ):
                    pool.dma_start(dst, src).then_inc(params_in, 16)
                nc.gpsimd.memset(w_shared, 0.0).then_inc(aT_zero.sem, 1)
                banks.enter("layer", l)
                banks.wait_emptied(pool, "v", 0)
                apart(pool)
                pool.dma_start(new_v[0][l].rearrange("t h d -> t (h d)"), val[:, 0, :]).then_inc(results_out, 16)
                banks.wait_emptied(pool, "k_rows")
                apart(pool)
                pool.dma_start(new_k[0][l].rearrange("t h d -> t (h d)"), k_rows[:, :]).then_inc(results_out, 16)
                banks.wait_emptied(pool, "st", 0)
                apart(pool)
                pool.dma_start(new_state[0][l].rearrange("d (a b) k v -> (b k) (d a) v", b=2), st_out[:, :, :])\
                    .then_inc(results_out, 16)
                banks.read(pool, "ho", 1)
                apart(pool)
                for i, src in enumerate((T["ws_gate"][l].rearrange("(p j) f -> p (j f)", j=NJ),
                                         T["ws_up"][l].rearrange("(p j) f -> p (j f)", j=NJ), T["ws_down"][l])):
                    pool.dma_start(w_shared[:, i * D:(i + 1) * D], src).then_inc(shared_in, 16)
                pool.wait_ge(results_out, l * 48 + 48)
                banks.wait_emptied(pool, "gT")
                apart(pool)
                pool.dma_start(gates_dram, gatesT[:, :]).then_inc(gates_out, 16)
                pool.wait_ge(gates_out, l * 16 + 16)
                apart(pool)

                def load_gates(i, e0):
                    pool.dma_start(gate_b[:, i, :, :].rearrange("p e t -> p (e t)"),
                                   over_partitions(gates_dram[bass.ds(e0, NSLOT), :].rearrange("e t -> (e t)")))\
                        .then_inc(gate_in[i], 16)

                for i in range(2):
                    load_gates(i, i * NSLOT)
                with pool.Fori(1, E // (2 * NSLOT)) as turn:
                    for i in range(2):
                        pool.wait_ge(act_ready.sem, l * (E + 1) + turn * (2 * NSLOT) + (1 + (i + 1) * NSLOT - 2 * NSLOT))
                        apart(pool)
                        load_gates(i, turn * (2 * NSLOT) + i * NSLOT)

        @block.tensor
        def _(pe):
            mm = nc.tensor.matmul
            tr = nc.tensor.transpose
            pe.wait_ge(consts_in, 16 * NCONST)
            pe.wait_ge(ones_ready, 1)
            banks.enter("start")
            for bank_empty in banks.empty_sem:
                pe.sem_inc(bank_empty, 1)
            for t in range(NTILE):
                for half in range(2):
                    bk = banks.claim(pe, "xT", 2 * t + half)
                    for j in range(4):
                        last = tr(bk[:, j * P:(j + 1) * P], rows[:, t, 4 * half + j:D:NJ], ident)
                    banks.filled(last, "xT", 2 * t + half)
            pe.wait_ge(scond_ready, 1)

            def mean_square(stage):
                bk = banks.claim(pe, stage)
                for j in range(NJ):
                    last = mm(bk[:, 0:TOK], ones[:, :], squares[:, j, :], start=(j == 0), stop=(j == NJ - 1))
                banks.filled(last, stage)

            with pe.Fori(0, DEPTH) as l:
                banks.enter("layer", l)

                pe.wait_ge(squared.sem, squared.at(l, 1))
                mean_square("ms1")

                for b in range(12):
                    m, half = divmod(b, 2)
                    w = block_in(pe, l, b).rearrange("p (j n) -> p j n", j=4)
                    if b == 0:
                        bk = banks.claim(pe, "mod")
                    for jo in range(NJ):
                        at = (m * NJ + jo) * 2
                        for ji in range(4):
                            last = mm(bk[:, at:at + 2], w[:, ji, jo:D:NJ], scond[:, 4 * half + ji, :],
                                      start=(b == 0 and jo == 0 and ji == 0), stop=(b == 11 and jo == NJ - 1 and ji == 3),
                                      skip_group_check=True)
                    if b == 11:
                        banks.filled(last, "mod")
                    else:
                        last.then_inc(slot_read, 1)

                pe.wait_ge(h_ready.sem, h_ready.at(l, 1))
                for b, stage in ((12, "q"), (13, "k")):
                    w = block_in(pe, l, b).rearrange("p (j n) -> p j n", j=NJ)
                    for i in range(DH):
                        bk = banks.claim(pe, stage, i)
                        for j in range(NJ):
                            last = mm(bk[:, 0:TOK], w[:, j, i * P:(i + 1) * P], h[:, j, :], start=(j == 0), stop=(j == NJ - 1))
                        banks.filled(last, stage, i)

                def token_major(stage, w, n):
                    for t in range(NTILE):
                        bk = banks.claim(pe, stage, t)
                        for j in range(NJ):
                            last = mm(bk[:, 0:n], h[:, j, t * P:(t + 1) * P], w[:, j, 0:n], start=(j == 0), stop=(j == NJ - 1))
                        banks.filled(last, stage, t)

                token_major("v", block_in(pe, l, 14).rearrange("p (j n) -> p j n", j=NJ), DA)
                w = block_in(pe, l, 15)
                token_major("fn", w[:, 0:2048].rearrange("p (j n) -> p j n", j=NJ), FN)
                w = w[:, 2048:4096].rearrange("p (j n) -> p j n", j=NJ)
                for i in range(2):
                    bk = banks.claim(pe, "hq", i)
                    for j in range(NJ):
                        last = mm(bk[:, 0:TOK], w[:, j, i * P:(i + 1) * P], h[:, j, :], start=(j == 0), stop=(j == NJ - 1))
                    banks.filled(last, "hq", i)
                token_major("hif", block_in(pe, l, 16).rearrange("p (j n) -> p j n", j=NJ), 2 * HW)
                token_major("hbg", block_in(pe, l, 17).rearrange("p (j n) -> p j n", j=NJ), 2 * HW)

                bk = banks.claim(pe, "k_rows")
                for i in range(DH):
                    banks.wait_emptied(pe, "k", i)
                    last = tr(bk[:, i * P:(i + 1) * P], kT[:, i, 0:P], ident)
                banks.filled(last, "k_rows")
                bk = banks.claim(pe, "ckT")
                pe.wait_ge(params_in, l * (16 * NPARAM) + 16 * NPARAM)
                for i in range(DH):
                    last = tr(bk[:, i * P:(i + 1) * P], cache_k[:, i * P:(i + 1) * P], ident)
                banks.filled(last, "ckT")
                for stage, src in (("rotq", qT), ("rotk", kT)):
                    for i in range(2):
                        bk = banks.claim(pe, stage, i)
                        for a in range(2):
                            banks.wait_emptied(pe, "q" if src is qT else "k", 2 * i + a)
                            last = mm(bk[:, a * 256:(a + 1) * 256], const("rot"), src[:, 2 * i + a, P:TOK], start=True, stop=True)
                        banks.filled(last, stage, i)

                for c in range(2):
                    for k, (cc, cl) in enumerate((("c_ctx", "c_lat"), ("s_ctx", "s_lat"))):
                        bk = banks.claim(pe, "four1", 2 * c + k)
                        banks.wait_emptied(pe, "fn", 0)
                        mm(bk[:, 0:P], u_fn[:, 0, c * P:(c + 1) * P], const(cc), start=True, stop=True)
                        for t in range(2):
                            banks.wait_emptied(pe, "fn", 1 + t)
                            last = mm(bk[:, P:TOK], u_fn[:, 1 + t, c * P:(c + 1) * P], const(cl)[:, t * 256:(t + 1) * 256],
                                      start=(t == 0), stop=(t == 1))
                        banks.filled(last, "four1", 2 * c + k)
                for c in range(2):
                    bk = banks.claim(pe, "zT", c)
                    for k, name in enumerate(("c_chan", "s_chan")):
                        banks.wait_emptied(pe, "four1", 2 * c + k)
                        last = mm(bk[:, 0:TOK], const(name), four1[:, 2 * c + k, :], start=(k == 0), stop=(k == 1))
                    banks.filled(last, "zT", c)
                for c in range(2):
                    bk = banks.claim(pe, "fnT", c)
                    for k in range(2):
                        banks.wait_emptied(pe, "zT", k)
                        last = mm(bk[:, 0:TOK], w_four[:, k, c * P:(c + 1) * P], zT[:, k, :], start=(k == 0), stop=(k == 1))
                    banks.filled(last, "fnT", c)

                pe.wait_ge(kk_ready.sem, kk_ready.at(l, 1))
                for g in range(4):
                    bk = banks.claim(pe, "kkT", g)
                    for t in range(NTILE):
                        last = tr(bk[:, t * P:(t + 1) * P], kk[:, t, g * P:(g + 1) * P], ident)
                    banks.filled(last, "kkT", g)
                pe.wait_ge(logf_ready.sem, logf_ready.at(l, 1))
                for g in range(4):
                    bk = banks.claim(pe, "cum", g)
                    for t in range(NTILE):
                        last = mm(bk[:, t * P:(t + 1) * P], logf[:, t, g * P:(g + 1) * P], const("tri_f" if g < 2 else "tri_b"),
                                  start=True, stop=True)
                    banks.filled(last, "cum", g)
                for i, tiles in enumerate(((0, 0), (1, 2))):
                    bk = banks.claim(pe, "past", i)
                    for d, t in enumerate(tiles):
                        last = mm(bk[:, d * HW:(d + 1) * HW], const("past_f" if d == 0 else "past_b"),
                                  logf[:, t, d * HW:(d + 1) * HW], start=True, stop=True)
                    banks.filled(last, "past", i)

                for n in range(NLEV):
                    lv = n % LEVELS
                    ka = pair[:, n % 2, :, :]
                    qa = ka if lv < LEVELS - 1 else pair2[:, :, :]
                    pe.wait_ge(pair_ready.sem, pair_ready.at(l, n + 1))
                    for t in range(NTILE):
                        for odd in range(2):
                            use = (n * NTILE + t) * 2 + odd
                            bk = banks.claim(pe, "lev", use)
                            r = slice(HK * odd, HK * (odd + 1))
                            for c in range(2):
                                last = mm(bk[:, c * P:(c + 1) * P], ka[r, c, t * P:(t + 1) * P],
                                          qa[r, c, t * P:(t + 1) * P], start=True, stop=True)
                            banks.filled(last, "lev", use)

                pe.wait_ge(kdec_ready.sem, kdec_ready.at(l, 1))
                for i, tiles in enumerate(((0, 0), (1, 2))):
                    bk = banks.claim(pe, "st", i)
                    for d, t in enumerate(tiles):
                        for a in range(2):
                            last = mm(bk[:, (2 * d + a) * P:(2 * d + a + 1) * P], kdec[:, 2 * i + d, a * P:(a + 1) * P],
                                      hv[:, t, a * P:(a + 1) * P], start=True, stop=True)
                    banks.filled(last, "st", i)

                pe.wait_ge(qdec_ready.sem, qdec_ready.at(l, 1))
                banks.wait_emptied(pe, "lev", 2 * NLEV * NTILE - 1)
                banks.wait_emptied(pe, "st", 1)
                for odd in range(2):
                    bk = banks.claim(pe, "ho", odd)
                    r = slice(HK * odd, HK * (odd + 1))
                    for t in range(NTILE):
                        for c in range(2):
                            hd = 2 * c + odd
                            out = bk[:, (2 * t + c) * HK:(2 * t + c + 1) * HK]
                            v = hv[:, t, hd * HK:(hd + 1) * HK]
                            mm(out, aT[:, 0, t, hd * P:(hd + 1) * P], v, start=True, stop=False)
                            last = mm(out, aT[:, 1, t, hd * P:(hd + 1) * P], v, start=False, stop=(t == 0))
                            if t > 0:
                                for d in range(2):
                                    src = state0 if (t == 1) == (d == 0) else st_mid
                                    last = mm(out, qdec[r, 2 * d + c, t * P:(t + 1) * P], src[r, 2 * d + c, :],
                                              start=False, stop=(d == 1))
                    banks.filled(last, "ho", odd)

                pe.wait_ge(rope_done.sem, rope_done.at(l, 1))
                for u in range(NU + 3):
                    if u < NU:
                        t, hd = UNITS[u]
                        keys = slice(0, P) if t == 0 else slice(P, KEYS)
                        for m in range(2):
                            bk = banks.claim(pe, "sc", 2 * u + m)
                            r = slice(m * DK, (m + 1) * DK)
                            last = mm(bk[:, 0:keys.stop - keys.start], qT[r, hd, t * P:(t + 1) * P], kT[r, hd, keys],
                                      start=True, stop=True)
                            banks.filled(last, "sc", 2 * u + m)
                    if 2 <= u < NU + 2:
                        v = u - 2
                        bk = banks.claim(pe, "wT", v)
                        pe.wait_ge(wts_ready.sem, wts_ready.at(l, v + 1))
                        for i in range(1 if UNITS[v][0] == 0 else 3):
                            last = tr(bk[:, i * P:(i + 1) * P], wts[:, v % 2, i * P:(i + 1) * P], ident)
                        banks.filled(last, "wT", v)
                    if u >= 3:
                        v = u - 3
                        t, hd = UNITS[v]
                        if hd == 0:
                            obk = banks.claim(pe, "o", t)
                        banks.wait_emptied(pe, "wT", v)
                        srcs = [val[:, 0, :]] if t == 0 else [val[:, 1, :], val[:, 2, :], cache_v[:, :]]
                        for i, src in enumerate(srcs):
                            last = mm(obk[:, hd * P:(hd + 1) * P], wT[:, v % 2, i * P:(i + 1) * P], src[:, hd * VD:(hd + 1) * VD],
                                      start=(i == 0), stop=(i == len(srcs) - 1))
                        if hd == DH - 1:
                            banks.filled(last, "o", t)
                for t in range(NTILE):
                    bk = banks.claim(pe, "oT", t)
                    pe.wait_ge(anorm_ready.sem, anorm_ready.at(l, 1))
                    for hd in range(DH):
                        last = tr(bk[:, hd * P:(hd + 1) * P], att[:, t, hd * P:(hd + 1) * P], ident)
                    banks.filled(last, "oT", t)
                pe.wait_ge(hnorm_ready.sem, hnorm_ready.at(l, 1))
                for c in range(2):
                    bk = banks.claim(pe, "hgT", c)
                    for t in range(NTILE):
                        last = tr(bk[:, t * P:(t + 1) * P], gate_o[:, t, c * P:(c + 1) * P], ident)
                    banks.filled(last, "hgT", c)

                for c in range(2):
                    banks.wait_emptied(pe, "fnT", c)
                    banks.wait_emptied(pe, "hgT", c)
                for t in range(NTILE):
                    banks.wait_emptied(pe, "oT", t)
                for half in range(2):
                    w = block_in(pe, l, 18 + half).rearrange("p (c n) -> p c n", c=4)
                    for j in range(NJ):
                        if half == 0:
                            banks.claim(pe, "out", j)
                        bk = banks.banks[banks.uses["layer"]["out", j][0]]
                        for c in range(4):
                            last = mm(bk[:, 0:TOK], w[:, c, j:D:NJ], mixT[:, 4 * half + c, :],
                                      start=(half == 0 and c == 0), stop=(half == 1 and c == 3))
                        if half == 1:
                            banks.filled(last, "out", j)
                    if half == 0:
                        last.then_inc(slot_read, 1)

                pe.wait_ge(squared.sem, squared.at(l, 2))
                mean_square("ms2")
                pe.wait_ge(h_ready.sem, h_ready.at(l, 2))
                bk = banks.claim(pe, "router")
                for t in range(NTILE):
                    for j in range(NJ):
                        last = mm(bk[:, t * E:(t + 1) * E], h[:, j, t * P:(t + 1) * P], w_router[:, j, :],
                                  start=(j == 0), stop=(j == NJ - 1))
                banks.filled(last, "router")

                def up(w, n):
                    for k, stage in enumerate(("G", "U")):
                        bk = banks.claim(pe, stage, 0, n)
                        for j in range(NJ):
                            last = mm(bk[:, 0:TOK], w[:, k * D + j * P:k * D + (j + 1) * P], h[:, j, :],
                                      start=(j == 0), stop=(j == NJ - 1))
                        banks.filled(last, stage)

                def down(w, n, buf, first, last_one):
                    pe.wait_ge(act_ready.sem, l * (E + 1) + n + 1)
                    for t in range(NTILE):
                        for c in range(2):
                            if first:
                                banks.claim(pe, "y", 2 * t + c)
                            last = mm(banks.banks[2 * t + c][:, :], act[:, buf, t * P:(t + 1) * P],
                                      w[:, 2 * D + c * 512:2 * D + (c + 1) * 512], start=first, stop=last_one)
                            if last_one:
                                banks.filled(last, "y", 2 * t + c)
                    if not first and not last_one:
                        last.then_inc(slot_read, 1)

                def expert_in(s, turn):
                    pe.wait_ge(slot_full[s], l * slot_layer[s] + turn * 48 + (fix_sum[s] + 48))

                pe.wait_ge(shared_in, l * 48 + 48)
                up(w_shared, 0)
                pe.wait_ge(gsel_ready.sem, gsel_ready.at(l, 1))
                bk = banks.claim(pe, "gT")
                apart(pe)
                for t in range(NTILE):
                    last = tr(bk[0:E, t * P:(t + 1) * P], gsel[:, t, :], ident)
                banks.filled(last, "gT")
                expert_in(0, 0)
                up(ring[:, 0, :], 1)
                down(w_shared, 0, 0, True, False)
                with pe.Fori(0, E // NSLOT - 1) as turn:
                    for s in range(NSLOT):
                        expert_in((s + 1) % NSLOT, turn + (s + 1) // NSLOT)
                        up(ring[:, (s + 1) % NSLOT, :], turn * NSLOT + (s + 2))
                        down(ring[:, s, :], turn * NSLOT + (s + 1), (s + 1) % 2, False, False)
                for s in range(NSLOT):
                    if s + 1 < NSLOT:
                        expert_in(s + 1, E // NSLOT - 1)
                        up(ring[:, s + 1, :], E - NSLOT + s + 2)
                    down(ring[:, s, :], E - NSLOT + s + 1, (s + 1) % 2, False, s == NSLOT - 1)

                for i in range(6):
                    banks.wait_emptied(pe, "y", i)
                for j in range(NJ):
                    bk = banks.claim(pe, "yT", j)
                    for t in range(NTILE):
                        last = tr(bk[:, t * P:(t + 1) * P], rows[:, t, j:D:NJ], ident)
                    banks.filled(last, "yT", j)

            banks.enter("final")
            pe.wait_ge(squared.sem, squared.at(DEPTH, 1))
            mean_square("ms")
            pe.wait_ge(final_ready, 1)
            for t in range(NTILE):
                for half in range(2):
                    bk = banks.claim(pe, "rows", 2 * t + half)
                    for j in range(4):
                        last = tr(bk[:, j * P:(j + 1) * P], h[:, 4 * half + j, t * P:(t + 1) * P], ident)
                    banks.filled(last, "rows", 2 * t + half)

        @block.scalar
        def _(act_e):
            af = nc.scalar.activation
            order = InOrder(act_e, act_order, 0, 4, DEPTH)
            after = order.after

            act_e.wait_ge(consts_in, 16 * NCONST)
            af(scond[:, :, :], cond[:, :, :].rearrange("p s j -> p j s"), ACT.Silu).then_inc(scond_ready, 1)
            act_e.wait_ge(lb_diff, 1)
            af(kk[:, 1:3, :], kk[:, 1:3, :], ACT.Exp).then_inc(lb_exp, 1)

            def squares_of_x(state, count):
                act_e.wait_ge(x_ready.sem, state)
                af(squares, x[:, :, :], ACT.Square).then_inc(squared.sem, 1)

            def root_of_mean(stage):
                bk = banks.read(act_e, stage)
                banks.emptied(af(rms[:, :], bk[:, 0:TOK], ACT.Sqrt, bias=eps_t[:, :], scale=1.0 / D), stage)

            with act_e.Fori(0, DEPTH) as l:
                order.enter("layer", l)
                banks.enter("layer", l)
                squares_of_x(x_ready.at(l, 0), 1)
                root_of_mean("ms1")

                for stage, dst in (("q", qT), ("k", kT)):
                    for i in range(DH):
                        bk = banks.read(act_e, stage, i)
                        banks.emptied(af(dst[:, i, 0:TOK], bk[:, 0:TOK], ACT.Copy), stage, i)
                for t in range(NTILE):
                    bk = banks.read(act_e, "fn", t)
                    banks.emptied(af(u_fn[:, t, :], bk[:, 0:FN], ACT.Copy), "fn", t)
                for i in range(2):
                    bk = banks.read(act_e, "hq", i)
                    banks.emptied(af(hqT[:, i, :], bk[:, 0:TOK], ACT.Silu), "hq", i)
                for t in range(NTILE):
                    bk = banks.read(act_e, "hif", t)
                    af(hv[:, t, :], bk[:, 0:HW], ACT.Copy)
                    af(logf[:, t, 0:HW], bk[:, HW:2 * HW], ACT.Sigmoid)
                    banks.emptied(af(kk[:, t, 0:HW], bk[:, HW:2 * HW], ACT.Sigmoid, scale=-1.0), "hif", t)
                for t in range(NTILE):
                    bk = banks.read(act_e, "hbg", t)
                    af(logf[:, t, HW:2 * HW], bk[:, 0:HW], ACT.Sigmoid)
                    af(kk[:, t, HW:2 * HW], bk[:, 0:HW], ACT.Sigmoid, scale=-1.0)
                    banks.emptied(af(gate_o[:, t, :], bk[:, HW:2 * HW], ACT.Silu), "hbg", t)

                for i in range(4):
                    bk = banks.read(act_e, "four1", i)
                    banks.emptied(af(four1[:, i, :], bk[:, 0:TOK], ACT.Copy), "four1", i)
                for c in range(2):
                    bk = banks.read(act_e, "zT", c)
                    banks.emptied(af(zT[:, c, :], bk[:, 0:TOK], ACT.Copy), "zT", c)
                for c in range(2):
                    bk = banks.read(act_e, "fnT", c)
                    banks.emptied(af(mixT[:, c, :], bk[:, 0:TOK], ACT.Copy), "fnT", c)

                act_e.wait_ge(fgate_ready.sem, fgate_ready.at(l, 1))
                af(logf[:, :, :], logf[:, :, :], ACT.Ln).then_inc(logf_ready.sem, 1)
                for g in range(4):
                    bk = banks.read(act_e, "kkT", g)
                    banks.emptied(af(kkT[:, g, :], bk[:, 0:TOK], ACT.Copy), "kkT", g)
                for g in range(4):
                    bk = banks.read(act_e, "cum", g)
                    banks.emptied(af(cum[:, g, :], bk[:, 0:TOK], ACT.Copy), "cum", g)
                banks.read(act_e, "past", 1)
                for i in range(2):
                    bk = banks.read(act_e, "past", i)
                    banks.emptied(af(kdec[:, 2 * i:2 * i + 2, :], bk[:, :], ACT.Exp), "past", i)
                for g in range(4):
                    banks.wait_emptied(act_e, "cum", g)
                af(qdec[:, :, :], cum[:, :, :], ACT.Exp).then_inc(ecum_ready.sem, 1)
                act_e.wait_ge(lam_sum.sem, lam_sum.at(l, 1))
                af(lam_s[:, :], lam_s[:, :], ACT.Exp).then_inc(lam_exp.sem, 1)

                for n in range(NLEV):
                    d, lv = divmod(n, LEVELS)
                    act_e.wait_ge(diff_ready.sem, diff_ready.at(l, n + 1))
                    if lv < LEVELS - 1:
                        w = HALVES[lv]
                        dv = diff[:, :, :].rearrange("p c t -> p (c t)").rearrange("p (b w) -> p b w", w=2 * w)
                        fv = fac[:, :, :].rearrange("p c t -> p (c t)").rearrange("p (b w) -> p b w", w=2 * w)
                        early, late = (-1.0, 1.0) if d == 0 else (1.0, -1.0)
                        af(fv[:, :, 0:w], dv[:, :, 0:w], ACT.Exp, scale=early)
                        af(fv[:, :, w:2 * w], dv[:, :, w:2 * w], ACT.Exp, scale=late).then_inc(fac_ready.sem, 1)
                    else:
                        af(fac[:, :, :], diff[:, :, :], ACT.Exp)
                        af(fac2[:, :, :], diff[:, :, :], ACT.Exp, scale=-1.0).then_inc(fac_ready.sem, 1)

                for odd in range(2):
                    bk = banks.read(act_e, "ho", odd)
                    src = bk[:, 0:6 * HK].rearrange("p (i a d) -> p i a d", i=NTILE, a=2)
                    of_heads = lambda ap: ap.rearrange("p i (a b d) -> p i a b d", a=2, b=2)[:, :, :, odd, :]
                    af(of_heads(ho[:, :, :]), src, ACT.Copy)
                    banks.emptied(af(of_heads(ho_sq), src, ACT.Square), "ho", odd)

                for u in range(NU + 3):
                    if u < NU:
                        nk = P if UNITS[u][0] == 0 else KEYS - P
                        act_e.wait_ge(ntop_ready.sem, ntop_ready.at(l, u + 1))
                        for m in range(2):
                            bk = banks.read(act_e, "sc", 2 * u + m)
                            ins = af(prob[:, u % 2, m, 0:nk], bk[:, 0:nk], ACT.Exp, bias=ntop[:, u % 2, m:m + 1],
                                     scale=SCALE, accum_out=den[:, u % 2, m:m + 1])
                            banks.emptied(ins, "sc", 2 * u + m)
                    if 2 <= u < NU + 2:
                        v = u - 2
                        nk = P if UNITS[v][0] == 0 else 3 * P
                        bk = banks.read(act_e, "wT", v)
                        banks.emptied(af(wT[:, v % 2, 0:nk], bk[:, 0:nk], ACT.Copy), "wT", v)
                    if u >= 3 and UNITS[u - 3][1] == DH - 1:
                        t = UNITS[u - 3][0]
                        bk = banks.read(act_e, "o", t)
                        af(att[:, t, :], bk[:, :], ACT.Copy)
                        banks.emptied(af(att_sq[:, t, :], bk[:, :], ACT.Square), "o", t)
                act_e.wait_ge(sums_ready.sem, sums_ready.at(l, 1))
                af(att_r[:, 1, :], att_r[:, 0, :], ACT.Sqrt, bias=eps_t[:, :], scale=1.0 / VD)
                af(ho_r[:, 1, :], ho_r[:, 0, :], ACT.Sqrt, bias=eps_t[:, :], scale=1.0 / HK).then_inc(roots_ready.sem, 1)
                for t in range(NTILE):
                    bk = banks.read(act_e, "oT", t)
                    banks.emptied(af(mixT[:, 2:6, t * P:(t + 1) * P], bk[:, :].rearrange("p (a t) -> p a t", a=DH), ACT.Copy), "oT", t)
                for c in range(2):
                    bk = banks.read(act_e, "hgT", c)
                    banks.emptied(af(mixT[:, 6 + c, :], bk[:, 0:TOK], ACT.Copy), "hgT", c)

                squares_of_x(x_ready.at(l, 1), 2)
                root_of_mean("ms2")
                bk = banks.read(act_e, "router")
                banks.emptied(af(score[:, :, :].rearrange("p i e -> p (i e)"), bk[:, 0:NTILE * E], ACT.Sigmoid), "router")

                def silu_gate(n, buf, waits=True):
                    if waits:
                        act_e.wait_ge(act_ready.sem, l * (E + 1) + n - 1)
                    bk = banks.read(act_e, "G", 0, n)
                    banks.emptied(af(sil[:, buf, :], bk[:, 0:TOK], ACT.Silu), "G")

                silu_gate(0, 0, False)
                silu_gate(1, 1, False)
                with act_e.Fori(0, E // NSLOT - 1) as turn:
                    for s in range(NSLOT):
                        silu_gate(turn * NSLOT + (s + 2), s % 2)
                for s in range(NSLOT - 1):
                    silu_gate(E - NSLOT + s + 2, s % 2)
                for t in range(NTILE):
                    bk = banks.read(act_e, "y", 2 * t)
                    banks.emptied(af(rows[:, t, 0:512], bk[:, :], ACT.Copy), "y", 2 * t)

            banks.enter("final")
            squares_of_x(x_ready.at(DEPTH, 0), 0)
            root_of_mean("ms")

        @block.vector
        def _(dve):
            tt, ts, stt = nc.vector.tensor_tensor, nc.vector.tensor_scalar, nc.vector.scalar_tensor_tensor
            copy, red = nc.vector.tensor_copy, nc.vector.tensor_reduce
            order = InOrder(dve, dve_order, 5, LAYER_DVE, DEPTH)
            after = order.after
            order.enter("start")
            banks.enter("start")
            nc.vector.memset(eps_t[:, :], EPS)
            nc.vector.memset(ones[:, :], 1.0).then_inc(ones_ready, 1)
            dve.wait_ge(consts_in, 16 * NCONST)
            copy(masks[:, :, :], masks_f)
            after(tt(kk[:, 0, :], lb_all[:, 0, :], lb_all[:, 1, :], ALU.max))
            tt(kk[:, 1:3, :], lb_all[:, :, :], kk[:, 0, :].unsqueeze(1).broadcast_to([P, 2, 2 * HW]), ALU.subtract).then_inc(lb_diff, 1)
            for t in range(NTILE):
                for half in range(2):
                    bk = banks.read(dve, "xT", 2 * t + half)
                    banks.emptied(copy(x[:, 4 * half:4 * half + 4, t * P:(t + 1) * P],
                                       bk[:, :].rearrange("p (j t) -> p j t", j=4)), "xT", 2 * t + half)
            dve.wait_ge(lb_exp, 1)
            after(tt(kk[:, 0, :], kk[:, 1, :], kk[:, 2, :], ALU.add))
            after(nc.vector.reciprocal(kk[:, 0, :], kk[:, 0, :]))
            after(nc.vector.memset(lb_all[:, 0, :], 0.0))
            after(tt(lb_all[:, 1, :], kk[:, 2, :], kk[:, 0, :], ALU.mult))
            nc.vector.memset(tick[:, :], 0.0).then_inc(x_ready.sem, 1)
            order.leave()

            def norm(stage, m, gi):
                banks.wait_emptied(dve, stage)
                after(nc.vector.reciprocal(rstd[:, :], rms[:, :]))
                after(tt(h[:, :, :], x[:, :, :], rstd[:, :].unsqueeze(1).broadcast_to([P, NJ, TOK]), ALU.mult))
                for j in range(NJ):
                    for s in range(2):
                        last = ts(h[:, j, SPAN[s]], h[:, j, SPAN[s]], gain[:, j, s:s + 1], mod[:, m, j, s:s + 1], ALU.mult, ALU.add)
                last.then_inc(h_ready.sem, 1)

            def gain_of(m, gi):
                return stt(gain[:, :, :], mod[:, m, :, :], 1.0, norm_g[:, gi, :].unsqueeze(2).broadcast_to([P, NJ, 2]), ALU.add, ALU.mult)

            def gated_residual(stage, m):
                for j in range(NJ):
                    bk = banks.read(dve, stage, j)
                    for s in range(2):
                        last = stt(x[:, j, SPAN[s]], bk[:, SPAN[s]], mod[:, m, j, s:s + 1], x[:, j, SPAN[s]], ALU.mult, ALU.add)
                    banks.emptied(last, stage, j)

            with dve.Fori(0, DEPTH) as l:
                order.enter("layer", l)
                banks.enter("layer", l)
                after(copy(lb[:, :], lb_all[:, l, :]))
                after(ts(om[:, :], lb[:, :], -1.0, 1.0, ALU.mult, ALU.add))
                dve.wait_ge(params_in, l * (16 * NPARAM) + 16 * NPARAM)
                after(tt(lam_p[:, :, :], lambdas[:, 0:4:2, :], lambdas[:, 1:4:2, :], ALU.mult))
                red(lam_s[:, :], lam_p[:, :, :], AX.X, ALU.add).then_inc(lam_sum.sem, 1)
                after(ts(attn_g[:, :], attn_g[:, :], lam_init[:, 1:2], None, ALU.mult))
                bk = banks.read(dve, "mod")
                banks.emptied(tt(mod[:, :, :, :].rearrange("p m j s -> p (m j) s"), bk[:, 0:12 * NJ].rearrange("p (a s) -> p a s", s=2),
                                 b_ada[:, :, :].rearrange("p m j -> p (m j)").unsqueeze(2).broadcast_to([P, 6 * NJ, 2]), ALU.add), "mod")
                banks.wait_emptied(dve, "mod")
                after(gain_of(1, 0))
                norm("ms1", 0, 0)

                for t in range(NTILE):
                    bk = banks.read(dve, "v", t)
                    banks.emptied(copy(val[:, t, :], bk[:, :]), "v", t)

                for i in range(2):
                    banks.wait_emptied(dve, "hq", i)
                after(ts(hqT[:, :, :], hqT[:, :, :], HK ** -0.5, None, ALU.mult))
                for t in range(NTILE):
                    banks.wait_emptied(dve, "hif", t)
                    banks.wait_emptied(dve, "hbg", t)
                over_tiles = lambda ap: ap.unsqueeze(1).broadcast_to([P, NTILE, 2 * HW])
                after(tt(logf[:, :, :], logf[:, :, :], over_tiles(om[:, :]), ALU.mult))
                after(tt(logf[:, :, :], logf[:, :, :], over_tiles(lb[:, :]), ALU.add))
                ts(logf[:, :, :], logf[:, :, :], LOG_DECAY_FLOOR, None, ALU.max).then_inc(fgate_ready.sem, 1)
                tt(kk[:, :, :], kk[:, :, :], over_tiles(om[:, :]), ALU.mult).then_inc(kk_ready.sem, 1)

                bk = banks.read(dve, "k_rows")
                banks.emptied(copy(k_rows[:, :], bk[:, :]), "k_rows")
                bk = banks.read(dve, "ckT")
                banks.emptied(copy(kT[:, :, TOK:KEYS], bk[:, :].rearrange("p (a t) -> p a t", a=DH)), "ckT")
                over_heads = lambda ap: ap.unsqueeze(1).broadcast_to([P, 2, TOK - P])
                for stage, dst in (("rotq", qT), ("rotk", kT)):
                    for i in range(2):
                        heads = dst[:, 2 * i:2 * i + 2, P:TOK]
                        bk = banks.read(dve, stage, i)
                        banks.emptied(tt(rot_t[:, :, :], bk[:, :].rearrange("p (a t) -> p a t", a=2), over_heads(const("sin")), ALU.mult), stage, i)
                        after(tt(heads, heads, over_heads(const("cos")), ALU.mult))
                        banks.wait_emptied(dve, stage, i)
                        last = tt(heads, heads, rot_t[:, :, :], ALU.add)
                        if stage == "rotk" and i == 1:
                            last.then_inc(rope_done.sem, 1)
                        else:
                            after(last)

                for i, tiles in enumerate(((0, 0), (1, 2))):
                    banks.wait_emptied(dve, "past", i)
                    for d, t in enumerate(tiles):
                        last = tt(kdec[:, 2 * i + d, :], kdec[:, 2 * i + d, :], kk[:, t, d * HW:(d + 1) * HW], ALU.mult)
                last.then_inc(kdec_ready.sem, 1)
                dve.wait_ge(ecum_ready.sem, ecum_ready.at(l, 1))
                copy(edge[:, 0:2], qdec[:, 0:2, 2 * P - 1])
                after(copy(edge[:, 2:4], qdec[:, 2:4, 2 * P]))
                qd = qdec[:, :, :].rearrange("p (d c) t -> p d (c t)", d=2)
                tt(qd, qd, hqT[:, :, :].rearrange("p c t -> p (c t)").unsqueeze(1).broadcast_to([P, 2, 2 * TOK]), ALU.mult)\
                    .then_inc(qdec_ready.sem, 1)

                def flat(ap):
                    return ap.rearrange("p c t -> p (c t)")

                def masked(n):
                    d, lv = divmod(n, LEVELS)
                    for t in range(NTILE):
                        for odd in range(2):
                            use = (n * NTILE + t) * 2 + odd
                            bk = banks.read(dve, "lev", use)
                            apart(dve)
                            ins = nc.vector.copy_predicated(aT[:, d, t, :].rearrange("p (a b t) -> p a b t", a=2, b=2)[:, :, odd, :],
                                                            masks[:, n, :].unsqueeze(1).broadcast_to([P, 2, P]),
                                                            bk[:, 0:2 * P].rearrange("p (a t) -> p a t", a=2))
                            banks.emptied(ins, "lev", use)

                for n in range(NLEV):
                    d, lv = divmod(n, LEVELS)
                    w = HALVES[lv] if lv < LEVELS - 1 else BASE // 2
                    blocks = lambda ap, w=w: flat(ap).rearrange("p (b w) -> p b w", w=2 * w)
                    cd = blocks(cum[:, 2 * d:2 * d + 2, :])
                    nb = 2 * TOK // (2 * w)
                    at = w - 1 if d == 0 else w
                    tt(blocks(diff[:, :, :]), cd, cd[:, :, at:at + 1].broadcast_to([P, nb, 2 * w]), ALU.subtract)\
                        .then_inc(diff_ready.sem, 1)
                    if n == 0:
                        dve.wait_ge(aT_zero.sem, aT_zero.at(l, 1))
                    else:
                        masked(n - 1)
                    dve.wait_ge(fac_ready.sem, fac_ready.at(l, n + 1))
                    keys, out = kkT[:, 2 * d:2 * d + 2, :], pair[:, n % 2, :, :]
                    if lv < LEVELS - 1:
                        first, second = (keys, hqT[:, :, :]) if d == 0 else (hqT[:, :, :], keys)
                        tt(blocks(out)[:, :, 0:w], blocks(first)[:, :, 0:w], blocks(fac[:, :, :])[:, :, 0:w], ALU.mult)
                        last = tt(blocks(out)[:, :, w:2 * w], blocks(second)[:, :, w:2 * w], blocks(fac[:, :, :])[:, :, w:2 * w], ALU.mult)
                    else:
                        tt(flat(pair2[:, :, :]), flat(hqT[:, :, :]), flat(fac[:, :, :]), ALU.mult)
                        last = tt(flat(out), flat(keys), flat(fac2[:, :, :]), ALU.mult)
                    last.then_inc(pair_ready.sem, 1)
                masked(NLEV - 1)

                bk = banks.read(dve, "st", 0)
                sv = bk[:, :].rearrange("p (g n) -> p g n", g=4)
                copy(st_out[0:HK, :, :], sv[0:HK, :, 0:HK])
                banks.emptied(copy(st_out[HK:P, :, :], sv[HK:P, :, HK:P]), "st", 0)
                after(tt(st_mid[:, :, :], state0[:, :, :], edge[:, :].unsqueeze(2).broadcast_to([P, 4, HK]), ALU.mult))
                bk = banks.read(dve, "st", 1)
                sv = bk[:, :].rearrange("p (g n) -> p g n", g=4)
                tt(st_mid[0:HK, :, :], st_mid[0:HK, :, :], sv[0:HK, :, 0:HK], ALU.add)
                banks.emptied(tt(st_mid[HK:P, :, :], st_mid[HK:P, :, :], sv[HK:P, :, HK:P], ALU.add), "st", 1)

                dve.wait_ge(lam_exp.sem, lam_exp.at(l, 1))
                after(stt(neg_lam[:, :], lam_s[:, 1:2], lam_s[:, 0:1], lam_init[:, 0:1], ALU.subtract, ALU.subtract))

                for u in range(NU + 1):
                    if u < NU:
                        nk = P if UNITS[u][0] == 0 else KEYS - P
                        for m in range(2):
                            bk = banks.read(dve, "sc", 2 * u + m)
                            last = red(top[:, u % 2, m:m + 1], bk[:, 0:nk], AX.X, ALU.max)
                        after(last)
                        ts(ntop[:, u % 2, :], top[:, u % 2, :], -SCALE, None, ALU.mult).then_inc(ntop_ready.sem, 1)
                    if u >= 1:
                        v = u - 1
                        nk = P if UNITS[v][0] == 0 else KEYS - P
                        for m in range(2):
                            banks.wait_emptied(dve, "sc", 2 * v + m)
                        after(nc.vector.reciprocal(rden[:, v % 2, :], den[:, v % 2, :]))
                        after(tt(rden[:, v % 2, 1:2], rden[:, v % 2, 1:2], neg_lam[:, :], ALU.mult))
                        if v >= 2:
                            banks.read(dve, "wT", v - 2)
                        after(ts(wts[:, v % 2, 0:nk], prob[:, v % 2, 0, 0:nk], rden[:, v % 2, 0:1], None, ALU.mult))
                        stt(wts[:, v % 2, 0:nk], prob[:, v % 2, 1, 0:nk], rden[:, v % 2, 1:2], wts[:, v % 2, 0:nk], ALU.mult, ALU.add)\
                            .then_inc(wts_ready.sem, 1)

                for t in range(NTILE):
                    banks.wait_emptied(dve, "o", t)
                for odd in range(2):
                    banks.wait_emptied(dve, "ho", odd)
                heads_a = lambda ap: ap.rearrange("p i (a d) -> p (i a) d", a=DH)
                heads_h = lambda ap: ap.rearrange("p i (a d) -> p (i a) d", a=HH)
                red(att_r[:, 0, :], heads_a(att_sq), AX.X, ALU.add)
                red(ho_r[:, 0, :], heads_h(ho_sq[:, :, :]), AX.X, ALU.add).then_inc(sums_ready.sem, 1)
                dve.wait_ge(roots_ready.sem, roots_ready.at(l, 1))
                nc.vector.reciprocal(att_r[:, 0, :], att_r[:, 1, :])
                after(nc.vector.reciprocal(ho_r[:, 0, :], ho_r[:, 1, :]))
                after(tt(heads_a(att[:, :, :]), heads_a(att[:, :, :]), att_r[:, 0, :].unsqueeze(2).broadcast_to([P, NTILE * DH, VD]), ALU.mult))
                tt(heads_a(att[:, :, :]), heads_a(att[:, :, :]), attn_g[:, :].unsqueeze(1).broadcast_to([P, NTILE * DH, VD]), ALU.mult)\
                    .then_inc(anorm_ready.sem, 1)
                after(tt(heads_h(ho[:, :, :]), heads_h(ho[:, :, :]), ho_r[:, 0, :].unsqueeze(2).broadcast_to([P, NTILE * HH, HK]), ALU.mult))
                after(tt(heads_h(ho[:, :, :]), heads_h(ho[:, :, :]), hg_g[:, :].unsqueeze(1).broadcast_to([P, NTILE * HH, HK]), ALU.mult))
                tt(gate_o[:, :, :], gate_o[:, :, :], ho[:, :, :], ALU.mult).then_inc(hnorm_ready.sem, 1)

                gated_residual("out", 2)
                gain_of(4, 1).then_inc(x_ready.sem, 1)
                dve.wait_ge(x_ready.sem, x_ready.at(l, 1))
                norm("ms2", 3, 1)

                banks.wait_emptied(dve, "router")
                after(tt(biased[:, :, :], score[:, :, :], r_bias[:, :].unsqueeze(1).broadcast_to([P, NTILE, E]), ALU.add))
                apart(dve)
                for t in range(NTILE):
                    for g in range(NG):
                        last = nc.vector.max(tops[:, t * NG + g, :], biased[:, t, g * PG:(g + 1) * PG])
                after(last)
                gs = gsum[:, :, :]
                after(tt(gs.rearrange("p i g -> p (i g)"), tops[:, :, 0], tops[:, :, 1], ALU.add))
                other = gs.unsqueeze(2).broadcast_to([P, NTILE, NG, NG])
                own = gs.unsqueeze(3).broadcast_to([P, NTILE, NG, NG])
                sq4 = lambda ap: ap.rearrange("p i (a b) -> p i a b", a=NG)
                tt(sq4(cmp_a[:, :, :]), other, own, ALU.is_gt)
                after(tt(sq4(cmp_b[:, :, :]), other, own, ALU.is_equal))
                after(tt(cmp_b[:, :, :], cmp_b[:, :, :], const("tie").unsqueeze(1).broadcast_to([P, NTILE, NG * NG]), ALU.mult))
                after(tt(cmp_a[:, :, :], cmp_a[:, :, :], cmp_b[:, :, :], ALU.add))
                after(red(rank[:, :], cmp_a[:, :, :].rearrange("p i (a b) -> p (i a) b", a=NG), AX.X, ALU.add))
                after(ts(rank[:, :], rank[:, :], float(TOPK_GROUPS), None, ALU.is_lt))
                after(ts(gpen[:, :], rank[:, :], NEVER, -NEVER, ALU.mult, ALU.add))
                grouped = biased[:, :, :].rearrange("p i (g k) -> p (i g) k", g=NG)
                wide = lambda ap: ap.unsqueeze(2).broadcast_to([P, NTILE * NG, PG])
                after(tt(grouped, grouped, wide(rank[:, :]), ALU.mult))
                after(tt(grouped, grouped, wide(gpen[:, :]), ALU.add))
                apart(dve)
                for t in range(NTILE):
                    last = nc.vector.max(best[:, t, :], biased[:, t, :])
                after(last)
                apart(dve)
                for t in range(NTILE):
                    last = nc.vector.match_replace(gsel[:, t, :], best[:, t, :], biased[:, t, :], TAKEN)
                after(last)
                after(ts(gsel[:, :, :], gsel[:, :, :], NEVER * 1.05, None, ALU.is_gt))
                after(tt(gsel[:, :, :], gsel[:, :, :], score[:, :, :], ALU.mult))
                after(red(wsum[:, :], gsel[:, :, :], AX.X, ALU.add))
                after(nc.vector.reciprocal(wsum[:, :], wsum[:, :]))
                after(ts(wsum[:, :], wsum[:, :], ROUTED_SCALE, None, ALU.mult))
                tt(gsel[:, :, :], gsel[:, :, :], wsum[:, :].unsqueeze(2).broadcast_to([P, NTILE, E]), ALU.mult).then_inc(gsel_ready.sem, 1)

                def gated_act(n, buf, gates):
                    banks.wait_emptied(dve, "G", 0, n)
                    bk = banks.read(dve, "U", 0, n)
                    banks.emptied(tt(sil[:, buf, :], sil[:, buf, :], bk[:, 0:TOK], ALU.mult), "U")
                    banks.wait_emptied(dve, "U", 0, n)
                    if gates is None:
                        copy(act[:, buf, :], sil[:, buf, :]).then_inc(act_ready.sem, 1)
                    else:
                        tt(act[:, buf, :], sil[:, buf, :], gates, ALU.mult).then_inc(act_ready.sem, 1)

                gated_act(0, 0, None)
                bk = banks.read(dve, "gT")
                banks.emptied(copy(gatesT[:, :], bk[0:E, 0:TOK]), "gT")
                with dve.Fori(0, E // (2 * NSLOT)) as turn:
                    for i in range(2):
                        dve.wait_ge(gate_in[i], l * (16 * E // (2 * NSLOT)) + turn * 16 + 16)
                        for s in range(NSLOT):
                            gated_act(turn * (2 * NSLOT) + (i * NSLOT + s + 1), (s + 1) % 2, gate_b[:, i, s, :])
                for t in range(NTILE):
                    bk = banks.read(dve, "y", 2 * t + 1)
                    banks.emptied(copy(rows[:, t, 512:1024], bk[:, :]), "y", 2 * t + 1)
                gated_residual("yT", 5)
                nc.vector.memset(tick[:, :], 0.0).then_inc(x_ready.sem, 1)
                order.leave()

            order.enter("final")
            banks.enter("final")
            banks.wait_emptied(dve, "ms")
            after(nc.vector.reciprocal(rstd[:, :], rms[:, :]))
            dve.wait_ge(x_ready.sem, x_ready.at(DEPTH, 0))
            after(tt(h[:, :, :], x[:, :, :], rstd[:, :].unsqueeze(1).broadcast_to([P, NJ, TOK]), ALU.mult))
            for j in range(NJ):
                last = ts(h[:, j, :], h[:, j, :], final_g[:, j:j + 1], None, ALU.mult)
            last.then_inc(final_ready, 1)
            for t in range(NTILE):
                for half in range(2):
                    bk = banks.read(dve, "rows", 2 * t + half)
                    banks.emptied(copy(rows[:, t, :].rearrange("p (q j) -> p j q", j=NJ)[:, 4 * half:4 * half + 4, :],
                                       bk[:, :].rearrange("p (j q) -> p j q", j=4)), "rows", 2 * t + half)


_INS = ["x_prompt", "x_sample", "cache_k", "cache_v", "state_hgrn", "c", "c_ctx", "w_ada", "b_ada", "norm_g", "w_in",
        "w_fourier", "lambdas", "attn_norm_g", "lower_bounds", "hg_norm_g", "w_out", "w_router", "router_bias",
        "w_gate", "w_up", "w_down", "ws_gate", "ws_up", "ws_down", "final_g"]


def shape_constants(depth):
    import numpy as np

    i = np.arange(P)
    out = {"ident": np.eye(P), "tri_f": i[:, None] <= i[None, :], "tri_b": i[:, None] >= i[None, :],
           "past_f": i[:, None] > i[None, :], "past_b": i[:, None] < i[None, :]}
    rot = np.zeros((P, P))
    for a in range(0, P, 32):
        for k in range(16):
            rot[a + 16 + k, a + k] = -1.0
            rot[a + k, a + 16 + k] = 1.0
    out["rot"] = rot
    for name, n in (("ctx", 128), ("lat", 256)):
        k = np.arange(n)
        ang = 2 * np.pi * ((k[:, None] * k[None, :]) % n) / n
        for c, m in (("c", np.cos(ang)), ("s", np.sin(ang))):
            out[f"{c}_{name}"] = (m / np.sqrt(n * 64.0)).reshape(n // P, P, n).transpose(1, 0, 2).reshape(P, -1)
    k = np.arange(64)
    ang = 2 * np.pi * ((k[:, None] * k[None, :]) % 64) / 64
    out["c_chan"] = np.kron(np.eye(2), np.cos(ang))
    out["s_chan"] = -np.kron(np.eye(2), np.sin(ang))
    t = np.arange(256)
    inv = (10000.0 ** (-np.arange(0, 32, 2) / 32.0)).astype(np.float32)
    row, col = (t // 64)[None, :] * inv[:, None], (t % 64)[None, :] * inv[:, None]
    ang = np.concatenate([row, row, col, col] * 2, 0)
    out["cos"], out["sin"] = np.cos(ang), np.sin(ang)
    g = np.arange(8)
    out["tie"] = np.broadcast_to((g[None, :] < g[:, None]).reshape(1, 64), (P, 64))
    packed = np.concatenate([np.asarray(out[name], np.float32) for name, _ in CONST_COLS], 1)

    masks = []
    for d in range(2):
        s, t = (i[:, None], i[None, :]) if d == 0 else (P - 1 - i[:, None], P - 1 - i[None, :])
        for w in HALVES:
            masks.append((s // (2 * w) == t // (2 * w)) & (s % (2 * w) < w) & (t % (2 * w) >= w))
        masks.append((s // BASE == t // BASE) & (s <= t))
    init = np.array([0.8 - 0.6 * np.exp(-0.3 * n) for n in range(depth)])
    lam = np.stack([init, 1.0 - init], 1).astype(np.float32)
    return packed, np.stack(masks).astype(np.float32), lam


def kernel(**inputs):
    import numpy as np
    import concourse.bacc as bacc
    from concourse.bass_utils import run_bass_kernel_spmd

    nc = bacc.Bacc("TRN2", target_bir_lowering=False, num_devices=1, dynamic_dma_scratch_size=4096)
    arrays = {name: np.ascontiguousarray(inputs[name]) for name in _INS}
    depth, past, heads, kd = arrays["cache_k"].shape[1:]
    arrays["const_f"], arrays["const_m"], arrays["lam_init"] = shape_constants(depth)
    T = {name: nc.dram_tensor("in_" + name, a.shape, mybir.dt.from_np(a.dtype), kind="ExternalInput").ap()
         for name, a in arrays.items()}
    seq = arrays["x_prompt"].shape[1]
    shapes = {"y_prompt": arrays["x_prompt"].shape, "y_sample": arrays["x_sample"].shape,
              "new_k": (1, depth, seq, heads, kd), "new_v": (1, depth, seq, heads, arrays["cache_v"].shape[4]),
              "new_state": arrays["state_hgrn"].shape}
    outs = {name: nc.dram_tensor("out_" + name, shape, F32, kind="ExternalOutput").ap() for name, shape in shapes.items()}
    trunk_program(nc, T, T["const_f"], T["const_m"], *outs.values())
    r = run_bass_kernel_spmd(nc, [{"in_" + name: a for name, a in arrays.items()}], core_ids=[0])
    return tuple(r.results[0]["out_" + name] for name in shapes)
```

```python
from contextlib import ExitStack

import concourse.bass as bass
from concourse import mybir

F32 = mybir.dt.float32
F32R = mybir.dt.float32r
U8 = mybir.dt.uint8
ALU = mybir.AluOpType
ACT = mybir.ActivationFunctionType
AX = mybir.AxisListType

P = 128
EPS = 1e-6
ROUTED_SCALE = 2.5
TOPK_GROUPS = 4
LOG_DECAY_FLOOR = 2.0611536e-09
NEVER = 3.0e38
TAKEN = 3.3e38
HALVES = (64, 32, 16, 8)
BASE = 8
LAYER_DVE = 92
NSLOT = 2
GSLOT = 4

CONST_COLS = (("ident", 128), ("tri_f", 128), ("tri_b", 128), ("past_f", 128), ("past_b", 128), ("rot", 128),
              ("c_ctx", 128), ("s_ctx", 128), ("c_chan", 128), ("s_chan", 128), ("cos", 256), ("sin", 256),
              ("c_lat", 512), ("s_lat", 512), ("tie", 64))


def const_offsets():
    out, at = {}, 0
    for name, width in CONST_COLS:
        out[name] = (at, at + width)
        at += width
    return out, at


class Signal:

    def __init__(self, sem, start=0, layer=1):
        self.sem, self.start, self.layer = sem, start, layer

    def at(self, l, n):
        return self.start + l * self.layer + n


class InOrder:

    def __init__(self, eng, sem, start, layer, depth):
        self.eng, self.sem, self.start, self.layer, self.depth = eng, sem, start, layer, depth
        self.base, self.n, self.seen = 0, 0, {}

    def enter(self, phase, l=0):
        self.seen[phase] = 0
        self.phase = phase
        self.base = {"start": 0, "layer": self.start + l * self.layer, "final": self.start + self.depth * self.layer}[phase]
        self.n = 0

    def leave(self):
        want = {"start": self.start, "layer": self.layer}.get(self.phase, self.n)
        assert self.n == want, (self.phase, self.n, want)

    def after(self, ins):
        self.n += 1
        ins.then_inc(self.sem, 1)
        self.eng.wait_ge(self.sem, self.base + self.n)


class Banks:

    def __init__(self, banks, full, empty, depth):
        self.banks, self.full_sem, self.empty_sem, self.depth = banks, full, empty, depth
        self.count = {"start": [0] * 8, "layer": [0] * 8, "final": [0] * 8}
        self.uses = {"start": {}, "layer": {}, "final": {}}
        self.turn = 0

    def plan(self, phase, stage, n, bank=None, each=1):
        for i in range(n):
            b = bank[i] if bank is not None else self.turn % 8
            if bank is None:
                self.turn += 1
            self.uses[phase][stage, i] = (b, self.count[phase][b])
            self.count[phase][b] += each

    def plan_one(self, phase, stage, i, bank):
        self.uses[phase][stage, i] = (bank, self.count[phase][bank])
        self.count[phase][bank] += 1

    def enter(self, phase, l=0):
        self.phase, self.l = phase, l

    def _at(self, stage, i, more):
        b, nth = self.uses[self.phase][stage, i]
        if self.phase != "start":
            nth = nth + self.count["start"][b]
        if self.phase == "layer":
            nth = self.l * self.count["layer"][b] + nth
        if self.phase == "final":
            nth = nth + self.depth * self.count["layer"][b]
        return b, nth + more

    def claim(self, pe, stage, i=0, more=0):
        b, v = self._at(stage, i, more)
        pe.wait_ge(self.empty_sem[b], v + 1)
        return self.banks[b]

    def filled(self, ins, stage, i=0):
        ins.then_inc(self.full_sem[self.uses[self.phase][stage, i][0]], 1)

    def read(self, eng, stage, i=0, more=0):
        b, v = self._at(stage, i, more + 1)
        eng.wait_ge(self.full_sem[b], v)
        return self.banks[b]

    def emptied(self, ins, stage, i=0):
        ins.then_inc(self.empty_sem[self.uses[self.phase][stage, i][0]], 1)

    def wait_emptied(self, eng, stage, i=0, more=0):
        b, v = self._at(stage, i, more + 1)
        eng.wait_ge(self.empty_sem[b], v + 1)


def trunk_program(nc, T, CF, CM, y_prompt, y_sample, new_k, new_v, new_state):
    DEPTH, _, _, DH, VD = T["cache_k"].shape[1], 0, 0, T["cache_k"].shape[3], T["cache_k"].shape[4]
    D = T["x_prompt"].shape[2]
    NJ = D // P
    NTILE = (T["x_prompt"].shape[1] + T["x_sample"].shape[1]) // P
    TOK = NTILE * P
    SPAN = (slice(0, P), slice(P, TOK))
    DK = VD // 2
    HH, HK = T["state_hgrn"].shape[3], T["state_hgrn"].shape[4]
    HW = HH * HK
    DA = DH * VD
    FN = T["w_fourier"].shape[1]
    E = T["w_router"].shape[2]
    NG = 8
    PG = E // NG
    PROJ = T["w_in"].shape[2]
    KEYS = TOK + T["cache_k"].shape[2]
    SCALE = DK ** -0.5
    Q0, K0, V0, HQ0, HI0, HB0 = FN, FN + DA, FN + 2 * DA, FN + 3 * DA, FN + 3 * DA + HW, FN + 3 * DA + 3 * HW
    assert PROJ == HB0 + 2 * HW and NTILE == 3 and D == 1024 and E % NSLOT == 0

    ctx = ExitStack()
    with ctx:
        def sb(name, shape, dt=F32):
            return ctx.enter_context(nc.sbuf_tensor(name, shape, dt))

        def sem(name):
            return ctx.enter_context(nc.semaphore(name))

        ring = sb("ring", [P, NSLOT, 4096])
        x = sb("x", [P, NJ, TOK])
        h_at = nc.sbuf_base + -nc.sbuf_base % 32
        h = sb("h", [P, NJ, TOK])
        h_lo = nc.alloc_sbuf_tensor_at("h_lo", [P, NJ, TOK], F32R, offset=h_at)
        slab_at = nc.sbuf_base + -nc.sbuf_base % 32
        slab = sb("slab", [P, 12 * D])
        slab_used = [0]

        def mixer(*shape):
            n = 1
            for k in shape:
                n *= k
            a = slab_used[0]
            slab_used[0] += n
            assert slab_used[0] <= 12 * D
            v = slab[:, a:a + n]
            return v.rearrange("p (a b) -> p a b", a=shape[0]) if len(shape) == 2 else v

        def overlay(name, shape, at):
            return nc.alloc_sbuf_tensor_at(name, shape, F32R, offset=at)

        gu_hi = overlay("gu_hi", [P, 2, 2 * D], slab_at)
        gu_lo = overlay("gu_lo", [P, 2, 2 * D], slab_at + 16 * D)
        dn_hi = overlay("dn_hi", [P, 2, D], slab_at + 32 * D)
        dn_lo = overlay("dn_lo", [P, 2, D], slab_at + 40 * D)
        h_hi = sb("h_hi", [P, NJ, TOK], F32R)
        act_hi = sb("act_hi", [P, 2, TOK], F32R)
        big = sb("big", [P, NJ * TOK])
        squares = big[:, :].rearrange("p (j t) -> p j t", j=NJ)
        mixT = squares
        rows = big[:, :].rearrange("p (i d) -> p i d", i=NTILE)
        aT = sb("aT", [P, 2, NTILE, 4 * P])
        w_shared = aT[:, :, :, :].rearrange("p d i t -> p (d i t)")
        work_at = nc.sbuf_base + -nc.sbuf_base % 32
        work = sb("work", [P, 12 * TOK])
        act_lo = nc.alloc_sbuf_tensor_at("act_lo", [P, 2, TOK], F32R, offset=work_at + 40 * TOK)

        def part(a, b, inner=TOK):
            return work[:, a * TOK:b * TOK].rearrange("p (c t) -> p c t", t=inner)

        hflat = h[:, :, :].rearrange("p j t -> p (j t)")
        rstd = sb("rstd", [P, TOK])
        rms = sb("rms", [P, TOK])
        consts = sb("consts", [P, CF.shape[1]])
        masks = sb("masks", [P, 2 * (len(HALVES) + 1), P], U8)
        masks_f = hflat[:, 0:2 * (len(HALVES) + 1) * P].rearrange("p (m t) -> p m t", t=P)
        ones = sb("ones", [P, P])
        eps_t = sb("eps_t", [P, 1])
        cond = sb("cond", [P, 2, NJ])
        scond = sb("scond", [P, NJ, 2])
        mod = sb("mod", [P, 6, NJ, 2])
        gain = sb("gain", [P, NJ, 2])
        mod_rows = sb("mod_rows", [2, 2, D])
        b_ada = sb("b_ada", [P, 6, NJ])
        norm_g = sb("norm_g", [P, 2, NJ])
        attn_g = sb("attn_g", [P, VD])
        hg_g = sb("hg_g", [P, HK])
        lambdas = sb("lambdas", [P, 4, DK])
        lam_init = sb("lam_init", [P, 2])
        r_bias = sb("r_bias", [P, E])
        w_four = mixer(2, FN)
        w_router = sb("w_router", [P, NJ, E])
        cache_k = mixer(DA)
        cache_v = mixer(DA)
        state0 = sb("state0", [P, 4, HK])
        final_g = sb("final_g", [P, NJ])
        lb_all = sb("lb_all", [P, DEPTH, 2 * HW])
        lb = sb("lb", [P, 2 * HW])
        om = sb("om", [P, 2 * HW])
        qT = mixer(DH, TOK)
        kT = mixer(DH, KEYS)
        val = mixer(NTILE, DA)
        k_rows = mixer(DA)
        rot_t = mixer(2, 256)
        lam_p = sb("lam_p", [P, 2, DK])
        lam_s = sb("lam_s", [P, 2])
        neg_lam = sb("neg_lam", [P, 1])
        top = sb("top", [P, 2, 2])
        ntop = sb("ntop", [P, 2, 2])
        den = sb("den", [P, 2, 2])
        rden = sb("rden", [P, 2, 2])
        prob = hflat[:, 0:4 * TOK].rearrange("p (a m t) -> p a m t", a=2, m=2)
        wts = hflat[:, 4 * TOK:6 * TOK].rearrange("p (a t) -> p a t", a=2)
        wT = hflat[:, 6 * TOK:8 * TOK].rearrange("p (a t) -> p a t", a=2)
        logf = mixer(NTILE, 2 * HW)
        att = logf
        att_r = sb("att_r", [P, 2, NTILE * DH])
        u_fn = mixer(NTILE, FN)
        ho = u_fn
        four1 = part(0, 4)
        att_sq = part(0, 4, DA)
        zT = part(4, 6)
        hqT = mixer(2, TOK)
        hv = mixer(NTILE, HW)
        gate_o = mixer(NTILE, HW)
        kk = part(6, 10, 2 * HW)
        kkT = hflat[:, 0:4 * TOK].rearrange("p (g t) -> p g t", g=4)
        cum = hflat[:, 4 * TOK:8 * TOK].rearrange("p (g t) -> p g t", g=4)
        qdec = big[:, 2 * TOK:6 * TOK].rearrange("p (g t) -> p g t", g=4)
        kdec = logf[:, :, :].rearrange("p i f -> p (i f)")[:, 0:4 * HW].rearrange("p (g f) -> p g f", g=4)
        diff = part(0, 2)
        fac = part(2, 4)
        fac2 = part(4, 6)
        pair = work[:, 6 * TOK:10 * TOK].rearrange("p (a c t) -> p a c t", a=2, c=2)
        pair2 = part(10, 12)
        st_out = sb("st_out", [P, 4, HK])
        st_mid = sb("st_mid", [P, 4, HK])
        ho_sq = big[:, 6 * TOK:8 * TOK].rearrange("p (i f) -> p i f", i=NTILE)
        ho_r = sb("ho_r", [P, 2, NTILE * HH])
        edge = sb("edge", [P, 4])
        tick = sb("tick", [P, 1])
        at = [0]

        def scratch(*shape):
            n = 1
            for k in shape:
                n *= k
            v = work[:, at[0]:at[0] + n]
            at[0] += n
            assert at[0] <= 8 * TOK
            return v.rearrange("p (a b) -> p a b", a=shape[0]) if len(shape) == 2 else v

        score, biased, gsel = scratch(NTILE, E), scratch(NTILE, E), scratch(NTILE, E)
        tops, gsum = scratch(NTILE * NG, 8), scratch(NTILE, NG)
        cmp_a, cmp_b = scratch(NTILE, NG * NG), scratch(NTILE, NG * NG)
        rank, gpen, best, wsum = scratch(NTILE * NG), scratch(NTILE * NG), scratch(NTILE, 8), scratch(NTILE)
        gatesT = sb("gatesT", [E, TOK])
        gate_b = work[:, 0:8 * TOK].rearrange("p (i s t) -> p i s t", i=2, s=GSLOT)
        sil = part(8, 10)
        act = part(10, 12)

        coff, _ = const_offsets()

        def const(name):
            a, b = coff[name]
            return consts[:, a:b]

        ident = const("ident")
        gates_dram = nc.dram_tensor("gates_scratch", (E, TOK), F32, kind="Internal").ap()

        banks = Banks([ctx.enter_context(nc.psum_tensor(f"bank{b}", [P, 512], F32)) for b in range(8)],
                      [sem(f"bank{b}_full") for b in range(8)], [sem(f"bank{b}_empty") for b in range(8)], DEPTH)
        LEVELS = len(HALVES) + 1
        banks.plan("start", "xT", 2 * NTILE)
        banks.turn = 0
        for stage, n in (("ada0", 2), ("ms1", 1), ("modT0", 1), ("ada1", 2), ("modT1", 1), ("ada2", 2),
                         ("q", DH), ("modT2", 1), ("k", DH), ("v", NTILE), ("fn", NTILE), ("hq", 2),
                         ("hif", NTILE), ("hbg", NTILE), ("k_rows", 1), ("ckT", 1), ("rotq", 2), ("rotk", 2),
                         ("four1", 4), ("zT", 2), ("fnT", 2), ("ada3", 2), ("kkT", 4), ("cum", 4), ("past", 2), ("modT3", 1),
                         ("lev", 4 * LEVELS * NTILE), ("st", 2), ("ho", 2)):
            banks.plan("layer", stage, n)
        UNITS = [(t, hd) for t in range(NTILE) for hd in range(DH)]
        NU = len(UNITS)
        ring6 = 0
        for u in range(NU + 3):
            if u < NU:
                for m in range(2):
                    banks.plan_one("layer", "sc", 2 * u + m, ring6 % 6)
                    ring6 += 1
            if 2 <= u < NU + 2:
                banks.plan_one("layer", "wT", u - 2, ring6 % 6)
                ring6 += 1
            if u >= 3 and UNITS[u - 3][1] == 0:
                banks.plan_one("layer", "o", UNITS[u - 3][0], 6 + UNITS[u - 3][0] % 2)
        banks.turn = 0
        for stage, n in (("ada4", 2), ("oT", NTILE), ("hgT", 2), ("modT4", 1)):
            banks.plan("layer", stage, n)
        for stage, n in (("out", NJ), ("ada5", 2), ("ms2", 1), ("router", 1), ("modT5", 1), ("gT", 1)):
            banks.plan("layer", stage, n)
        banks.plan("layer", "G", 1, [6], each=E + 1)
        banks.plan("layer", "U", 1, [7], each=E + 1)
        banks.plan("layer", "y", 6, range(6))
        banks.turn = 0
        banks.plan("layer", "yT", NJ)
        banks.plan("final", "ms", 1)
        banks.plan("final", "rows", 2 * NTILE)

        waited = sem("waited")
        consts_in = sem("consts_in")
        params_in = sem("params_in")
        slot_full = [sem(f"slot{s}_full") for s in range(NSLOT)]
        slot_read = sem("slot_read")
        slots_idle = Signal(sem("slots_idle"), 1, 1)
        aT_zero = Signal(sem("aT_zero"))
        shared_in = sem("shared_in")
        gates_out = sem("gates_out")
        gate_in = [sem(f"gate{i}_in") for i in range(2)]
        results_out = sem("results_out")
        y_out = sem("y_out")
        squared = Signal(sem("squared"), 0, 2)
        h_ready = Signal(sem("h_ready"), 0, 2)
        scond_ready = sem("scond_ready")
        ones_ready = sem("ones_ready")
        rope_done = Signal(sem("rope_done"))
        fgate_ready = Signal(sem("fgate_ready"))
        logf_ready = Signal(sem("logf_ready"))
        kk_ready = Signal(sem("kk_ready"))
        lam_sum = Signal(sem("lam_sum"))
        lam_exp = Signal(sem("lam_exp"))
        ecum_ready = Signal(sem("ecum_ready"))
        qdec_ready = Signal(sem("qdec_ready"))
        kdec_ready = Signal(sem("kdec_ready"))
        NLEV = 2 * LEVELS
        diff_ready = Signal(sem("diff_ready"), 0, NLEV)
        fac_ready = Signal(sem("fac_ready"), 0, NLEV)
        pair_ready = Signal(sem("pair_ready"), 0, NLEV)
        sums_ready = Signal(sem("sums_ready"))
        roots_ready = Signal(sem("roots_ready"))
        hnorm_ready = Signal(sem("hnorm_ready"))
        ntop_ready = Signal(sem("ntop_ready"), 0, NU)
        wts_ready = Signal(sem("wts_ready"), 0, NU)
        anorm_ready = Signal(sem("anorm_ready"))
        gsel_ready = Signal(sem("gsel_ready"))
        VIS = E + 1
        gu_hi_ready, gu_lo_ready = Signal(sem("gu_hi_ready"), 0, VIS), Signal(sem("gu_lo_ready"), 0, VIS)
        dn_hi_ready, dn_lo_ready = Signal(sem("dn_hi_ready"), 0, VIS), Signal(sem("dn_lo_ready"), 0, VIS)
        h_hi_ready, h_lo_ready = Signal(sem("h_hi_ready")), Signal(sem("h_lo_ready"))
        act_ready = Signal(sem("act_ready"), 0, VIS)
        act_hi_ready = Signal(sem("act_hi_ready"), 0, VIS)
        act_lo_ready = Signal(sem("act_lo_ready"), 0, VIS)
        applied = Signal(sem("applied"), 0, VIS - 1)
        x_ready = Signal(sem("x_ready"), 1, 2)
        final_ready = sem("final_ready")
        lb_diff = sem("lb_diff")
        lb_exp = sem("lb_exp")
        dve_order, act_order = sem("dve_order"), sem("act_order")

        w_ada_v = T["w_ada"].rearrange("l (p j) n -> l p j n", j=NJ)
        w_in_v = T["w_in"].rearrange("l (p j) n -> l p j n", j=NJ)
        w_out_v = T["w_out"].rearrange("l (c p) n -> l p c n", p=P)
        w_gate_v = T["w_gate"].rearrange("l e (p j) f -> l e p (j f)", j=NJ)
        w_up_v = T["w_up"].rearrange("l e (p j) f -> l e p (j f)", j=NJ)
        w_down_v = T["w_down"]

        def in_cols(l, c0, n):
            return w_in_v[l][:, :, c0:c0 + n]

        fixed = []

        def modulation_blocks(m):
            for half in range(2):
                fixed.append((f"ada{m}", [(4, 1024, 0, lambda l, m=m, half=half:
                                           w_ada_v[l][:, 4 * half:4 * half + 4, m * D:(m + 1) * D])]))

        for m in range(3):
            modulation_blocks(m)
        for name, c0 in (("q", Q0), ("k", K0), ("v", V0)):
            fixed.append((name, [(NJ, 512, 0, lambda l, c0=c0: in_cols(l, c0, 512))]))
        fixed.append(("fn+hq", [(NJ, 256, 0, lambda l: in_cols(l, 0, 256)), (NJ, 256, 2048, lambda l: in_cols(l, HQ0, 256))]))
        fixed.append(("hif", [(NJ, 512, 0, lambda l: in_cols(l, HI0, 512))]))
        fixed.append(("hbg", [(NJ, 512, 0, lambda l: in_cols(l, HB0, 512))]))
        for m in (3, 4):
            modulation_blocks(m)
        for half in range(2):
            fixed.append(("out", [(4, 1024, 0, lambda l, half=half: w_out_v[l][:, 4 * half:4 * half + 4, :])]))
        modulation_blocks(5)
        NFIX = len(fixed)
        NBLK = NFIX + E
        assert NFIX % NSLOT == 0
        landed, fix_sum = [], [0] * NSLOT
        for b, (_, parts) in enumerate(fixed):
            fix_sum[b % NSLOT] += 16 * len(parts)
            landed.append(fix_sum[b % NSLOT])
        slot_layer = [fix_sum[s] + 48 * (E // NSLOT) for s in range(NSLOT)]

        def block_in(eng, l, b):
            eng.wait_ge(slot_full[b % NSLOT], l * slot_layer[b % NSLOT] + landed[b])
            return ring[:, b % NSLOT, :]

        def block_of(name, nth=0):
            return [b for b, (n, _) in enumerate(fixed) if n == name][nth]

        last_fill = {block_of("q"): ("q", DH - 1), block_of("k"): ("k", DH - 1), block_of("v"): ("v", NTILE - 1),
                     block_of("fn+hq"): ("hq", 1), block_of("hif"): ("hif", NTILE - 1), block_of("hbg"): ("hbg", NTILE - 1),
                     block_of("out", 1): ("out", NJ - 1)}
        for m in range(6):
            last_fill[block_of(f"ada{m}", 1)] = (f"ada{m}", 1)
        READS = NFIX - len(last_fill)

        def slot_released(sp, l, b):
            prev = b - NSLOT
            if prev < 0:
                sp.wait_ge(slots_idle.sem, slots_idle.at(l, 0))
            elif prev in last_fill:
                banks.read(sp, *last_fill[prev])
            else:
                sp.wait_ge(slot_read, l * READS + sum(1 for k in range(prev + 1) if k not in last_fill))
            apart(sp)

        NCONST, NPARAM = 8, 12

        def apart(eng):
            eng.sem_inc(waited, 1)

        block = ctx.enter_context(nc.Block())

        @block.sync
        def _(sp):
            sp.dma_start(rows[:, 0, :], T["x_prompt"][0]).then_inc(consts_in, 16)
            sp.dma_start(rows[:, 1:3, :], T["x_sample"][0].rearrange("(i p) d -> p i d", p=P)).then_inc(consts_in, 16)
            sp.dma_start(consts[:, :], CF).then_inc(consts_in, 16)
            sp.dma_start(masks_f, CM.rearrange("m p t -> p m t")).then_inc(consts_in, 16)
            sp.dma_start(cond[:, 0, :], T["c_ctx"].rearrange("(p j) -> p j", j=NJ)).then_inc(consts_in, 16)
            sp.dma_start(cond[:, 1, :], T["c"][0].rearrange("(p j) -> p j", j=NJ)).then_inc(consts_in, 16)
            sp.dma_start(final_g[:, :], T["final_g"].rearrange("(p j) -> p j", j=NJ)).then_inc(consts_in, 16)
            sp.dma_start(lb_all[:, :, :], T["lower_bounds"].rearrange("l d w -> l (d w)").partition_broadcast(P))\
              .then_inc(consts_in, 16)
            with sp.Fori(0, DEPTH) as l:
                banks.enter("layer", l)
                for b, (_, parts) in enumerate(fixed):
                    slot_released(sp, l, b)
                    for j, n, at, src in parts:
                        dst = ring[:, b % NSLOT, at:at + j * n].rearrange("p (j n) -> p j n", j=j)
                        sp.dma_start(dst, src(l)).then_inc(slot_full[b % NSLOT], 16)

                def load_expert(s, e):
                    sp.dma_start(ring[:, s, 0:D], w_gate_v[l, e]).then_inc(slot_full[s], 16)
                    sp.dma_start(ring[:, s, D:2 * D], w_up_v[l, e]).then_inc(slot_full[s], 16)
                    sp.dma_start(ring[:, s, 2 * D:3 * D], w_down_v[l, e]).then_inc(slot_full[s], 16)

                for s in range(NSLOT):
                    slot_released(sp, l, NFIX + s)
                    load_expert(s, s)
                with sp.Fori(1, E // NSLOT) as turn:
                    for s in range(NSLOT):
                        sp.wait_ge(dn_lo_ready.sem, l * VIS + turn * NSLOT + s)
                        load_expert(s, turn * NSLOT + s)
            banks.enter("final")
            for i in range(2 * NTILE):
                banks.wait_emptied(sp, "rows", i)
            sp.dma_start(y_prompt[0], rows[:, 0, :]).then_inc(y_out, 16)
            sp.dma_start(y_sample[0].rearrange("(i p) d -> p i d", p=P), rows[:, 1:3, :]).then_inc(y_out, 16)
            sp.wait_ge(y_out, 32)
            sp.wait_ge(results_out, 48 * DEPTH)

        @block.gpsimd
        def _(pool):
            def over_partitions(ap):
                return ap.partition_broadcast(P)

            with pool.Fori(0, DEPTH) as l:
                pool.wait_ge(x_ready.sem, x_ready.at(l, 0))
                apart(pool)
                for dst, src in (
                    (b_ada[:, :, :], T["b_ada"][l].rearrange("(m p j) -> p m j", p=P, j=NJ)),
                    (norm_g[:, :, :], T["norm_g"][l].rearrange("m (p j) -> p m j", j=NJ)),
                    (attn_g[:, :], over_partitions(T["attn_norm_g"][l])),
                    (hg_g[:, :], over_partitions(T["hg_norm_g"][l])),
                    (lambdas[:, :, :], over_partitions(T["lambdas"][l])),
                    (lam_init[:, :], over_partitions(T["lam_init"][l])),
                    (r_bias[:, :], over_partitions(T["router_bias"][l])),
                    (w_four[:, :, :], T["w_fourier"][l].rearrange("(c p) n -> p c n", p=P)),
                    (w_router[:, :, :], T["w_router"][l].rearrange("(p j) e -> p j e", j=NJ)),
                    (cache_k[:, :], T["cache_k"][0][l].rearrange("t h d -> t (h d)")),
                    (cache_v[:, :], T["cache_v"][0][l].rearrange("t h d -> t (h d)")),
                    (state0[:, :, :], T["state_hgrn"][0][l].rearrange("d (a b) k v -> (b k) (d a) v", b=2)),
                ):
                    pool.dma_start(dst, src).then_inc(params_in, 16)
                nc.gpsimd.memset(w_shared, 0.0).then_inc(aT_zero.sem, 1)
                banks.enter("layer", l)
                banks.wait_emptied(pool, "v", 0)
                apart(pool)
                pool.dma_start(new_v[0][l].rearrange("t h d -> t (h d)"), val[:, 0, :]).then_inc(results_out, 16)
                banks.wait_emptied(pool, "k_rows")
                apart(pool)
                pool.dma_start(new_k[0][l].rearrange("t h d -> t (h d)"), k_rows[:, :]).then_inc(results_out, 16)
                banks.wait_emptied(pool, "st", 0)
                apart(pool)
                pool.dma_start(new_state[0][l].rearrange("d (a b) k v -> (b k) (d a) v", b=2), st_out[:, :, :])\
                    .then_inc(results_out, 16)
                banks.read(pool, "ho", 1)
                apart(pool)
                for i, src in enumerate((T["ws_gate"][l].rearrange("(p j) f -> p (j f)", j=NJ),
                                         T["ws_up"][l].rearrange("(p j) f -> p (j f)", j=NJ), T["ws_down"][l])):
                    pool.dma_start(w_shared[:, i * D:(i + 1) * D], src).then_inc(shared_in, 16)
                pool.wait_ge(results_out, l * 48 + 48)
                banks.wait_emptied(pool, "gT")
                apart(pool)
                pool.dma_start(gates_dram, gatesT[:, :]).then_inc(gates_out, 16)
                pool.wait_ge(gates_out, l * 16 + 16)
                apart(pool)

                def load_gates(i, e0):
                    pool.dma_start(gate_b[:, i, :, :].rearrange("p e t -> p (e t)"),
                                   over_partitions(gates_dram[bass.ds(e0, GSLOT), :].rearrange("e t -> (e t)")))\
                        .then_inc(gate_in[i], 16)

                for i in range(2):
                    load_gates(i, i * GSLOT)
                with pool.Fori(0, E // (2 * GSLOT) - 1) as turn:
                    for i in range(2):
                        pool.wait_ge(act_ready.sem, l * VIS + turn * (2 * GSLOT) + (1 + (i + 1) * GSLOT))
                        apart(pool)
                        load_gates(i, turn * (2 * GSLOT) + (2 + i) * GSLOT)

        @block.tensor
        def _(pe):
            mm = nc.tensor.matmul
            tr = nc.tensor.transpose
            pe.wait_ge(consts_in, 16 * NCONST)
            pe.wait_ge(ones_ready, 1)
            banks.enter("start")
            for bank_empty in banks.empty_sem:
                pe.sem_inc(bank_empty, 1)
            for t in range(NTILE):
                for half in range(2):
                    bk = banks.claim(pe, "xT", 2 * t + half)
                    for j in range(4):
                        last = tr(bk[:, j * P:(j + 1) * P], rows[:, t, 4 * half + j:D:NJ], ident)
                    banks.filled(last, "xT", 2 * t + half)
            pe.wait_ge(scond_ready, 1)

            def mean_square(stage):
                bk = banks.claim(pe, stage)
                for j in range(NJ):
                    last = mm(bk[:, 0:TOK], ones[:, :], squares[:, j, :], start=(j == 0), stop=(j == NJ - 1))
                banks.filled(last, stage)

            with pe.Fori(0, DEPTH) as l:
                banks.enter("layer", l)

                def modulation_product(m, halves=(0, 1)):
                    for half in halves:
                        b = block_of(f"ada{m}", half)
                        w = block_in(pe, l, b).rearrange("p (j n) -> p j n", j=4)
                        for ji in range(4):
                            for c in range(2):
                                if half == 0 and ji == 0:
                                    banks.claim(pe, f"ada{m}", c)
                                bk = banks.banks[banks.uses["layer"][f"ada{m}", c][0]]
                                last = mm(bk[0:2, :], scond[:, 4 * half + ji, :], w[:, ji, c * 512:(c + 1) * 512],
                                          start=(half == 0 and ji == 0), stop=(half == 1 and ji == 3))
                                if half == 1 and ji == 3:
                                    banks.filled(last, f"ada{m}", c)
                        if half == 0:
                            last.then_inc(slot_read, 1)

                def modulation_turned(m):
                    for c in range(2):
                        banks.wait_emptied(pe, f"ada{m}", c)
                    bk = banks.claim(pe, f"modT{m}")
                    apart(pe)
                    for j in range(NJ):
                        last = tr(bk[:, 2 * j:2 * j + 2], mod_rows[0:2, m % 2, j:D:NJ], ident[0:2, 0:2])
                    banks.filled(last, f"modT{m}")

                modulation_product(0)
                pe.wait_ge(squared.sem, squared.at(l, 1))
                mean_square("ms1")
                modulation_turned(0)
                modulation_product(1)
                modulation_turned(1)
                modulation_product(2)

                pe.wait_ge(h_ready.sem, h_ready.at(l, 1))
                for stage in ("q", "k"):
                    w = block_in(pe, l, block_of(stage)).rearrange("p (j n) -> p j n", j=NJ)
                    for i in range(DH):
                        bk = banks.claim(pe, stage, i)
                        for j in range(NJ):
                            last = mm(bk[:, 0:TOK], w[:, j, i * P:(i + 1) * P], h[:, j, :], start=(j == 0), stop=(j == NJ - 1))
                        banks.filled(last, stage, i)
                    if stage == "q":
                        modulation_turned(2)

                def token_major(stage, w, n):
                    for t in range(NTILE):
                        bk = banks.claim(pe, stage, t)
                        for j in range(NJ):
                            last = mm(bk[:, 0:n], h[:, j, t * P:(t + 1) * P], w[:, j, 0:n], start=(j == 0), stop=(j == NJ - 1))
                        banks.filled(last, stage, t)

                token_major("v", block_in(pe, l, block_of("v")).rearrange("p (j n) -> p j n", j=NJ), DA)
                w = block_in(pe, l, block_of("fn+hq"))
                token_major("fn", w[:, 0:2048].rearrange("p (j n) -> p j n", j=NJ), FN)
                w = w[:, 2048:4096].rearrange("p (j n) -> p j n", j=NJ)
                for i in range(2):
                    bk = banks.claim(pe, "hq", i)
                    for j in range(NJ):
                        last = mm(bk[:, 0:TOK], w[:, j, i * P:(i + 1) * P], h[:, j, :], start=(j == 0), stop=(j == NJ - 1))
                    banks.filled(last, "hq", i)
                token_major("hif", block_in(pe, l, block_of("hif")).rearrange("p (j n) -> p j n", j=NJ), 2 * HW)
                token_major("hbg", block_in(pe, l, block_of("hbg")).rearrange("p (j n) -> p j n", j=NJ), 2 * HW)

                bk = banks.claim(pe, "k_rows")
                for i in range(DH):
                    banks.wait_emptied(pe, "k", i)
                    last = tr(bk[:, i * P:(i + 1) * P], kT[:, i, 0:P], ident)
                banks.filled(last, "k_rows")
                bk = banks.claim(pe, "ckT")
                pe.wait_ge(params_in, l * (16 * NPARAM) + 16 * NPARAM)
                for i in range(DH):
                    last = tr(bk[:, i * P:(i + 1) * P], cache_k[:, i * P:(i + 1) * P], ident)
                banks.filled(last, "ckT")
                for stage, src in (("rotq", qT), ("rotk", kT)):
                    for i in range(2):
                        bk = banks.claim(pe, stage, i)
                        for a in range(2):
                            banks.wait_emptied(pe, "q" if src is qT else "k", 2 * i + a)
                            last = mm(bk[:, a * 256:(a + 1) * 256], const("rot"), src[:, 2 * i + a, P:TOK], start=True, stop=True)
                        banks.filled(last, stage, i)

                for c in range(2):
                    for k, (cc, cl) in enumerate((("c_ctx", "c_lat"), ("s_ctx", "s_lat"))):
                        bk = banks.claim(pe, "four1", 2 * c + k)
                        banks.wait_emptied(pe, "fn", 0)
                        mm(bk[:, 0:P], u_fn[:, 0, c * P:(c + 1) * P], const(cc), start=True, stop=True)
                        for t in range(2):
                            banks.wait_emptied(pe, "fn", 1 + t)
                            last = mm(bk[:, P:TOK], u_fn[:, 1 + t, c * P:(c + 1) * P], const(cl)[:, t * 256:(t + 1) * 256],
                                      start=(t == 0), stop=(t == 1))
                        banks.filled(last, "four1", 2 * c + k)
                for c in range(2):
                    bk = banks.claim(pe, "zT", c)
                    for k, name in enumerate(("c_chan", "s_chan")):
                        banks.wait_emptied(pe, "four1", 2 * c + k)
                        last = mm(bk[:, 0:TOK], const(name), four1[:, 2 * c + k, :], start=(k == 0), stop=(k == 1))
                    banks.filled(last, "zT", c)
                for c in range(2):
                    bk = banks.claim(pe, "fnT", c)
                    for k in range(2):
                        banks.wait_emptied(pe, "zT", k)
                        last = mm(bk[:, 0:TOK], w_four[:, k, c * P:(c + 1) * P], zT[:, k, :], start=(k == 0), stop=(k == 1))
                    banks.filled(last, "fnT", c)

                modulation_product(3)
                pe.wait_ge(kk_ready.sem, kk_ready.at(l, 1))
                for g in range(4):
                    bk = banks.claim(pe, "kkT", g)
                    for t in range(NTILE):
                        last = tr(bk[:, t * P:(t + 1) * P], kk[:, t, g * P:(g + 1) * P], ident)
                    banks.filled(last, "kkT", g)
                pe.wait_ge(logf_ready.sem, logf_ready.at(l, 1))
                for g in range(4):
                    bk = banks.claim(pe, "cum", g)
                    for t in range(NTILE):
                        last = mm(bk[:, t * P:(t + 1) * P], logf[:, t, g * P:(g + 1) * P], const("tri_f" if g < 2 else "tri_b"),
                                  start=True, stop=True)
                    banks.filled(last, "cum", g)
                for i, tiles in enumerate(((0, 0), (1, 2))):
                    bk = banks.claim(pe, "past", i)
                    for d, t in enumerate(tiles):
                        last = mm(bk[:, d * HW:(d + 1) * HW], const("past_f" if d == 0 else "past_b"),
                                  logf[:, t, d * HW:(d + 1) * HW], start=True, stop=True)
                    banks.filled(last, "past", i)
                modulation_turned(3)

                for n in range(NLEV):
                    lv = n % LEVELS
                    ka = pair[:, n % 2, :, :]
                    qa = ka if lv < LEVELS - 1 else pair2[:, :, :]
                    pe.wait_ge(pair_ready.sem, pair_ready.at(l, n + 1))
                    for t in range(NTILE):
                        for odd in range(2):
                            use = (n * NTILE + t) * 2 + odd
                            bk = banks.claim(pe, "lev", use)
                            r = slice(HK * odd, HK * (odd + 1))
                            for c in range(2):
                                last = mm(bk[:, c * P:(c + 1) * P], ka[r, c, t * P:(t + 1) * P],
                                          qa[r, c, t * P:(t + 1) * P], start=True, stop=True)
                            banks.filled(last, "lev", use)

                pe.wait_ge(kdec_ready.sem, kdec_ready.at(l, 1))
                for i, tiles in enumerate(((0, 0), (1, 2))):
                    bk = banks.claim(pe, "st", i)
                    for d, t in enumerate(tiles):
                        for a in range(2):
                            last = mm(bk[:, (2 * d + a) * P:(2 * d + a + 1) * P], kdec[:, 2 * i + d, a * P:(a + 1) * P],
                                      hv[:, t, a * P:(a + 1) * P], start=True, stop=True)
                    banks.filled(last, "st", i)

                pe.wait_ge(qdec_ready.sem, qdec_ready.at(l, 1))
                banks.wait_emptied(pe, "lev", 2 * NLEV * NTILE - 1)
                banks.wait_emptied(pe, "st", 1)
                for odd in range(2):
                    bk = banks.claim(pe, "ho", odd)
                    r = slice(HK * odd, HK * (odd + 1))
                    for t in range(NTILE):
                        for c in range(2):
                            hd = 2 * c + odd
                            out = bk[:, (2 * t + c) * HK:(2 * t + c + 1) * HK]
                            v = hv[:, t, hd * HK:(hd + 1) * HK]
                            mm(out, aT[:, 0, t, hd * P:(hd + 1) * P], v, start=True, stop=False)
                            last = mm(out, aT[:, 1, t, hd * P:(hd + 1) * P], v, start=False, stop=(t == 0))
                            if t > 0:
                                for d in range(2):
                                    src = state0 if (t == 1) == (d == 0) else st_mid
                                    last = mm(out, qdec[r, 2 * d + c, t * P:(t + 1) * P], src[r, 2 * d + c, :],
                                              start=False, stop=(d == 1))
                    banks.filled(last, "ho", odd)

                pe.wait_ge(rope_done.sem, rope_done.at(l, 1))
                for u in range(NU + 3):
                    if u < NU:
                        t, hd = UNITS[u]
                        keys = slice(0, P) if t == 0 else slice(P, KEYS)
                        for m in range(2):
                            bk = banks.claim(pe, "sc", 2 * u + m)
                            r = slice(m * DK, (m + 1) * DK)
                            last = mm(bk[:, 0:keys.stop - keys.start], qT[r, hd, t * P:(t + 1) * P], kT[r, hd, keys],
                                      start=True, stop=True)
                            banks.filled(last, "sc", 2 * u + m)
                    if 2 <= u < NU + 2:
                        v = u - 2
                        bk = banks.claim(pe, "wT", v)
                        pe.wait_ge(wts_ready.sem, wts_ready.at(l, v + 1))
                        for i in range(1 if UNITS[v][0] == 0 else 3):
                            last = tr(bk[:, i * P:(i + 1) * P], wts[:, v % 2, i * P:(i + 1) * P], ident)
                        banks.filled(last, "wT", v)
                    if u >= 3:
                        v = u - 3
                        t, hd = UNITS[v]
                        if hd == 0:
                            obk = banks.claim(pe, "o", t)
                        banks.wait_emptied(pe, "wT", v)
                        srcs = [val[:, 0, :]] if t == 0 else [val[:, 1, :], val[:, 2, :], cache_v[:, :]]
                        for i, src in enumerate(srcs):
                            last = mm(obk[:, hd * P:(hd + 1) * P], wT[:, v % 2, i * P:(i + 1) * P], src[:, hd * VD:(hd + 1) * VD],
                                      start=(i == 0), stop=(i == len(srcs) - 1))
                        if hd == DH - 1:
                            banks.filled(last, "o", t)
                modulation_product(4)
                for t in range(NTILE):
                    bk = banks.claim(pe, "oT", t)
                    pe.wait_ge(anorm_ready.sem, anorm_ready.at(l, 1))
                    for hd in range(DH):
                        last = tr(bk[:, hd * P:(hd + 1) * P], att[:, t, hd * P:(hd + 1) * P], ident)
                    banks.filled(last, "oT", t)
                pe.wait_ge(hnorm_ready.sem, hnorm_ready.at(l, 1))
                for c in range(2):
                    bk = banks.claim(pe, "hgT", c)
                    for t in range(NTILE):
                        last = tr(bk[:, t * P:(t + 1) * P], gate_o[:, t, c * P:(c + 1) * P], ident)
                    banks.filled(last, "hgT", c)
                modulation_turned(4)

                for c in range(2):
                    banks.wait_emptied(pe, "fnT", c)
                    banks.wait_emptied(pe, "hgT", c)
                for t in range(NTILE):
                    banks.wait_emptied(pe, "oT", t)
                for half in range(2):
                    w = block_in(pe, l, block_of("out", half)).rearrange("p (c n) -> p c n", c=4)
                    for j in range(NJ):
                        if half == 0:
                            banks.claim(pe, "out", j)
                        bk = banks.banks[banks.uses["layer"]["out", j][0]]
                        for c in range(4):
                            last = mm(bk[:, 0:TOK], w[:, c, j:D:NJ], mixT[:, 4 * half + c, :],
                                      start=(half == 0 and c == 0), stop=(half == 1 and c == 3))
                        if half == 1:
                            banks.filled(last, "out", j)
                    if half == 0:
                        last.then_inc(slot_read, 1)

                modulation_product(5, (0,))
                pe.wait_ge(squared.sem, squared.at(l, 2))
                mean_square("ms2")
                modulation_product(5, (1,))
                pe.wait_ge(h_ready.sem, h_ready.at(l, 2))
                bk = banks.claim(pe, "router")
                for t in range(NTILE):
                    for j in range(NJ):
                        last = mm(bk[:, t * E:(t + 1) * E], h[:, j, t * P:(t + 1) * P], w_router[:, j, :],
                                  start=(j == 0), stop=(j == NJ - 1))
                banks.filled(last, "router")

                def up(n, buf):
                    pe.wait_ge(gu_lo_ready.sem, l * VIS + n + 1)
                    for k, stage in enumerate(("G", "U")):
                        bk = banks.claim(pe, stage, 0, n)
                        for j in range(NJ):
                            cols = slice(k * D + j * P, k * D + (j + 1) * P)
                            mm(bk[:, 0:TOK], gu_hi[:, buf, cols], h_hi[:, j, :], start=(j == 0), stop=False)
                            mm(bk[:, 0:TOK], gu_hi[:, buf, cols], h_lo[:, j, :], start=False, stop=False)
                            last = mm(bk[:, 0:TOK], gu_lo[:, buf, cols], h_hi[:, j, :], start=False, stop=(j == NJ - 1))
                        banks.filled(last, stage)

                def down(n, buf, first, last_one):
                    pe.wait_ge(dn_lo_ready.sem, l * VIS + n + 1)
                    pe.wait_ge(act_lo_ready.sem, l * VIS + n + 1)
                    for t in range(NTILE):
                        rows_of = slice(t * P, (t + 1) * P)
                        for c in range(2):
                            if first:
                                banks.claim(pe, "y", 2 * t + c)
                            y, cols = banks.banks[2 * t + c][:, :], slice(c * 512, (c + 1) * 512)
                            mm(y, act_hi[:, buf, rows_of], dn_hi[:, buf, cols], start=first, stop=False)
                            mm(y, act_hi[:, buf, rows_of], dn_lo[:, buf, cols], start=False, stop=False)
                            last = mm(y, act_lo[:, buf, rows_of], dn_hi[:, buf, cols], start=False, stop=last_one)
                            if last_one:
                                banks.filled(last, "y", 2 * t + c)
                    if not last_one:
                        last.then_inc(applied.sem, 1)

                pe.wait_ge(h_lo_ready.sem, h_lo_ready.at(l, 1))
                up(0, 0)
                modulation_turned(5)
                pe.wait_ge(gsel_ready.sem, gsel_ready.at(l, 1))
                bk = banks.claim(pe, "gT")
                apart(pe)
                for t in range(NTILE):
                    last = tr(bk[0:E, t * P:(t + 1) * P], gsel[:, t, :], ident)
                banks.filled(last, "gT")
                up(1, 1)
                down(0, 0, True, False)
                with pe.Fori(0, E // 2 - 1) as turn:
                    for s in range(2):
                        up(turn * 2 + (s + 2), s)
                        down(turn * 2 + (s + 1), 1 - s, False, False)
                up(E, 0)
                down(E - 1, 1, False, False)
                down(E, 0, False, True)

                for i in range(6):
                    banks.wait_emptied(pe, "y", i)
                for j in range(NJ):
                    bk = banks.claim(pe, "yT", j)
                    for t in range(NTILE):
                        last = tr(bk[:, t * P:(t + 1) * P], rows[:, t, j:D:NJ], ident)
                    banks.filled(last, "yT", j)

            banks.enter("final")
            pe.wait_ge(squared.sem, squared.at(DEPTH, 1))
            mean_square("ms")
            pe.wait_ge(final_ready, 1)
            for t in range(NTILE):
                for half in range(2):
                    bk = banks.claim(pe, "rows", 2 * t + half)
                    for j in range(4):
                        last = tr(bk[:, j * P:(j + 1) * P], h[:, 4 * half + j, t * P:(t + 1) * P], ident)
                    banks.filled(last, "rows", 2 * t + half)

        @block.scalar
        def _(act_e):
            af = nc.scalar.activation
            order = InOrder(act_e, act_order, 0, 4, DEPTH)
            after = order.after

            act_e.wait_ge(consts_in, 16 * NCONST)
            af(scond[:, :, :], cond[:, :, :].rearrange("p s j -> p j s"), ACT.Silu).then_inc(scond_ready, 1)
            act_e.wait_ge(lb_diff, 1)
            af(kk[:, 1:3, :], kk[:, 1:3, :], ACT.Exp).then_inc(lb_exp, 1)

            def squares_of_x(state, count):
                act_e.wait_ge(x_ready.sem, state)
                af(squares, x[:, :, :], ACT.Square).then_inc(squared.sem, 1)

            def root_of_mean(stage):
                bk = banks.read(act_e, stage)
                banks.emptied(af(rms[:, :], bk[:, 0:TOK], ACT.Sqrt, bias=eps_t[:, :], scale=1.0 / D), stage)

            def rows_of_modulation(m):
                if m >= 2:
                    banks.read(act_e, f"modT{m - 2}")
                for c in range(2):
                    bk = banks.read(act_e, f"ada{m}", c)
                    banks.emptied(af(mod_rows[0:2, m % 2, c * 512:(c + 1) * 512], bk[0:2, :], ACT.Copy), f"ada{m}", c)

            with act_e.Fori(0, DEPTH) as l:
                order.enter("layer", l)
                banks.enter("layer", l)
                squares_of_x(x_ready.at(l, 0), 1)
                rows_of_modulation(0)
                root_of_mean("ms1")
                rows_of_modulation(1)
                rows_of_modulation(2)

                for stage, dst in (("q", qT), ("k", kT)):
                    for i in range(DH):
                        bk = banks.read(act_e, stage, i)
                        banks.emptied(af(dst[:, i, 0:TOK], bk[:, 0:TOK], ACT.Copy), stage, i)
                for t in range(NTILE):
                    bk = banks.read(act_e, "fn", t)
                    banks.emptied(af(u_fn[:, t, :], bk[:, 0:FN], ACT.Copy), "fn", t)
                for i in range(2):
                    bk = banks.read(act_e, "hq", i)
                    banks.emptied(af(hqT[:, i, :], bk[:, 0:TOK], ACT.Silu), "hq", i)
                for t in range(NTILE):
                    bk = banks.read(act_e, "hif", t)
                    af(hv[:, t, :], bk[:, 0:HW], ACT.Copy)
                    af(logf[:, t, 0:HW], bk[:, HW:2 * HW], ACT.Sigmoid)
                    banks.emptied(af(kk[:, t, 0:HW], bk[:, HW:2 * HW], ACT.Sigmoid, scale=-1.0), "hif", t)
                for t in range(NTILE):
                    bk = banks.read(act_e, "hbg", t)
                    af(logf[:, t, HW:2 * HW], bk[:, 0:HW], ACT.Sigmoid)
                    af(kk[:, t, HW:2 * HW], bk[:, 0:HW], ACT.Sigmoid, scale=-1.0)
                    banks.emptied(af(gate_o[:, t, :], bk[:, HW:2 * HW], ACT.Silu), "hbg", t)

                for i in range(4):
                    bk = banks.read(act_e, "four1", i)
                    banks.emptied(af(four1[:, i, :], bk[:, 0:TOK], ACT.Copy), "four1", i)
                for c in range(2):
                    bk = banks.read(act_e, "zT", c)
                    banks.emptied(af(zT[:, c, :], bk[:, 0:TOK], ACT.Copy), "zT", c)
                for c in range(2):
                    bk = banks.read(act_e, "fnT", c)
                    banks.emptied(af(mixT[:, c, :], bk[:, 0:TOK], ACT.Copy), "fnT", c)

                act_e.wait_ge(fgate_ready.sem, fgate_ready.at(l, 1))
                af(logf[:, :, :], logf[:, :, :], ACT.Ln).then_inc(logf_ready.sem, 1)
                rows_of_modulation(3)
                for g in range(4):
                    bk = banks.read(act_e, "kkT", g)
                    banks.emptied(af(kkT[:, g, :], bk[:, 0:TOK], ACT.Copy), "kkT", g)
                for g in range(4):
                    bk = banks.read(act_e, "cum", g)
                    banks.emptied(af(cum[:, g, :], bk[:, 0:TOK], ACT.Copy), "cum", g)
                banks.read(act_e, "past", 1)
                for i in range(2):
                    bk = banks.read(act_e, "past", i)
                    banks.emptied(af(kdec[:, 2 * i:2 * i + 2, :], bk[:, :], ACT.Exp), "past", i)
                for g in range(4):
                    banks.wait_emptied(act_e, "cum", g)
                af(qdec[:, :, :], cum[:, :, :], ACT.Exp).then_inc(ecum_ready.sem, 1)
                act_e.wait_ge(lam_sum.sem, lam_sum.at(l, 1))
                af(lam_s[:, :], lam_s[:, :], ACT.Exp).then_inc(lam_exp.sem, 1)

                for n in range(NLEV):
                    d, lv = divmod(n, LEVELS)
                    act_e.wait_ge(diff_ready.sem, diff_ready.at(l, n + 1))
                    if lv < LEVELS - 1:
                        w = HALVES[lv]
                        dv = diff[:, :, :].rearrange("p c t -> p (c t)").rearrange("p (b w) -> p b w", w=2 * w)
                        fv = fac[:, :, :].rearrange("p c t -> p (c t)").rearrange("p (b w) -> p b w", w=2 * w)
                        early, late = (-1.0, 1.0) if d == 0 else (1.0, -1.0)
                        af(fv[:, :, 0:w], dv[:, :, 0:w], ACT.Exp, scale=early)
                        af(fv[:, :, w:2 * w], dv[:, :, w:2 * w], ACT.Exp, scale=late).then_inc(fac_ready.sem, 1)
                    else:
                        af(fac[:, :, :], diff[:, :, :], ACT.Exp)
                        af(fac2[:, :, :], diff[:, :, :], ACT.Exp, scale=-1.0).then_inc(fac_ready.sem, 1)

                for odd in range(2):
                    bk = banks.read(act_e, "ho", odd)
                    src = bk[:, 0:6 * HK].rearrange("p (i a d) -> p i a d", i=NTILE, a=2)
                    of_heads = lambda ap: ap.rearrange("p i (a b d) -> p i a b d", a=2, b=2)[:, :, :, odd, :]
                    af(of_heads(ho[:, :, :]), src, ACT.Copy)
                    banks.emptied(af(of_heads(ho_sq), src, ACT.Square), "ho", odd)

                for u in range(NU + 3):
                    if u < NU:
                        nk = P if UNITS[u][0] == 0 else KEYS - P
                        act_e.wait_ge(ntop_ready.sem, ntop_ready.at(l, u + 1))
                        for m in range(2):
                            bk = banks.read(act_e, "sc", 2 * u + m)
                            ins = af(prob[:, u % 2, m, 0:nk], bk[:, 0:nk], ACT.Exp, bias=ntop[:, u % 2, m:m + 1],
                                     scale=SCALE, accum_out=den[:, u % 2, m:m + 1])
                            banks.emptied(ins, "sc", 2 * u + m)
                    if 2 <= u < NU + 2:
                        v = u - 2
                        nk = P if UNITS[v][0] == 0 else 3 * P
                        bk = banks.read(act_e, "wT", v)
                        banks.emptied(af(wT[:, v % 2, 0:nk], bk[:, 0:nk], ACT.Copy), "wT", v)
                    if u >= 3 and UNITS[u - 3][1] == DH - 1:
                        t = UNITS[u - 3][0]
                        bk = banks.read(act_e, "o", t)
                        af(att[:, t, :], bk[:, :], ACT.Copy)
                        banks.emptied(af(att_sq[:, t, :], bk[:, :], ACT.Square), "o", t)
                act_e.wait_ge(sums_ready.sem, sums_ready.at(l, 1))
                af(att_r[:, 1, :], att_r[:, 0, :], ACT.Sqrt, bias=eps_t[:, :], scale=1.0 / VD)
                af(ho_r[:, 1, :], ho_r[:, 0, :], ACT.Sqrt, bias=eps_t[:, :], scale=1.0 / HK).then_inc(roots_ready.sem, 1)
                rows_of_modulation(4)
                for t in range(NTILE):
                    bk = banks.read(act_e, "oT", t)
                    banks.emptied(af(mixT[:, 2:6, t * P:(t + 1) * P], bk[:, :].rearrange("p (a t) -> p a t", a=DH), ACT.Copy), "oT", t)
                for c in range(2):
                    bk = banks.read(act_e, "hgT", c)
                    banks.emptied(af(mixT[:, 6 + c, :], bk[:, 0:TOK], ACT.Copy), "hgT", c)

                banks.read(act_e, "hgT", 1)
                act_e.wait_ge(results_out, l * 48 + 48)
                act_e.wait_ge(shared_in, l * 48 + 48)
                af(gu_hi[:, 0, :], w_shared[:, 0:2 * D], ACT.Copy).then_inc(gu_hi_ready.sem, 1)
                af(dn_hi[:, 0, :], w_shared[:, 2 * D:3 * D], ACT.Copy).then_inc(dn_hi_ready.sem, 1)

                squares_of_x(x_ready.at(l, 1), 2)
                root_of_mean("ms2")
                act_e.wait_ge(h_ready.sem, h_ready.at(l, 2))
                af(h_hi[:, :, :], h[:, :, :], ACT.Copy).then_inc(h_hi_ready.sem, 1)
                rows_of_modulation(5)
                bk = banks.read(act_e, "router")
                banks.emptied(af(score[:, :, :].rearrange("p i e -> p (i e)"), bk[:, 0:NTILE * E], ACT.Sigmoid), "router")

                def act_step(n, buf, e_mod, turn, has_gu, has_dn):
                    if not (isinstance(n, int) and n < 2):
                        act_e.wait_ge(act_ready.sem, l * VIS + n - 1)
                    bk = banks.read(act_e, "G", 0, n)
                    banks.emptied(af(sil[:, buf, :], bk[:, 0:TOK], ACT.Silu), "G")
                    act_e.wait_ge(act_ready.sem, l * VIS + n + 1)
                    af(act_hi[:, buf, :], act[:, buf, :], ACT.Copy).then_inc(act_hi_ready.sem, 1)
                    if has_gu:
                        banks.read(act_e, "U", 0, n)
                        split_gu(n + 2, buf, (e_mod + 1) % NSLOT, turn + (e_mod + 1) // NSLOT)
                    if has_dn:
                        if not (isinstance(n, int) and n == 0):
                            act_e.wait_ge(applied.sem, l * (VIS - 1) + n)
                        split_dn(1 - buf, ring[:, e_mod % NSLOT, 2 * D:3 * D])

                def split_gu(n, buf, slot, turn):
                    act_e.wait_ge(slot_full[slot], l * slot_layer[slot] + turn * 48 + (fix_sum[slot] + 48))
                    af(gu_hi[:, buf, :], ring[:, slot, 0:2 * D], ACT.Copy).then_inc(gu_hi_ready.sem, 1)

                def split_dn(buf, src):
                    af(dn_hi[:, buf, :], src, ACT.Copy).then_inc(dn_hi_ready.sem, 1)

                split_gu(1, 1, 0, 0)
                act_step(0, 0, 0, 0, True, True)
                with act_e.Fori(0, (E - 8) // 8) as turn:
                    for k in range(8):
                        act_step(turn * 8 + (k + 1), (k + 1) % 2, k + 1, turn * 4, True, True)
                for e in range(E - 8, E):
                    act_step(e + 1, (e + 1) % 2, e + 1 - (E - 8), (E - 8) // 2, e + 2 < E, e + 1 < E)
                for t in range(NTILE):
                    bk = banks.read(act_e, "y", 2 * t)
                    banks.emptied(af(rows[:, t, 0:512], bk[:, :], ACT.Copy), "y", 2 * t)

            banks.enter("final")
            squares_of_x(x_ready.at(DEPTH, 0), 0)
            root_of_mean("ms")

        @block.vector
        def _(dve):
            tt, ts, stt = nc.vector.tensor_tensor, nc.vector.tensor_scalar, nc.vector.scalar_tensor_tensor
            copy, red = nc.vector.tensor_copy, nc.vector.tensor_reduce
            order = InOrder(dve, dve_order, 5, LAYER_DVE, DEPTH)
            after = order.after
            order.enter("start")
            banks.enter("start")
            nc.vector.memset(eps_t[:, :], EPS)
            nc.vector.memset(ones[:, :], 1.0).then_inc(ones_ready, 1)
            dve.sem_inc(slots_idle.sem, 1)
            dve.wait_ge(consts_in, 16 * NCONST)
            copy(masks[:, :, :], masks_f)
            after(tt(kk[:, 0, :], lb_all[:, 0, :], lb_all[:, 1, :], ALU.max))
            tt(kk[:, 1:3, :], lb_all[:, :, :], kk[:, 0, :].unsqueeze(1).broadcast_to([P, 2, 2 * HW]), ALU.subtract).then_inc(lb_diff, 1)
            for t in range(NTILE):
                for half in range(2):
                    bk = banks.read(dve, "xT", 2 * t + half)
                    banks.emptied(copy(x[:, 4 * half:4 * half + 4, t * P:(t + 1) * P],
                                       bk[:, :].rearrange("p (j t) -> p j t", j=4)), "xT", 2 * t + half)
            dve.wait_ge(lb_exp, 1)
            after(tt(kk[:, 0, :], kk[:, 1, :], kk[:, 2, :], ALU.add))
            after(nc.vector.reciprocal(kk[:, 0, :], kk[:, 0, :]))
            after(nc.vector.memset(lb_all[:, 0, :], 0.0))
            after(tt(lb_all[:, 1, :], kk[:, 2, :], kk[:, 0, :], ALU.mult))
            nc.vector.memset(tick[:, :], 0.0).then_inc(x_ready.sem, 1)
            order.leave()

            def modulation(m):
                bk = banks.read(dve, f"modT{m}")
                banks.emptied(tt(mod[:, m, :, :], bk[:, 0:2 * NJ].rearrange("p (j s) -> p j s", s=2),
                                 b_ada[:, m, :].unsqueeze(2).broadcast_to([P, NJ, 2]), ALU.add), f"modT{m}")

            def scaled_to_one(stage):
                banks.wait_emptied(dve, stage)
                after(nc.vector.reciprocal(rstd[:, :], rms[:, :]))
                after(tt(h[:, :, :], x[:, :, :], rstd[:, :].unsqueeze(1).broadcast_to([P, NJ, TOK]), ALU.mult))

            def modulated(m):
                for j in range(NJ):
                    for s in range(2):
                        last = ts(h[:, j, SPAN[s]], h[:, j, SPAN[s]], gain[:, j, s:s + 1], mod[:, m, j, s:s + 1], ALU.mult, ALU.add)
                last.then_inc(h_ready.sem, 1)

            def gain_of(m, gi):
                return stt(gain[:, :, :], mod[:, m, :, :], 1.0, norm_g[:, gi, :].unsqueeze(2).broadcast_to([P, NJ, 2]), ALU.add, ALU.mult)

            def low_part(lo, full, hi):
                return tt(lo, full, hi.bitcast(F32), ALU.subtract)

            def gated_residual(stage, m):
                for j in range(NJ):
                    bk = banks.read(dve, stage, j)
                    for s in range(2):
                        last = stt(x[:, j, SPAN[s]], bk[:, SPAN[s]], mod[:, m, j, s:s + 1], x[:, j, SPAN[s]], ALU.mult, ALU.add)
                    banks.emptied(last, stage, j)

            with dve.Fori(0, DEPTH) as l:
                order.enter("layer", l)
                banks.enter("layer", l)
                after(copy(lb[:, :], lb_all[:, l, :]))
                after(ts(om[:, :], lb[:, :], -1.0, 1.0, ALU.mult, ALU.add))
                dve.wait_ge(params_in, l * (16 * NPARAM) + 16 * NPARAM)
                after(tt(lam_p[:, :, :], lambdas[:, 0:4:2, :], lambdas[:, 1:4:2, :], ALU.mult))
                red(lam_s[:, :], lam_p[:, :, :], AX.X, ALU.add).then_inc(lam_sum.sem, 1)
                after(ts(attn_g[:, :], attn_g[:, :], lam_init[:, 1:2], None, ALU.mult))
                scaled_to_one("ms1")
                modulation(0)
                modulation(1)
                banks.wait_emptied(dve, "modT1")
                after(gain_of(1, 0))
                modulated(0)
                modulation(2)

                for t in range(NTILE):
                    bk = banks.read(dve, "v", t)
                    banks.emptied(copy(val[:, t, :], bk[:, :]), "v", t)

                for i in range(2):
                    banks.wait_emptied(dve, "hq", i)
                after(ts(hqT[:, :, :], hqT[:, :, :], HK ** -0.5, None, ALU.mult))
                for t in range(NTILE):
                    banks.wait_emptied(dve, "hif", t)
                    banks.wait_emptied(dve, "hbg", t)
                over_tiles = lambda ap: ap.unsqueeze(1).broadcast_to([P, NTILE, 2 * HW])
                after(tt(logf[:, :, :], logf[:, :, :], over_tiles(om[:, :]), ALU.mult))
                after(tt(logf[:, :, :], logf[:, :, :], over_tiles(lb[:, :]), ALU.add))
                ts(logf[:, :, :], logf[:, :, :], LOG_DECAY_FLOOR, None, ALU.max).then_inc(fgate_ready.sem, 1)
                tt(kk[:, :, :], kk[:, :, :], over_tiles(om[:, :]), ALU.mult).then_inc(kk_ready.sem, 1)

                bk = banks.read(dve, "k_rows")
                banks.emptied(copy(k_rows[:, :], bk[:, :]), "k_rows")
                bk = banks.read(dve, "ckT")
                banks.emptied(copy(kT[:, :, TOK:KEYS], bk[:, :].rearrange("p (a t) -> p a t", a=DH)), "ckT")
                over_heads = lambda ap: ap.unsqueeze(1).broadcast_to([P, 2, TOK - P])
                for stage, dst in (("rotq", qT), ("rotk", kT)):
                    for i in range(2):
                        heads = dst[:, 2 * i:2 * i + 2, P:TOK]
                        bk = banks.read(dve, stage, i)
                        banks.emptied(tt(rot_t[:, :, :], bk[:, :].rearrange("p (a t) -> p a t", a=2), over_heads(const("sin")), ALU.mult), stage, i)
                        after(tt(heads, heads, over_heads(const("cos")), ALU.mult))
                        banks.wait_emptied(dve, stage, i)
                        last = tt(heads, heads, rot_t[:, :, :], ALU.add)
                        if stage == "rotk" and i == 1:
                            last.then_inc(rope_done.sem, 1)
                        else:
                            after(last)

                for i, tiles in enumerate(((0, 0), (1, 2))):
                    banks.wait_emptied(dve, "past", i)
                    for d, t in enumerate(tiles):
                        last = tt(kdec[:, 2 * i + d, :], kdec[:, 2 * i + d, :], kk[:, t, d * HW:(d + 1) * HW], ALU.mult)
                last.then_inc(kdec_ready.sem, 1)
                modulation(3)
                dve.wait_ge(ecum_ready.sem, ecum_ready.at(l, 1))
                copy(edge[:, 0:2], qdec[:, 0:2, 2 * P - 1])
                after(copy(edge[:, 2:4], qdec[:, 2:4, 2 * P]))
                qd = qdec[:, :, :].rearrange("p (d c) t -> p d (c t)", d=2)
                tt(qd, qd, hqT[:, :, :].rearrange("p c t -> p (c t)").unsqueeze(1).broadcast_to([P, 2, 2 * TOK]), ALU.mult)\
                    .then_inc(qdec_ready.sem, 1)

                def flat(ap):
                    return ap.rearrange("p c t -> p (c t)")

                def masked(n):
                    d, lv = divmod(n, LEVELS)
                    if n > 0:
                        banks.wait_emptied(dve, "lev", 2 * NTILE * n - 1)
                    for t in range(NTILE):
                        for odd in range(2):
                            use = (n * NTILE + t) * 2 + odd
                            bk = banks.read(dve, "lev", use)
                            apart(dve)
                            ins = nc.vector.copy_predicated(aT[:, d, t, :].rearrange("p (a b t) -> p a b t", a=2, b=2)[:, :, odd, :],
                                                            masks[:, n, :].unsqueeze(1).broadcast_to([P, 2, P]),
                                                            bk[:, 0:2 * P].rearrange("p (a t) -> p a t", a=2))
                            banks.emptied(ins, "lev", use)

                def less_middle(n):
                    d, lv = divmod(n, LEVELS)
                    w = HALVES[lv] if lv < LEVELS - 1 else BASE // 2
                    blocks = lambda ap: flat(ap).rearrange("p (b w) -> p b w", w=2 * w)
                    cd = blocks(cum[:, 2 * d:2 * d + 2, :])
                    nb = 2 * TOK // (2 * w)
                    at = w - 1 if d == 0 else w
                    tt(blocks(diff[:, :, :]), cd, cd[:, :, at:at + 1].broadcast_to([P, nb, 2 * w]), ALU.subtract)\
                        .then_inc(diff_ready.sem, 1)

                less_middle(0)
                for n in range(NLEV):
                    d, lv = divmod(n, LEVELS)
                    dve.wait_ge(fac_ready.sem, fac_ready.at(l, n + 1))
                    keys, out = kkT[:, 2 * d:2 * d + 2, :], pair[:, n % 2, :, :]
                    if lv < LEVELS - 1:
                        w = HALVES[lv]
                        blocks = lambda ap, w=w: flat(ap).rearrange("p (b w) -> p b w", w=2 * w)
                        first, second = (keys, hqT[:, :, :]) if d == 0 else (hqT[:, :, :], keys)
                        tt(blocks(out)[:, :, 0:w], blocks(first)[:, :, 0:w], blocks(fac[:, :, :])[:, :, 0:w], ALU.mult)
                        last = tt(blocks(out)[:, :, w:2 * w], blocks(second)[:, :, w:2 * w], blocks(fac[:, :, :])[:, :, w:2 * w], ALU.mult)
                    else:
                        tt(flat(pair2[:, :, :]), flat(hqT[:, :, :]), flat(fac[:, :, :]), ALU.mult)
                        last = tt(flat(out), flat(keys), flat(fac2[:, :, :]), ALU.mult)
                    last.then_inc(pair_ready.sem, 1)
                    if n + 1 < NLEV:
                        less_middle(n + 1)
                    if n == 0:
                        dve.wait_ge(aT_zero.sem, aT_zero.at(l, 1))
                    else:
                        masked(n - 1)
                masked(NLEV - 1)

                bk = banks.read(dve, "st", 0)
                sv = bk[:, :].rearrange("p (g n) -> p g n", g=4)
                copy(st_out[0:HK, :, :], sv[0:HK, :, 0:HK])
                banks.emptied(copy(st_out[HK:P, :, :], sv[HK:P, :, HK:P]), "st", 0)
                after(tt(st_mid[:, :, :], state0[:, :, :], edge[:, :].unsqueeze(2).broadcast_to([P, 4, HK]), ALU.mult))
                bk = banks.read(dve, "st", 1)
                sv = bk[:, :].rearrange("p (g n) -> p g n", g=4)
                tt(st_mid[0:HK, :, :], st_mid[0:HK, :, :], sv[0:HK, :, 0:HK], ALU.add)
                banks.emptied(tt(st_mid[HK:P, :, :], st_mid[HK:P, :, :], sv[HK:P, :, HK:P], ALU.add), "st", 1)

                dve.wait_ge(lam_exp.sem, lam_exp.at(l, 1))
                after(stt(neg_lam[:, :], lam_s[:, 1:2], lam_s[:, 0:1], lam_init[:, 0:1], ALU.subtract, ALU.subtract))

                for u in range(NU + 1):
                    if u < NU:
                        nk = P if UNITS[u][0] == 0 else KEYS - P
                        for m in range(2):
                            bk = banks.read(dve, "sc", 2 * u + m)
                            last = red(top[:, u % 2, m:m + 1], bk[:, 0:nk], AX.X, ALU.max)
                        after(last)
                        ts(ntop[:, u % 2, :], top[:, u % 2, :], -SCALE, None, ALU.mult).then_inc(ntop_ready.sem, 1)
                    if u >= 1:
                        v = u - 1
                        nk = P if UNITS[v][0] == 0 else KEYS - P
                        for m in range(2):
                            banks.wait_emptied(dve, "sc", 2 * v + m)
                        after(nc.vector.reciprocal(rden[:, v % 2, :], den[:, v % 2, :]))
                        after(tt(rden[:, v % 2, 1:2], rden[:, v % 2, 1:2], neg_lam[:, :], ALU.mult))
                        if v >= 2:
                            banks.read(dve, "wT", v - 2)
                        after(ts(wts[:, v % 2, 0:nk], prob[:, v % 2, 0, 0:nk], rden[:, v % 2, 0:1], None, ALU.mult))
                        stt(wts[:, v % 2, 0:nk], prob[:, v % 2, 1, 0:nk], rden[:, v % 2, 1:2], wts[:, v % 2, 0:nk], ALU.mult, ALU.add)\
                            .then_inc(wts_ready.sem, 1)

                for t in range(NTILE):
                    banks.wait_emptied(dve, "o", t)
                for odd in range(2):
                    banks.wait_emptied(dve, "ho", odd)
                heads_a = lambda ap: ap.rearrange("p i (a d) -> p (i a) d", a=DH)
                heads_h = lambda ap: ap.rearrange("p i (a d) -> p (i a) d", a=HH)
                red(att_r[:, 0, :], heads_a(att_sq), AX.X, ALU.add)
                red(ho_r[:, 0, :], heads_h(ho_sq[:, :, :]), AX.X, ALU.add).then_inc(sums_ready.sem, 1)
                dve.wait_ge(roots_ready.sem, roots_ready.at(l, 1))
                nc.vector.reciprocal(att_r[:, 0, :], att_r[:, 1, :])
                after(nc.vector.reciprocal(ho_r[:, 0, :], ho_r[:, 1, :]))
                after(tt(heads_a(att[:, :, :]), heads_a(att[:, :, :]), att_r[:, 0, :].unsqueeze(2).broadcast_to([P, NTILE * DH, VD]), ALU.mult))
                tt(heads_a(att[:, :, :]), heads_a(att[:, :, :]), attn_g[:, :].unsqueeze(1).broadcast_to([P, NTILE * DH, VD]), ALU.mult)\
                    .then_inc(anorm_ready.sem, 1)
                after(tt(heads_h(ho[:, :, :]), heads_h(ho[:, :, :]), ho_r[:, 0, :].unsqueeze(2).broadcast_to([P, NTILE * HH, HK]), ALU.mult))
                after(tt(heads_h(ho[:, :, :]), heads_h(ho[:, :, :]), hg_g[:, :].unsqueeze(1).broadcast_to([P, NTILE * HH, HK]), ALU.mult))
                tt(gate_o[:, :, :], gate_o[:, :, :], ho[:, :, :], ALU.mult).then_inc(hnorm_ready.sem, 1)

                dve.wait_ge(gu_hi_ready.sem, gu_hi_ready.at(l, 1))
                low_part(gu_lo[:, 0, :], w_shared[:, 0:2 * D], gu_hi[:, 0, :]).then_inc(gu_lo_ready.sem, 1)
                dve.wait_ge(dn_hi_ready.sem, dn_hi_ready.at(l, 1))
                low_part(dn_lo[:, 0, :], w_shared[:, 2 * D:3 * D], dn_hi[:, 0, :]).then_inc(dn_lo_ready.sem, 1)

                modulation(4)
                banks.wait_emptied(dve, "modT4")
                gated_residual("out", 2)
                gain_of(4, 1).then_inc(x_ready.sem, 1)
                dve.wait_ge(x_ready.sem, x_ready.at(l, 1))
                scaled_to_one("ms2")
                modulated(3)

                banks.read(dve, "router")
                dve.wait_ge(h_hi_ready.sem, h_hi_ready.at(l, 1))
                low_part(h_lo[:, :, :], h[:, :, :], h_hi[:, :, :]).then_inc(h_lo_ready.sem, 1)

                banks.wait_emptied(dve, "router")
                after(tt(biased[:, :, :], score[:, :, :], r_bias[:, :].unsqueeze(1).broadcast_to([P, NTILE, E]), ALU.add))
                apart(dve)
                for t in range(NTILE):
                    for g in range(NG):
                        last = nc.vector.max(tops[:, t * NG + g, :], biased[:, t, g * PG:(g + 1) * PG])
                after(last)
                gs = gsum[:, :, :]
                after(tt(gs.rearrange("p i g -> p (i g)"), tops[:, :, 0], tops[:, :, 1], ALU.add))
                other = gs.unsqueeze(2).broadcast_to([P, NTILE, NG, NG])
                own = gs.unsqueeze(3).broadcast_to([P, NTILE, NG, NG])
                sq4 = lambda ap: ap.rearrange("p i (a b) -> p i a b", a=NG)
                tt(sq4(cmp_a[:, :, :]), other, own, ALU.is_gt)
                after(tt(sq4(cmp_b[:, :, :]), other, own, ALU.is_equal))
                after(tt(cmp_b[:, :, :], cmp_b[:, :, :], const("tie").unsqueeze(1).broadcast_to([P, NTILE, NG * NG]), ALU.mult))
                after(tt(cmp_a[:, :, :], cmp_a[:, :, :], cmp_b[:, :, :], ALU.add))
                after(red(rank[:, :], cmp_a[:, :, :].rearrange("p i (a b) -> p (i a) b", a=NG), AX.X, ALU.add))
                after(ts(rank[:, :], rank[:, :], float(TOPK_GROUPS), None, ALU.is_lt))
                after(ts(gpen[:, :], rank[:, :], NEVER, -NEVER, ALU.mult, ALU.add))
                grouped = biased[:, :, :].rearrange("p i (g k) -> p (i g) k", g=NG)
                wide = lambda ap: ap.unsqueeze(2).broadcast_to([P, NTILE * NG, PG])
                after(tt(grouped, grouped, wide(rank[:, :]), ALU.mult))
                after(tt(grouped, grouped, wide(gpen[:, :]), ALU.add))
                apart(dve)
                for t in range(NTILE):
                    last = nc.vector.max(best[:, t, :], biased[:, t, :])
                after(last)
                apart(dve)
                for t in range(NTILE):
                    last = nc.vector.match_replace(gsel[:, t, :], best[:, t, :], biased[:, t, :], TAKEN)
                after(last)
                after(ts(gsel[:, :, :], gsel[:, :, :], NEVER * 1.05, None, ALU.is_gt))
                after(tt(gsel[:, :, :], gsel[:, :, :], score[:, :, :], ALU.mult))
                after(red(wsum[:, :], gsel[:, :, :], AX.X, ALU.add))
                after(nc.vector.reciprocal(wsum[:, :], wsum[:, :]))
                after(ts(wsum[:, :], wsum[:, :], ROUTED_SCALE, None, ALU.mult))
                tt(gsel[:, :, :], gsel[:, :, :], wsum[:, :].unsqueeze(2).broadcast_to([P, NTILE, E]), ALU.mult).then_inc(gsel_ready.sem, 1)

                dve.wait_ge(gu_hi_ready.sem, gu_hi_ready.at(l, 2))
                low_part(gu_lo[:, 1, :], ring[:, 0, 0:2 * D], gu_hi[:, 1, :]).then_inc(gu_lo_ready.sem, 1)

                def dve_step(n, buf, gates, e_mod, has_gu, has_dn):
                    banks.wait_emptied(dve, "G", 0, n)
                    bk = banks.read(dve, "U", 0, n)
                    banks.emptied(tt(sil[:, buf, :], sil[:, buf, :], bk[:, 0:TOK], ALU.mult), "U")
                    banks.wait_emptied(dve, "U", 0, n)
                    if gates is None:
                        copy(act[:, buf, :], sil[:, buf, :]).then_inc(act_ready.sem, 1)
                    else:
                        tt(act[:, buf, :], sil[:, buf, :], gates, ALU.mult).then_inc(act_ready.sem, 1)
                    dve.wait_ge(act_hi_ready.sem, l * VIS + n + 1)
                    low_part(act_lo[:, buf, :], act[:, buf, :], act_hi[:, buf, :]).then_inc(act_lo_ready.sem, 1)
                    if has_gu:
                        slot = (e_mod + 1) % NSLOT
                        dve.wait_ge(gu_hi_ready.sem, l * VIS + n + 3)
                        low_part(gu_lo[:, buf, :], ring[:, slot, 0:2 * D], gu_hi[:, buf, :]).then_inc(gu_lo_ready.sem, 1)
                    if has_dn:
                        slot = e_mod % NSLOT
                        dve.wait_ge(dn_hi_ready.sem, l * VIS + n + 2)
                        low_part(dn_lo[:, 1 - buf, :], ring[:, slot, 2 * D:3 * D], dn_hi[:, 1 - buf, :]).then_inc(dn_lo_ready.sem, 1)

                modulation(5)
                dve_step(0, 0, None, 0, True, True)
                bk = banks.read(dve, "gT")
                banks.emptied(copy(gatesT[:, :], bk[0:E, 0:TOK]), "gT")

                def eight(turn, last):
                    for i in range(2):
                        dve.wait_ge(gate_in[i], l * (16 * E // (2 * GSLOT)) + turn * 16 + 16)
                        for s in range(GSLOT):
                            k = i * GSLOT + s
                            dve_step(turn * 8 + (k + 1), (k + 1) % 2, gate_b[:, i, s, :], k + 1, not last or k < 6, not last or k < 7)

                with dve.Fori(0, E // 8 - 1) as turn:
                    eight(turn, False)
                eight(E // 8 - 1, True)
                dve.wait_ge(dn_lo_ready.sem, l * VIS + VIS)
                dve.sem_inc(slots_idle.sem, 1)
                for t in range(NTILE):
                    bk = banks.read(dve, "y", 2 * t + 1)
                    banks.emptied(copy(rows[:, t, 512:1024], bk[:, :]), "y", 2 * t + 1)
                gated_residual("yT", 5)
                nc.vector.memset(tick[:, :], 0.0).then_inc(x_ready.sem, 1)
                order.leave()

            order.enter("final")
            banks.enter("final")
            banks.wait_emptied(dve, "ms")
            after(nc.vector.reciprocal(rstd[:, :], rms[:, :]))
            dve.wait_ge(x_ready.sem, x_ready.at(DEPTH, 0))
            after(tt(h[:, :, :], x[:, :, :], rstd[:, :].unsqueeze(1).broadcast_to([P, NJ, TOK]), ALU.mult))
            for j in range(NJ):
                last = ts(h[:, j, :], h[:, j, :], final_g[:, j:j + 1], None, ALU.mult)
            last.then_inc(final_ready, 1)
            for t in range(NTILE):
                for half in range(2):
                    bk = banks.read(dve, "rows", 2 * t + half)
                    banks.emptied(copy(rows[:, t, :].rearrange("p (q j) -> p j q", j=NJ)[:, 4 * half:4 * half + 4, :],
                                       bk[:, :].rearrange("p (j q) -> p j q", j=4)), "rows", 2 * t + half)


_INS = ["x_prompt", "x_sample", "cache_k", "cache_v", "state_hgrn", "c", "c_ctx", "w_ada", "b_ada", "norm_g", "w_in",
        "w_fourier", "lambdas", "attn_norm_g", "lower_bounds", "hg_norm_g", "w_out", "w_router", "router_bias",
        "w_gate", "w_up", "w_down", "ws_gate", "ws_up", "ws_down", "final_g"]


def shape_constants(depth):
    import numpy as np

    i = np.arange(P)
    out = {"ident": np.eye(P), "tri_f": i[:, None] <= i[None, :], "tri_b": i[:, None] >= i[None, :],
           "past_f": i[:, None] > i[None, :], "past_b": i[:, None] < i[None, :]}
    rot = np.zeros((P, P))
    for a in range(0, P, 32):
        for k in range(16):
            rot[a + 16 + k, a + k] = -1.0
            rot[a + k, a + 16 + k] = 1.0
    out["rot"] = rot
    for name, n in (("ctx", 128), ("lat", 256)):
        k = np.arange(n)
        ang = 2 * np.pi * ((k[:, None] * k[None, :]) % n) / n
        for c, m in (("c", np.cos(ang)), ("s", np.sin(ang))):
            out[f"{c}_{name}"] = (m / np.sqrt(n * 64.0)).reshape(n // P, P, n).transpose(1, 0, 2).reshape(P, -1)
    k = np.arange(64)
    ang = 2 * np.pi * ((k[:, None] * k[None, :]) % 64) / 64
    out["c_chan"] = np.kron(np.eye(2), np.cos(ang))
    out["s_chan"] = -np.kron(np.eye(2), np.sin(ang))
    t = np.arange(256)
    inv = (10000.0 ** (-np.arange(0, 32, 2) / 32.0)).astype(np.float32)
    row, col = (t // 64)[None, :] * inv[:, None], (t % 64)[None, :] * inv[:, None]
    ang = np.concatenate([row, row, col, col] * 2, 0)
    out["cos"], out["sin"] = np.cos(ang), np.sin(ang)
    g = np.arange(8)
    out["tie"] = np.broadcast_to((g[None, :] < g[:, None]).reshape(1, 64), (P, 64))
    packed = np.concatenate([np.asarray(out[name], np.float32) for name, _ in CONST_COLS], 1)

    masks = []
    for d in range(2):
        s, t = (i[:, None], i[None, :]) if d == 0 else (P - 1 - i[:, None], P - 1 - i[None, :])
        for w in HALVES:
            masks.append((s // (2 * w) == t // (2 * w)) & (s % (2 * w) < w) & (t % (2 * w) >= w))
        masks.append((s // BASE == t // BASE) & (s <= t))
    init = np.array([0.8 - 0.6 * np.exp(-0.3 * n) for n in range(depth)])
    lam = np.stack([init, 1.0 - init], 1).astype(np.float32)
    return packed, np.stack(masks).astype(np.float32), lam


def kernel(**inputs):
    import numpy as np
    import concourse.bacc as bacc
    from concourse.bass_utils import run_bass_kernel_spmd

    nc = bacc.Bacc("TRN2", target_bir_lowering=False, num_devices=1, dynamic_dma_scratch_size=4096)
    arrays = {name: np.ascontiguousarray(inputs[name]) for name in _INS}
    depth, past, heads, kd = arrays["cache_k"].shape[1:]
    arrays["const_f"], arrays["const_m"], arrays["lam_init"] = shape_constants(depth)
    T = {name: nc.dram_tensor("in_" + name, a.shape, mybir.dt.from_np(a.dtype), kind="ExternalInput").ap()
         for name, a in arrays.items()}
    seq = arrays["x_prompt"].shape[1]
    shapes = {"y_prompt": arrays["x_prompt"].shape, "y_sample": arrays["x_sample"].shape,
              "new_k": (1, depth, seq, heads, kd), "new_v": (1, depth, seq, heads, arrays["cache_v"].shape[4]),
              "new_state": arrays["state_hgrn"].shape}
    outs = {name: nc.dram_tensor("out_" + name, shape, F32, kind="ExternalOutput").ap() for name, shape in shapes.items()}
    trunk_program(nc, T, T["const_f"], T["const_m"], *outs.values())
    r = run_bass_kernel_spmd(nc, [{"in_" + name: a for name, a in arrays.items()}], core_ids=[0])
    return tuple(r.results[0]["out_" + name] for name in shapes)
```

```python
from contextlib import ExitStack

import concourse.bass as bass
from concourse import mybir

F32 = mybir.dt.float32
F32R = mybir.dt.float32r
U8 = mybir.dt.uint8
ALU = mybir.AluOpType
ACT = mybir.ActivationFunctionType
AX = mybir.AxisListType

P = 128
EPS = 1e-6
ROUTED_SCALE = 2.5
TOPK_GROUPS = 4
LOG_DECAY_FLOOR = 2.0611536e-09
NEVER = 3.0e38
TAKEN = 3.3e38
HALVES = (64, 32, 16, 8)
BASE = 8
LAYER_DVE = 93
NSLOT = 2
GSLOT = 4

CONST_COLS = (("ident", 128), ("tri_f", 128), ("tri_b", 128), ("past_f", 128), ("past_b", 128), ("rot", 128),
              ("c_ctx", 128), ("s_ctx", 128), ("c_chan", 128), ("s_chan", 128), ("cos", 256), ("sin", 256),
              ("c_lat", 512), ("s_lat", 512), ("tie", 64))


def const_offsets():
    out, at = {}, 0
    for name, width in CONST_COLS:
        out[name] = (at, at + width)
        at += width
    return out, at


class Signal:

    def __init__(self, sem, start=0, layer=1):
        self.sem, self.start, self.layer = sem, start, layer

    def at(self, l, n):
        return self.start + l * self.layer + n


class InOrder:

    def __init__(self, eng, sem, start, layer, depth):
        self.eng, self.sem, self.start, self.layer, self.depth = eng, sem, start, layer, depth
        self.base, self.n, self.seen = 0, 0, {}

    def enter(self, phase, l=0):
        self.seen[phase] = 0
        self.phase = phase
        self.base = {"start": 0, "layer": self.start + l * self.layer, "final": self.start + self.depth * self.layer}[phase]
        self.n = 0

    def leave(self):
        want = {"start": self.start, "layer": self.layer}.get(self.phase, self.n)
        assert self.n == want, (self.phase, self.n, want)

    def after(self, ins):
        self.n += 1
        ins.then_inc(self.sem, 1)
        self.eng.wait_ge(self.sem, self.base + self.n)


class Banks:

    def __init__(self, banks, full, empty, depth):
        self.banks, self.full_sem, self.empty_sem, self.depth = banks, full, empty, depth
        self.count = {"start": [0] * 8, "layer": [0] * 8, "final": [0] * 8}
        self.uses = {"start": {}, "layer": {}, "final": {}}
        self.turn = 0

    def plan(self, phase, stage, n, bank=None, each=1):
        for i in range(n):
            b = bank[i] if bank is not None else self.turn % 8
            if bank is None:
                self.turn += 1
            self.uses[phase][stage, i] = (b, self.count[phase][b])
            self.count[phase][b] += each

    def plan_one(self, phase, stage, i, bank):
        self.uses[phase][stage, i] = (bank, self.count[phase][bank])
        self.count[phase][bank] += 1

    def enter(self, phase, l=0):
        self.phase, self.l = phase, l

    def _at(self, stage, i, more):
        b, nth = self.uses[self.phase][stage, i]
        if self.phase != "start":
            nth = nth + self.count["start"][b]
        if self.phase == "layer":
            nth = self.l * self.count["layer"][b] + nth
        if self.phase == "final":
            nth = nth + self.depth * self.count["layer"][b]
        return b, nth + more

    def claim(self, pe, stage, i=0, more=0):
        b, v = self._at(stage, i, more)
        pe.wait_ge(self.empty_sem[b], v + 1)
        return self.banks[b]

    def filled(self, ins, stage, i=0):
        ins.then_inc(self.full_sem[self.uses[self.phase][stage, i][0]], 1)

    def read(self, eng, stage, i=0, more=0):
        b, v = self._at(stage, i, more + 1)
        eng.wait_ge(self.full_sem[b], v)
        return self.banks[b]

    def emptied(self, ins, stage, i=0):
        ins.then_inc(self.empty_sem[self.uses[self.phase][stage, i][0]], 1)

    def wait_emptied(self, eng, stage, i=0, more=0):
        b, v = self._at(stage, i, more + 1)
        eng.wait_ge(self.empty_sem[b], v + 1)


def trunk_program(nc, T, CF, CM, y_prompt, y_sample, new_k, new_v, new_state):
    DEPTH, _, _, DH, VD = T["cache_k"].shape[1], 0, 0, T["cache_k"].shape[3], T["cache_k"].shape[4]
    D = T["x_prompt"].shape[2]
    NJ = D // P
    NTILE = (T["x_prompt"].shape[1] + T["x_sample"].shape[1]) // P
    TOK = NTILE * P
    SPAN = (slice(0, P), slice(P, TOK))
    DK = VD // 2
    HH, HK = T["state_hgrn"].shape[3], T["state_hgrn"].shape[4]
    HW = HH * HK
    DA = DH * VD
    FN = T["w_fourier"].shape[1]
    E = T["w_router"].shape[2]
    NG = 8
    PG = E // NG
    PROJ = T["w_in"].shape[2]
    KEYS = TOK + T["cache_k"].shape[2]
    SCALE = DK ** -0.5
    Q0, K0, V0, HQ0, HI0, HB0 = FN, FN + DA, FN + 2 * DA, FN + 3 * DA, FN + 3 * DA + HW, FN + 3 * DA + 3 * HW
    assert PROJ == HB0 + 2 * HW and NTILE == 3 and D == 1024 and E % NSLOT == 0

    ctx = ExitStack()
    with ctx:
        def sb(name, shape, dt=F32):
            return ctx.enter_context(nc.sbuf_tensor(name, shape, dt))

        def sem(name):
            return ctx.enter_context(nc.semaphore(name))

        ring = sb("ring", [P, NSLOT, 4096])
        x = sb("x", [P, NJ, TOK])
        h_at = nc.sbuf_base + -nc.sbuf_base % 32
        h = sb("h", [P, NJ, TOK])
        h_lo = nc.alloc_sbuf_tensor_at("h_lo", [P, NJ, TOK], F32R, offset=h_at)
        slab_at = nc.sbuf_base + -nc.sbuf_base % 32
        slab = sb("slab", [P, 12 * D])
        slab_used = [0]

        def mixer(*shape):
            n = 1
            for k in shape:
                n *= k
            a = slab_used[0]
            slab_used[0] += n
            assert slab_used[0] <= 12 * D
            v = slab[:, a:a + n]
            return v.rearrange("p (a b) -> p a b", a=shape[0]) if len(shape) == 2 else v

        def overlay(name, shape, at):
            return nc.alloc_sbuf_tensor_at(name, shape, F32R, offset=at)

        gu_hi = overlay("gu_hi", [P, 2, 2 * D], slab_at)
        gu_lo = overlay("gu_lo", [P, 2, 2 * D], slab_at + 16 * D)
        dn_hi = overlay("dn_hi", [P, 2, D], slab_at + 32 * D)
        dn_lo = overlay("dn_lo", [P, 2, D], slab_at + 40 * D)
        h_hi = sb("h_hi", [P, NJ, TOK], F32R)
        act_hi = sb("act_hi", [P, 2, TOK], F32R)
        squares = h[:, :, :]
        big_at = nc.sbuf_base + -nc.sbuf_base % 32
        big = sb("big", [P, NJ * TOK])
        h_lo_late = overlay("h_lo_late", [P, NJ, TOK], big_at)
        mixT = big[:, :].rearrange("p (j t) -> p j t", j=NJ)
        rows = big[:, :].rearrange("p (i d) -> p i d", i=NTILE)
        aT_at = nc.sbuf_base + -nc.sbuf_base % 32
        aT = sb("aT", [P, 2, NTILE, 4 * P])
        w_shared = aT[:, :, :, :].rearrange("p d i t -> p (d i t)")
        work_at = nc.sbuf_base + -nc.sbuf_base % 32
        work = sb("work", [P, 12 * TOK])
        act_lo = nc.alloc_sbuf_tensor_at("act_lo", [P, 2, TOK], F32R, offset=work_at + 40 * TOK)

        UNIT = 2048
        w_hi = [overlay("w_hi0", [P, UNIT], big_at), overlay("w_hi1", [P, UNIT], work_at)]
        w_lo = [overlay("w_lo0", [P, UNIT], aT_at), sb("w_lo1", [P, UNIT], F32R)]
        assert UNIT <= 6 * TOK

        def part(a, b, inner=TOK):
            return work[:, a * TOK:b * TOK].rearrange("p (c t) -> p c t", t=inner)

        hflat = h[:, :, :].rearrange("p j t -> p (j t)")
        rstd = sb("rstd", [P, TOK])
        rms = sb("rms", [P, TOK])
        consts = sb("consts", [P, CF.shape[1]])
        masks = sb("masks", [P, len(HALVES) + 2, P], U8)
        masks_f = hflat[:, 0:(len(HALVES) + 2) * P].rearrange("p (m t) -> p m t", t=P)
        ones = sb("ones", [P, P])
        eps_t = sb("eps_t", [P, 1])
        cond = sb("cond", [P, 2, NJ])
        scond = sb("scond", [P, NJ, 2])
        mod = sb("mod", [P, 6, NJ, 2])
        gain = sb("gain", [P, NJ, 2])
        mod_rows = sb("mod_rows", [4, 2, D])
        scond_r = sb("scond_r", [P, NJ, 4], F32R)
        b_ada = sb("b_ada", [P, 6, NJ])
        norm_g = sb("norm_g", [P, 2, NJ])
        attn_g = sb("attn_g", [P, VD])
        hg_g = sb("hg_g", [P, HK])
        lambdas = sb("lambdas", [P, 4, DK])
        lam_init = sb("lam_init", [P, 2])
        r_bias = sb("r_bias", [P, E])
        w_four = mixer(2, FN)
        w_router = sb("w_router", [P, NJ, E])
        cache_k = mixer(DA)
        cache_v = mixer(DA)
        state0 = sb("state0", [P, 4, HK])
        final_g = hflat[:, 0:D]
        mean_sq = sb("mean_sq", [P, NTILE, 2])
        token_r = sb("token_r", [P, 2, NTILE])
        lb_all = sb("lb_all", [P, DEPTH, 2 * HW])
        lb = sb("lb", [P, 2 * HW])
        om = sb("om", [P, 2 * HW])
        qT = mixer(DH, TOK)
        kT = mixer(DH, KEYS)
        val = mixer(NTILE, DA)
        k_rows = mixer(DA)
        rot_t = mixer(2, 256)
        lam_p = sb("lam_p", [P, 2, DK])
        lam_s = sb("lam_s", [P, 2])
        neg_lam = sb("neg_lam", [P, 1])
        top = sb("top", [P, 2, 2])
        ntop = sb("ntop", [P, 2, 2])
        den = sb("den", [P, 2, 2])
        rden = sb("rden", [P, 2, 2])
        prob = hflat[:, 0:4 * TOK].rearrange("p (a m t) -> p a m t", a=2, m=2)
        wts = hflat[:, 4 * TOK:6 * TOK].rearrange("p (a t) -> p a t", a=2)
        wT = hflat[:, 6 * TOK:8 * TOK].rearrange("p (a t) -> p a t", a=2)
        logf = mixer(NTILE, 2 * HW)
        att = logf
        att_r = sb("att_r", [P, 2, NTILE * DH])
        u_fn = mixer(NTILE, FN)
        ho = u_fn
        four1 = part(0, 4)
        att_sq = part(0, 4, DA)
        zT = part(4, 6)
        hqT = mixer(2, TOK)
        hv = mixer(NTILE, HW)
        gate_o = mixer(NTILE, HW)
        kk = part(6, 10, 2 * HW)
        kkT = hflat[:, 0:4 * TOK].rearrange("p (g t) -> p g t", g=4)
        cum = hflat[:, 4 * TOK:8 * TOK].rearrange("p (g t) -> p g t", g=4)
        qdec = big[:, 2 * TOK:6 * TOK].rearrange("p (g t) -> p g t", g=4)
        kdec = logf[:, :, :].rearrange("p i f -> p (i f)")[:, 0:4 * HW].rearrange("p (g f) -> p g f", g=4)
        diff = part(0, 4)
        inverse = part(2, 4)
        key_side = work[:, 4 * TOK:8 * TOK].rearrange("p (a c t) -> p a c t", a=2, c=2)
        query_side = work[:, 8 * TOK:12 * TOK].rearrange("p (a c t) -> p a c t", a=2, c=2)
        st_out = sb("st_out", [P, 4, HK])
        st_mid = sb("st_mid", [P, 4, HK])
        ho_sq = big[:, 6 * TOK:8 * TOK].rearrange("p (i f) -> p i f", i=NTILE)
        ho_r = sb("ho_r", [P, 2, NTILE * HH])
        edge = sb("edge", [P, 4])
        tick = sb("tick", [P, 1])
        at = [0]

        def scratch(*shape):
            n = 1
            for k in shape:
                n *= k
            v = work[:, at[0]:at[0] + n]
            at[0] += n
            assert at[0] <= 8 * TOK
            return v.rearrange("p (a b) -> p a b", a=shape[0]) if len(shape) == 2 else v

        score, biased, gsel = scratch(NTILE, E), scratch(NTILE, E), scratch(NTILE, E)
        tops, gsum = scratch(NTILE * NG, 8), scratch(NTILE, NG)
        cmp_a, cmp_b = scratch(NTILE, NG * NG), scratch(NTILE, NG * NG)
        rank, gpen, best, wsum = scratch(NTILE * NG), scratch(NTILE * NG), scratch(NTILE, 8), scratch(NTILE)
        gatesT = sb("gatesT", [E, TOK])
        gate_b = work[:, 0:8 * TOK].rearrange("p (i s t) -> p i s t", i=2, s=GSLOT)
        sil = part(8, 10)
        act = part(10, 12)

        def flat(ap):
            return ap.rearrange("p c t -> p (c t)")

        coff, _ = const_offsets()

        def const(name):
            a, b = coff[name]
            return consts[:, a:b]

        ident = const("ident")
        gates_dram = nc.dram_tensor("gates_scratch", (E, TOK), F32, kind="Internal").ap()

        banks = Banks([ctx.enter_context(nc.psum_tensor(f"bank{b}", [P, 512], F32)) for b in range(8)],
                      [sem(f"bank{b}_full") for b in range(8)], [sem(f"bank{b}_empty") for b in range(8)], DEPTH)
        CUTS = len(HALVES)
        NLEV = CUTS + 2
        banks.plan("start", "xT", 2 * NTILE)
        banks.turn = 0
        for stage, n in (("ada0", 2), ("ms1", 1), ("modT0", 1), ("ada1", 2), ("modT1", 1),
                         ("ada2", 2), ("q", DH), ("k", DH), ("modT2", 1), ("v", NTILE), ("fn", NTILE), ("hq", 2),
                         ("hif", NTILE), ("hbg", NTILE), ("k_rows", 1), ("ckT", 1), ("rotq", 2), ("rotk", 2),
                         ("four1", 4), ("zT", 2), ("fnT", 2), ("kkT", 4), ("cum", 4), ("past", 2), ("ada3", 2)):
            banks.plan("layer", stage, n)
        for use in range(2 * NTILE * NLEV):
            if use == 2 * NTILE:
                banks.plan("layer", "modT3", 1)
            banks.plan_one("layer", "lev", use, banks.turn % 8)
            banks.turn += 1
        for stage, n in (("st", 2), ("ho", 2)):
            banks.plan("layer", stage, n)
        UNITS = [(t, hd) for t in range(NTILE) for hd in range(DH)]
        NU = len(UNITS)
        ring6 = 0
        for u in range(NU + 3):
            if u < NU:
                for m in range(2):
                    banks.plan_one("layer", "sc", 2 * u + m, ring6 % 6)
                    ring6 += 1
            if 2 <= u < NU + 2:
                banks.plan_one("layer", "wT", u - 2, ring6 % 6)
                ring6 += 1
            if u >= 3 and UNITS[u - 3][1] == 0:
                banks.plan_one("layer", "o", UNITS[u - 3][0], 6 + UNITS[u - 3][0] % 2)
        banks.turn = 0
        for stage, n in (("ada4", 2), ("oT", NTILE), ("hgT", 2), ("modT4", 1)):
            banks.plan("layer", stage, n)
        for stage, n in (("out", NJ), ("ms2", 1), ("ada5", 2), ("router", 1), ("modT5", 1), ("gT", 1)):
            banks.plan("layer", stage, n)
        banks.plan("layer", "G", 1, [6], each=E + 1)
        banks.plan("layer", "U", 1, [7], each=E + 1)
        banks.plan("layer", "y", 6, range(6))
        banks.turn = 0
        banks.plan("layer", "yT", NJ)
        banks.plan("final", "rows", 2 * NTILE)

        waited = sem("waited")
        consts_in = sem("consts_in")
        mod_params_in = sem("mod_params_in")
        params_in = sem("params_in")
        slot_full = [sem(f"slot{s}_full") for s in range(NSLOT)]
        slot_read = sem("slot_read")
        slots_idle = Signal(sem("slots_idle"), 1, 1)
        aT_zero = Signal(sem("aT_zero"))
        shared_in = sem("shared_in")
        gates_out = sem("gates_out")
        gate_in = [sem(f"gate{i}_in") for i in range(2)]
        results_out = sem("results_out")
        y_out = sem("y_out")
        squared = Signal(sem("squared"), 0, 1 + NJ)
        h_ready = Signal(sem("h_ready"), 0, 2 * NJ)
        scond_ready = sem("scond_ready")
        ones_ready = sem("ones_ready")
        rope_done = Signal(sem("rope_done"))
        fgate_ready = Signal(sem("fgate_ready"))
        logf_ready = Signal(sem("logf_ready"))
        kk_ready = Signal(sem("kk_ready"))
        lam_sum = Signal(sem("lam_sum"))
        lam_exp = Signal(sem("lam_exp"))
        ecum_ready = Signal(sem("ecum_ready"))
        qdec_ready = Signal(sem("qdec_ready"))
        kdec_ready = Signal(sem("kdec_ready"))
        diff_ready = Signal(sem("diff_ready"), 0, NLEV)
        fac_ready = Signal(sem("fac_ready"), 0, NLEV)
        pairs_summed = Signal(sem("pairs_summed"))
        pair_ready = Signal(sem("pair_ready"), 0, NLEV)
        sums_ready = Signal(sem("sums_ready"))
        roots_ready = Signal(sem("roots_ready"))
        hnorm_ready = Signal(sem("hnorm_ready"))
        ntop_ready = Signal(sem("ntop_ready"), 0, NU)
        wts_ready = Signal(sem("wts_ready"), 0, NU)
        anorm_ready = Signal(sem("anorm_ready"))
        gsel_ready = Signal(sem("gsel_ready"))
        VIS = E + 1
        gu_hi_ready, gu_lo_ready = Signal(sem("gu_hi_ready"), 0, VIS), Signal(sem("gu_lo_ready"), 0, VIS)
        dn_hi_ready, dn_lo_ready = Signal(sem("dn_hi_ready"), 0, VIS), Signal(sem("dn_lo_ready"), 0, VIS)
        h_hi_ready, h_lo_ready = Signal(sem("h_hi_ready"), 0, 2 * NJ), Signal(sem("h_lo_ready"), 0, NJ + 1)
        scond_split = sem("scond_split")
        scond_hi_ready = sem("scond_hi_ready")
        act_ready = Signal(sem("act_ready"), 0, VIS)
        act_hi_ready = Signal(sem("act_hi_ready"), 0, VIS)
        act_lo_ready = Signal(sem("act_lo_ready"), 0, VIS)
        applied = Signal(sem("applied"), 0, VIS - 1)
        x_ready = Signal(sem("x_ready"), 1, 2)
        final_g_in = sem("final_g_in")
        token_sums = sem("token_sums")
        token_mean = sem("token_mean")
        token_root = sem("token_root")
        lb_diff = sem("lb_diff")
        lb_exp = sem("lb_exp")
        dve_order, act_order = sem("dve_order"), sem("act_order")

        w_ada_v = T["w_ada"].rearrange("l (p j) n -> l p j n", j=NJ)
        w_in_v = T["w_in"].rearrange("l (p j) n -> l p j n", j=NJ)
        w_out_v = T["w_out"].rearrange("l (c p) n -> l p c n", p=P)
        w_gate_v = T["w_gate"].rearrange("l e (p j) f -> l e p (j f)", j=NJ)
        w_up_v = T["w_up"].rearrange("l e (p j) f -> l e p (j f)", j=NJ)
        w_down_v = T["w_down"]

        def in_cols(l, c0, n):
            return w_in_v[l][:, :, c0:c0 + n]

        fixed = []

        def modulation_blocks(m, halves=(0, 1)):
            for half in halves:
                fixed.append((f"ada{m}", [(4, 1024, 0, lambda l, m=m, half=half:
                                           w_ada_v[l][:, 4 * half:4 * half + 4, m * D:(m + 1) * D])]))

        for m in range(2):
            modulation_blocks(m)
        modulation_blocks(2, (0,))
        for name, c0 in (("q", Q0), ("k", K0), ("v", V0)):
            fixed.append((name, [(NJ, 512, 0, lambda l, c0=c0: in_cols(l, c0, 512))]))
            if name == "q":
                modulation_blocks(2, (1,))
        fixed.append(("fn+hq", [(NJ, 256, 0, lambda l: in_cols(l, 0, 256)), (NJ, 256, 2048, lambda l: in_cols(l, HQ0, 256))]))
        fixed.append(("hif", [(NJ, 512, 0, lambda l: in_cols(l, HI0, 512))]))
        fixed.append(("hbg", [(NJ, 512, 0, lambda l: in_cols(l, HB0, 512))]))
        for m in (3, 4):
            modulation_blocks(m)
        for half in range(2):
            fixed.append(("out", [(4, 1024, 0, lambda l, half=half: w_out_v[l][:, 4 * half:4 * half + 4, :])]))
        modulation_blocks(5)
        NFIX = len(fixed)
        NBLK = NFIX + E
        assert NFIX % NSLOT == 0
        landed, fix_sum = [], [0] * NSLOT
        for b, (_, parts) in enumerate(fixed):
            fix_sum[b % NSLOT] += 16 * len(parts)
            landed.append(fix_sum[b % NSLOT])
        slot_layer = [fix_sum[s] + 48 * (E // NSLOT) for s in range(NSLOT)]

        def block_in(eng, l, b):
            eng.wait_ge(slot_full[b % NSLOT], l * slot_layer[b % NSLOT] + landed[b])
            return ring[:, b % NSLOT, :]

        def block_of(name, nth=0):
            return [b for b, (n, _) in enumerate(fixed) if n == name][nth]

        last_fill = {block_of("q"): ("q", DH - 1), block_of("k"): ("k", DH - 1), block_of("v"): ("v", NTILE - 1),
                     block_of("fn+hq"): ("hq", 1), block_of("hif"): ("hif", NTILE - 1), block_of("hbg"): ("hbg", NTILE - 1),
                     block_of("out", 1): ("out", NJ - 1)}
        for m in range(6):
            last_fill[block_of(f"ada{m}", 1)] = (f"ada{m}", 1)
        split_blocks = [b for b, (n, _) in enumerate(fixed) if n in ("ada1", "q", "k", "v", "fn+hq", "hif", "hbg")]
        for b in split_blocks:
            last_fill.pop(b, None)
        READS = NFIX - len(last_fill) - len(split_blocks)
        SPLIT_MODS = (1,)
        NUNIT = 2 * len(split_blocks)

        def unit_of(name, nth=0, half=0):
            return 2 * split_blocks.index(block_of(name, nth)) + half

        unit_fill = {unit_of("q", 0, 1): ("q", DH - 1), unit_of("k", 0, 1): ("k", DH - 1), unit_of("v", 0, 1): ("v", NTILE - 1),
                     unit_of("fn+hq", 0, 0): ("fn", NTILE - 1), unit_of("fn+hq", 0, 1): ("hq", 1),
                     unit_of("hif", 0, 1): ("hif", NTILE - 1), unit_of("hbg", 0, 1): ("hbg", NTILE - 1)}
        for m in SPLIT_MODS:
            unit_fill[unit_of(f"ada{m}", 1, 1)] = (f"ada{m}", 1)
        w_used = Signal(sem("w_used"), 0, NUNIT - len(unit_fill))
        w_hi_ready, w_lo_ready = Signal(sem("w_hi_ready"), 0, NUNIT), Signal(sem("w_lo_ready"), 0, NUNIT)

        def unit_used(eng, l, u):
            if u in unit_fill:
                banks.read(eng, *unit_fill[u])
            else:
                eng.wait_ge(w_used.sem, w_used.at(l, sum(1 for k in range(u + 1) if k not in unit_fill)))

        def unit_src(u):
            return ring[:, split_blocks[u // 2] % NSLOT, (u % 2) * UNIT:(u % 2 + 1) * UNIT]

        def slot_released(sp, l, b):
            prev = b - NSLOT
            if prev < 0:
                sp.wait_ge(slots_idle.sem, slots_idle.at(l, 0))
            elif prev in split_blocks:
                sp.wait_ge(w_lo_ready.sem, w_lo_ready.at(l, 2 * split_blocks.index(prev) + 2))
            elif prev in last_fill:
                banks.read(sp, *last_fill[prev])
            else:
                sp.wait_ge(slot_read, l * READS + sum(1 for k in range(prev + 1) if k not in last_fill and k not in split_blocks))
            apart(sp)

        NCONST, NPARAM = 7, 10

        def apart(eng):
            eng.sem_inc(waited, 1)

        block = ctx.enter_context(nc.Block())

        @block.sync
        def _(sp):
            sp.dma_start(rows[:, 0, :], T["x_prompt"][0]).then_inc(consts_in, 16)
            sp.dma_start(rows[:, 1:3, :], T["x_sample"][0].rearrange("(i p) d -> p i d", p=P)).then_inc(consts_in, 16)
            sp.dma_start(consts[:, :], CF).then_inc(consts_in, 16)
            sp.dma_start(masks_f, CM.rearrange("m p t -> p m t")).then_inc(consts_in, 16)
            sp.dma_start(cond[:, 0, :], T["c_ctx"].rearrange("(p j) -> p j", j=NJ)).then_inc(consts_in, 16)
            sp.dma_start(cond[:, 1, :], T["c"][0].rearrange("(p j) -> p j", j=NJ)).then_inc(consts_in, 16)
            sp.dma_start(lb_all[:, :, :], T["lower_bounds"].rearrange("l d w -> l (d w)").partition_broadcast(P))\
              .then_inc(consts_in, 16)
            with sp.Fori(0, DEPTH) as l:
                banks.enter("layer", l)
                for b, (_, parts) in enumerate(fixed):
                    slot_released(sp, l, b)
                    for j, n, at, src in parts:
                        dst = ring[:, b % NSLOT, at:at + j * n].rearrange("p (j n) -> p j n", j=j)
                        sp.dma_start(dst, src(l)).then_inc(slot_full[b % NSLOT], 16)

                def load_expert(s, e):
                    sp.dma_start(ring[:, s, 0:D], w_gate_v[l, e]).then_inc(slot_full[s], 16)
                    sp.dma_start(ring[:, s, D:2 * D], w_up_v[l, e]).then_inc(slot_full[s], 16)
                    sp.dma_start(ring[:, s, 2 * D:3 * D], w_down_v[l, e]).then_inc(slot_full[s], 16)

                for s in range(NSLOT):
                    slot_released(sp, l, NFIX + s)
                    load_expert(s, s)
                with sp.Fori(1, E // NSLOT) as turn:
                    for s in range(NSLOT):
                        sp.wait_ge(dn_lo_ready.sem, l * VIS + turn * NSLOT + s)
                        load_expert(s, turn * NSLOT + s)
            banks.enter("final")
            sp.wait_ge(x_ready.sem, x_ready.at(DEPTH, 0))
            sp.dma_start(final_g, T["final_g"].partition_broadcast(P)).then_inc(final_g_in, 16)
            for i in range(2):
                banks.wait_emptied(sp, "rows", i)
            sp.dma_start(y_prompt[0], rows[:, 0, :]).then_inc(y_out, 16)
            for i in range(2, 2 * NTILE):
                banks.wait_emptied(sp, "rows", i)
            sp.dma_start(y_sample[0].rearrange("(i p) d -> p i d", p=P), rows[:, 1:3, :]).then_inc(y_out, 16)
            sp.wait_ge(y_out, 32)
            sp.wait_ge(results_out, 48 * DEPTH)

        @block.gpsimd
        def _(pool):
            def over_partitions(ap):
                return ap.partition_broadcast(P)

            with pool.Fori(0, DEPTH) as l:
                pool.wait_ge(x_ready.sem, x_ready.at(l, 0))
                apart(pool)
                pool.dma_start(b_ada[:, :, :], T["b_ada"][l].rearrange("(m p j) -> p m j", p=P, j=NJ)).then_inc(mod_params_in, 16)
                pool.dma_start(norm_g[:, :, :], T["norm_g"][l].rearrange("m (p j) -> p m j", j=NJ)).then_inc(mod_params_in, 16)
                for dst, src in (
                    (attn_g[:, :], over_partitions(T["attn_norm_g"][l])),
                    (hg_g[:, :], over_partitions(T["hg_norm_g"][l])),
                    (lambdas[:, :, :], over_partitions(T["lambdas"][l])),
                    (lam_init[:, :], over_partitions(T["lam_init"][l])),
                    (r_bias[:, :], over_partitions(T["router_bias"][l])),
                    (w_four[:, :, :], T["w_fourier"][l].rearrange("(c p) n -> p c n", p=P)),
                    (w_router[:, :, :], T["w_router"][l].rearrange("(p j) e -> p j e", j=NJ)),
                    (cache_k[:, :], T["cache_k"][0][l].rearrange("t h d -> t (h d)")),
                    (cache_v[:, :], T["cache_v"][0][l].rearrange("t h d -> t (h d)")),
                    (state0[:, :, :], T["state_hgrn"][0][l].rearrange("d (a b) k v -> (b k) (d a) v", b=2)),
                ):
                    pool.dma_start(dst, src).then_inc(params_in, 16)
                banks.enter("layer", l)
                banks.wait_emptied(pool, "v", 0)
                apart(pool)
                pool.dma_start(new_v[0][l].rearrange("t h d -> t (h d)"), val[:, 0, :]).then_inc(results_out, 16)
                unit_used(pool, l, NUNIT - 2)
                apart(pool)
                nc.gpsimd.memset(w_shared, 0.0).then_inc(aT_zero.sem, 1)
                banks.wait_emptied(pool, "k_rows")
                apart(pool)
                pool.dma_start(new_k[0][l].rearrange("t h d -> t (h d)"), k_rows[:, :]).then_inc(results_out, 16)
                banks.wait_emptied(pool, "st", 0)
                apart(pool)
                pool.dma_start(new_state[0][l].rearrange("d (a b) k v -> (b k) (d a) v", b=2), st_out[:, :, :])\
                    .then_inc(results_out, 16)
                banks.read(pool, "ho", 1)
                apart(pool)
                for i, src in enumerate((T["ws_gate"][l].rearrange("(p j) f -> p (j f)", j=NJ),
                                         T["ws_up"][l].rearrange("(p j) f -> p (j f)", j=NJ), T["ws_down"][l])):
                    pool.dma_start(w_shared[:, i * D:(i + 1) * D], src).then_inc(shared_in, 16)
                pool.wait_ge(results_out, l * 48 + 48)
                banks.wait_emptied(pool, "gT")
                apart(pool)
                pool.dma_start(gates_dram, gatesT[:, :]).then_inc(gates_out, 16)
                pool.wait_ge(gates_out, l * 16 + 16)
                apart(pool)

                def load_gates(i, e0):
                    pool.dma_start(gate_b[:, i, :, :].rearrange("p e t -> p (e t)"),
                                   over_partitions(gates_dram[bass.ds(e0, GSLOT), :].rearrange("e t -> (e t)")))\
                        .then_inc(gate_in[i], 16)

                for i in range(2):
                    load_gates(i, i * GSLOT)
                with pool.Fori(0, E // (2 * GSLOT) - 1) as turn:
                    for i in range(2):
                        pool.wait_ge(act_ready.sem, l * VIS + turn * (2 * GSLOT) + (1 + (i + 1) * GSLOT))
                        apart(pool)
                        load_gates(i, turn * (2 * GSLOT) + (2 + i) * GSLOT)

        @block.tensor
        def _(pe):
            mm = nc.tensor.matmul
            tr = nc.tensor.transpose
            pe.wait_ge(consts_in, 16 * NCONST)
            pe.wait_ge(ones_ready, 1)
            banks.enter("start")
            for bank_empty in banks.empty_sem:
                pe.sem_inc(bank_empty, 1)
            for t in range(NTILE):
                for half in range(2):
                    bk = banks.claim(pe, "xT", 2 * t + half)
                    for j in range(4):
                        last = tr(bk[:, j * P:(j + 1) * P], rows[:, t, 4 * half + j:D:NJ], ident)
                    banks.filled(last, "xT", 2 * t + half)
            pe.wait_ge(scond_split, 1)

            def mean_square(stage):
                bk = banks.claim(pe, stage)
                for j in range(NJ):
                    last = mm(bk[:, 0:TOK], ones[:, :], squares[:, j, :], start=(j == 0), stop=(j == NJ - 1))
                banks.filled(last, stage)

            with pe.Fori(0, DEPTH) as l:
                banks.enter("layer", l)

                def split_product(out, a, b, start, stop):
                    mm(out, a[0], b[0], start=start, stop=False)
                    mm(out, a[0], b[1], start=False, stop=False)
                    return mm(out, a[1], b[0], start=False, stop=stop)

                def unit_in(u):
                    pe.wait_ge(w_lo_ready.sem, w_lo_ready.at(l, u + 1))
                    return w_hi[u % 2], w_lo[u % 2]

                def modulation_product(m):
                    for q in range(4):
                        u = unit_of(f"ada{m}") + q
                        w = [part.rearrange("p (j n) -> p j n", j=2) for part in (ap[:, :] for ap in unit_in(u))]
                        for ji in range(2):
                            for c in range(2):
                                if q == 0 and ji == 0:
                                    banks.claim(pe, f"ada{m}", c)
                                bk = banks.banks[banks.uses["layer"][f"ada{m}", c][0]]
                                for k in range(2):
                                    last = mm(bk[0:4, :], scond_r[:, 2 * q + ji, :], w[k][:, ji, c * 512:(c + 1) * 512],
                                              start=(q == 0 and ji == 0 and k == 0), stop=(q == 3 and ji == 1 and k == 1))
                                if q == 3 and ji == 1:
                                    banks.filled(last, f"ada{m}", c)
                        if q < 3:
                            last.then_inc(w_used.sem, 1)

                def float32_modulation_product(m, halves=(0, 1)):
                    for half in halves:
                        b = block_of(f"ada{m}", half)
                        w = block_in(pe, l, b).rearrange("p (j n) -> p j n", j=4)
                        for ji in range(4):
                            for c in range(2):
                                if half == 0 and ji == 0:
                                    banks.claim(pe, f"ada{m}", c)
                                bk = banks.banks[banks.uses["layer"][f"ada{m}", c][0]]
                                last = mm(bk[0:2, :], scond[:, 4 * half + ji, :], w[:, ji, c * 512:(c + 1) * 512],
                                          start=(half == 0 and ji == 0), stop=(half == 1 and ji == 3))
                                if half == 1 and ji == 3:
                                    banks.filled(last, f"ada{m}", c)
                        if half == 0:
                            last.then_inc(slot_read, 1)

                def modulation_turned(m):
                    n = 4 if m in SPLIT_MODS else 2
                    for c in range(2):
                        banks.wait_emptied(pe, f"ada{m}", c)
                    bk = banks.claim(pe, f"modT{m}")
                    apart(pe)
                    for j in range(NJ):
                        last = tr(bk[:, n * j:n * (j + 1)], mod_rows[0:n, m % 2, j:D:NJ], ident[0:n, 0:n])
                    banks.filled(last, f"modT{m}")

                float32_modulation_product(0)
                pe.wait_ge(squared.sem, squared.at(l, 1))
                mean_square("ms1")
                modulation_turned(0)
                modulation_product(1)
                modulation_turned(1)
                float32_modulation_product(2, (0,))

                def h_in(j):
                    pe.wait_ge(h_lo_ready.sem, h_lo_ready.at(l, j + 1))

                def feature_major(stage, n, units, first=False):
                    per = NJ // len(units)
                    for k, u in enumerate(units):
                        w = [part[:, :].rearrange("p (j n) -> p j n", j=per) for part in unit_in(u)]
                        for i in range(n):
                            if k == 0:
                                banks.claim(pe, stage, i)
                            bk = banks.banks[banks.uses["layer"][stage, i][0]]
                            for jj in range(per):
                                j = k * per + jj
                                if first and i == 0:
                                    h_in(j)
                                last = split_product(bk[:, 0:TOK], [w[0][:, jj, i * P:(i + 1) * P], w[1][:, jj, i * P:(i + 1) * P]],
                                                     [h_hi[:, j, :], h_lo[:, j, :]], j == 0, j == NJ - 1)
                            if k == len(units) - 1:
                                banks.filled(last, stage, i)
                        if k < len(units) - 1:
                            last.then_inc(w_used.sem, 1)

                def token_major(stage, n, units):
                    per = NJ // len(units)
                    for k, u in enumerate(units):
                        w = [part[:, :].rearrange("p (j n) -> p j n", j=per) for part in unit_in(u)]
                        for t in range(NTILE):
                            if k == 0:
                                banks.claim(pe, stage, t)
                            bk = banks.banks[banks.uses["layer"][stage, t][0]]
                            cols = slice(t * P, (t + 1) * P)
                            for jj in range(per):
                                j = k * per + jj
                                last = split_product(bk[:, 0:n], [h_hi[:, j, cols], h_lo[:, j, cols]],
                                                     [w[0][:, jj, :], w[1][:, jj, :]], j == 0, j == NJ - 1)
                            if k == len(units) - 1:
                                banks.filled(last, stage, t)
                        if k < len(units) - 1:
                            last.then_inc(w_used.sem, 1)

                def units_of(name):
                    return [unit_of(name), unit_of(name, 0, 1)]

                feature_major("q", DH, units_of("q"), first=True)
                float32_modulation_product(2, (1,))
                feature_major("k", DH, units_of("k"))
                modulation_turned(2)
                token_major("v", DA, units_of("v"))
                token_major("fn", FN, units_of("fn+hq")[0:1])
                feature_major("hq", 2, units_of("fn+hq")[1:2])
                token_major("hif", 2 * HW, units_of("hif"))
                token_major("hbg", 2 * HW, units_of("hbg"))

                bk = banks.claim(pe, "k_rows")
                for i in range(DH):
                    banks.wait_emptied(pe, "k", i)
                    last = tr(bk[:, i * P:(i + 1) * P], kT[:, i, 0:P], ident)
                banks.filled(last, "k_rows")
                bk = banks.claim(pe, "ckT")
                pe.wait_ge(params_in, l * (16 * NPARAM) + 16 * NPARAM)
                for i in range(DH):
                    last = tr(bk[:, i * P:(i + 1) * P], cache_k[:, i * P:(i + 1) * P], ident)
                banks.filled(last, "ckT")
                for stage, src in (("rotq", qT), ("rotk", kT)):
                    for i in range(2):
                        bk = banks.claim(pe, stage, i)
                        for a in range(2):
                            banks.wait_emptied(pe, "q" if src is qT else "k", 2 * i + a)
                            last = mm(bk[:, a * 256:(a + 1) * 256], const("rot"), src[:, 2 * i + a, P:TOK], start=True, stop=True)
                        banks.filled(last, stage, i)

                for c in range(2):
                    for k, (cc, cl) in enumerate((("c_ctx", "c_lat"), ("s_ctx", "s_lat"))):
                        bk = banks.claim(pe, "four1", 2 * c + k)
                        banks.wait_emptied(pe, "fn", 0)
                        mm(bk[:, 0:P], u_fn[:, 0, c * P:(c + 1) * P], const(cc), start=True, stop=True)
                        for t in range(2):
                            banks.wait_emptied(pe, "fn", 1 + t)
                            last = mm(bk[:, P:TOK], u_fn[:, 1 + t, c * P:(c + 1) * P], const(cl)[:, t * 256:(t + 1) * 256],
                                      start=(t == 0), stop=(t == 1))
                        banks.filled(last, "four1", 2 * c + k)
                for c in range(2):
                    bk = banks.claim(pe, "zT", c)
                    for k, name in enumerate(("c_chan", "s_chan")):
                        banks.wait_emptied(pe, "four1", 2 * c + k)
                        last = mm(bk[:, 0:TOK], const(name), four1[:, 2 * c + k, :], start=(k == 0), stop=(k == 1))
                    banks.filled(last, "zT", c)
                for c in range(2):
                    bk = banks.claim(pe, "fnT", c)
                    for k in range(2):
                        banks.wait_emptied(pe, "zT", k)
                        last = mm(bk[:, 0:TOK], w_four[:, k, c * P:(c + 1) * P], zT[:, k, :], start=(k == 0), stop=(k == 1))
                    banks.filled(last, "fnT", c)

                pe.wait_ge(kk_ready.sem, kk_ready.at(l, 1))
                for g in range(4):
                    bk = banks.claim(pe, "kkT", g)
                    for t in range(NTILE):
                        last = tr(bk[:, t * P:(t + 1) * P], kk[:, t, g * P:(g + 1) * P], ident)
                    banks.filled(last, "kkT", g)
                pe.wait_ge(logf_ready.sem, logf_ready.at(l, 1))
                for g in range(4):
                    bk = banks.claim(pe, "cum", g)
                    for t in range(NTILE):
                        last = mm(bk[:, t * P:(t + 1) * P], logf[:, t, g * P:(g + 1) * P], const("tri_f" if g < 2 else "tri_b"),
                                  start=True, stop=True)
                    banks.filled(last, "cum", g)
                for i, tiles in enumerate(((0, 0), (1, 2))):
                    bk = banks.claim(pe, "past", i)
                    for d, t in enumerate(tiles):
                        last = mm(bk[:, d * HW:(d + 1) * HW], const("past_f" if d == 0 else "past_b"),
                                  logf[:, t, d * HW:(d + 1) * HW], start=True, stop=True)
                    banks.filled(last, "past", i)
                float32_modulation_product(3)

                for n in range(NLEV):
                    if n == 1:
                        modulation_turned(3)
                    ka, qa = key_side[:, n % 2, :, :], query_side[:, n % 2, :, :]
                    pe.wait_ge(pair_ready.sem, pair_ready.at(l, n + 1))
                    for t in range(NTILE):
                        for odd in range(2):
                            use = (n * NTILE + t) * 2 + odd
                            bk = banks.claim(pe, "lev", use)
                            r = slice(HK * odd, HK * (odd + 1))
                            for c in range(2):
                                last = mm(bk[:, c * P:(c + 1) * P], ka[r, c, t * P:(t + 1) * P],
                                          qa[r, c, t * P:(t + 1) * P], start=True, stop=True)
                            banks.filled(last, "lev", use)

                pe.wait_ge(kdec_ready.sem, kdec_ready.at(l, 1))
                for i, tiles in enumerate(((0, 0), (1, 2))):
                    bk = banks.claim(pe, "st", i)
                    for d, t in enumerate(tiles):
                        for a in range(2):
                            last = mm(bk[:, (2 * d + a) * P:(2 * d + a + 1) * P], kdec[:, 2 * i + d, a * P:(a + 1) * P],
                                      hv[:, t, a * P:(a + 1) * P], start=True, stop=True)
                    banks.filled(last, "st", i)

                pe.wait_ge(qdec_ready.sem, qdec_ready.at(l, 1))
                pe.wait_ge(pairs_summed.sem, pairs_summed.at(l, 1))
                banks.wait_emptied(pe, "st", 1)
                for odd in range(2):
                    bk = banks.claim(pe, "ho", odd)
                    r = slice(HK * odd, HK * (odd + 1))
                    for t in range(NTILE):
                        for c in range(2):
                            hd = 2 * c + odd
                            out = bk[:, (2 * t + c) * HK:(2 * t + c + 1) * HK]
                            v = hv[:, t, hd * HK:(hd + 1) * HK]
                            last = mm(out, aT[:, 0, t, hd * P:(hd + 1) * P], v, start=True, stop=(t == 0))
                            if t > 0:
                                for d in range(2):
                                    src = state0 if (t == 1) == (d == 0) else st_mid
                                    last = mm(out, qdec[r, 2 * d + c, t * P:(t + 1) * P], src[r, 2 * d + c, :],
                                              start=False, stop=(d == 1))
                    banks.filled(last, "ho", odd)

                pe.wait_ge(rope_done.sem, rope_done.at(l, 1))
                banks.wait_emptied(pe, "ckT")
                for u in range(NU + 3):
                    if u < NU:
                        t, hd = UNITS[u]
                        keys = slice(0, P) if t == 0 else slice(P, KEYS)
                        for m in range(2):
                            bk = banks.claim(pe, "sc", 2 * u + m)
                            r = slice(m * DK, (m + 1) * DK)
                            last = mm(bk[:, 0:keys.stop - keys.start], qT[r, hd, t * P:(t + 1) * P], kT[r, hd, keys],
                                      start=True, stop=True)
                            banks.filled(last, "sc", 2 * u + m)
                    if 2 <= u < NU + 2:
                        v = u - 2
                        bk = banks.claim(pe, "wT", v)
                        pe.wait_ge(wts_ready.sem, wts_ready.at(l, v + 1))
                        for i in range(1 if UNITS[v][0] == 0 else 3):
                            last = tr(bk[:, i * P:(i + 1) * P], wts[:, v % 2, i * P:(i + 1) * P], ident)
                        banks.filled(last, "wT", v)
                    if u >= 3:
                        v = u - 3
                        t, hd = UNITS[v]
                        if hd == 0:
                            obk = banks.claim(pe, "o", t)
                        banks.wait_emptied(pe, "wT", v)
                        srcs = [val[:, 0, :]] if t == 0 else [val[:, 1, :], val[:, 2, :], cache_v[:, :]]
                        for i, src in enumerate(srcs):
                            last = mm(obk[:, hd * P:(hd + 1) * P], wT[:, v % 2, i * P:(i + 1) * P], src[:, hd * VD:(hd + 1) * VD],
                                      start=(i == 0), stop=(i == len(srcs) - 1))
                        if hd == DH - 1:
                            banks.filled(last, "o", t)
                float32_modulation_product(4)
                for t in range(NTILE):
                    bk = banks.claim(pe, "oT", t)
                    pe.wait_ge(anorm_ready.sem, anorm_ready.at(l, 1))
                    for hd in range(DH):
                        last = tr(bk[:, hd * P:(hd + 1) * P], att[:, t, hd * P:(hd + 1) * P], ident)
                    banks.filled(last, "oT", t)
                pe.wait_ge(hnorm_ready.sem, hnorm_ready.at(l, 1))
                for c in range(2):
                    bk = banks.claim(pe, "hgT", c)
                    for t in range(NTILE):
                        last = tr(bk[:, t * P:(t + 1) * P], gate_o[:, t, c * P:(c + 1) * P], ident)
                    banks.filled(last, "hgT", c)
                modulation_turned(4)

                for c in range(2):
                    banks.wait_emptied(pe, "fnT", c)
                    banks.wait_emptied(pe, "hgT", c)
                for t in range(NTILE):
                    banks.wait_emptied(pe, "oT", t)
                def square_summed(j):
                    if j == 0:
                        banks.claim(pe, "ms2")
                    pe.wait_ge(squared.sem, squared.at(l, 2 + j))
                    bk = banks.banks[banks.uses["layer"]["ms2", 0][0]]
                    ins = mm(bk[:, 0:TOK], ones[:, :], squares[:, j, :], start=(j == 0), stop=(j == NJ - 1))
                    if j == NJ - 1:
                        banks.filled(ins, "ms2")

                for half in range(2):
                    w = block_in(pe, l, block_of("out", half)).rearrange("p (c n) -> p c n", c=4)
                    for j in range(NJ):
                        if half == 0:
                            banks.claim(pe, "out", j)
                        bk = banks.banks[banks.uses["layer"]["out", j][0]]
                        for c in range(4):
                            last = mm(bk[:, 0:TOK], w[:, c, j:D:NJ], mixT[:, 4 * half + c, :],
                                      start=(half == 0 and c == 0), stop=(half == 1 and c == 3))
                        if half == 1:
                            banks.filled(last, "out", j)
                            if j >= 2:
                                square_summed(j - 2)
                    if half == 0:
                        last.then_inc(slot_read, 1)

                for j in range(NJ - 2, NJ):
                    square_summed(j)
                float32_modulation_product(5)
                pe.wait_ge(h_ready.sem, h_ready.at(l, 2 * NJ))
                bk = banks.claim(pe, "router")
                for t in range(NTILE):
                    for j in range(NJ):
                        last = mm(bk[:, t * E:(t + 1) * E], h[:, j, t * P:(t + 1) * P], w_router[:, j, :],
                                  start=(j == 0), stop=(j == NJ - 1))
                banks.filled(last, "router")

                def up(n, buf):
                    pe.wait_ge(gu_lo_ready.sem, l * VIS + n + 1)
                    for k, stage in enumerate(("G", "U")):
                        bk = banks.claim(pe, stage, 0, n)
                        for j in range(NJ):
                            cols = slice(k * D + j * P, k * D + (j + 1) * P)
                            mm(bk[:, 0:TOK], gu_hi[:, buf, cols], h_hi[:, j, :], start=(j == 0), stop=False)
                            mm(bk[:, 0:TOK], gu_hi[:, buf, cols], h_lo_late[:, j, :], start=False, stop=False)
                            last = mm(bk[:, 0:TOK], gu_lo[:, buf, cols], h_hi[:, j, :], start=False, stop=(j == NJ - 1))
                        banks.filled(last, stage)

                def down(n, buf, first, last_one):
                    pe.wait_ge(dn_lo_ready.sem, l * VIS + n + 1)
                    pe.wait_ge(act_lo_ready.sem, l * VIS + n + 1)
                    for t in range(NTILE):
                        rows_of = slice(t * P, (t + 1) * P)
                        for c in range(2):
                            if first:
                                banks.claim(pe, "y", 2 * t + c)
                            y, cols = banks.banks[2 * t + c][:, :], slice(c * 512, (c + 1) * 512)
                            mm(y, act_hi[:, buf, rows_of], dn_hi[:, buf, cols], start=first, stop=False)
                            mm(y, act_hi[:, buf, rows_of], dn_lo[:, buf, cols], start=False, stop=False)
                            last = mm(y, act_lo[:, buf, rows_of], dn_hi[:, buf, cols], start=False, stop=last_one)
                            if last_one:
                                banks.filled(last, "y", 2 * t + c)
                    if not last_one:
                        last.then_inc(applied.sem, 1)

                pe.wait_ge(h_lo_ready.sem, h_lo_ready.at(l, NJ + 1))
                up(0, 0)
                modulation_turned(5)
                pe.wait_ge(gsel_ready.sem, gsel_ready.at(l, 1))
                bk = banks.claim(pe, "gT")
                apart(pe)
                for t in range(NTILE):
                    last = tr(bk[0:E, t * P:(t + 1) * P], gsel[:, t, :], ident)
                banks.filled(last, "gT")
                up(1, 1)
                down(0, 0, True, False)
                with pe.Fori(0, E // 2 - 1) as turn:
                    for s in range(2):
                        up(turn * 2 + (s + 2), s)
                        down(turn * 2 + (s + 1), 1 - s, False, False)
                up(E, 0)
                down(E - 1, 1, False, False)
                down(E, 0, False, True)

                for i in range(6):
                    banks.wait_emptied(pe, "y", i)
                for j in range(NJ):
                    bk = banks.claim(pe, "yT", j)
                    for t in range(NTILE):
                        last = tr(bk[:, t * P:(t + 1) * P], rows[:, t, j:D:NJ], ident)
                    banks.filled(last, "yT", j)

            banks.enter("final")
            pe.wait_ge(x_ready.sem, x_ready.at(DEPTH, 0))
            for t in range(NTILE):
                for half in range(2):
                    bk = banks.claim(pe, "rows", 2 * t + half)
                    for j in range(4):
                        last = tr(bk[:, j * P:(j + 1) * P], x[:, 4 * half + j, t * P:(t + 1) * P], ident)
                    banks.filled(last, "rows", 2 * t + half)

        @block.scalar
        def _(act_e):
            af = nc.scalar.activation
            order = InOrder(act_e, act_order, 0, 2, DEPTH)
            after = order.after

            act_e.wait_ge(consts_in, 16 * NCONST)
            af(scond[:, :, :], cond[:, :, :].rearrange("p s j -> p j s"), ACT.Silu).then_inc(scond_ready, 1)
            act_e.wait_ge(scond_ready, 1)
            af(scond_r[:, :, 0:2], scond[:, :, :], ACT.Copy).then_inc(scond_hi_ready, 1)
            act_e.wait_ge(lb_diff, 1)
            af(kk[:, 1:3, :], kk[:, 1:3, :], ACT.Exp).then_inc(lb_exp, 1)

            def squares_of_x(state):
                act_e.wait_ge(x_ready.sem, state)
                af(squares, x[:, :, :], ACT.Square).then_inc(squared.sem, 1)

            def root_of_mean(stage):
                bk = banks.read(act_e, stage)
                banks.emptied(af(rms[:, :], bk[:, 0:TOK], ACT.Sqrt, bias=eps_t[:, :], scale=1.0 / D), stage)

            def rows_of_modulation(m):
                n = 4 if m in SPLIT_MODS else 2
                if m >= 2:
                    banks.read(act_e, f"modT{m - 2}")
                for c in range(2):
                    bk = banks.read(act_e, f"ada{m}", c)
                    banks.emptied(af(mod_rows[0:n, m % 2, c * 512:(c + 1) * 512], bk[0:n, :], ACT.Copy), f"ada{m}", c)

            with act_e.Fori(0, DEPTH) as l:
                order.enter("layer", l)
                banks.enter("layer", l)

                def split(units):
                    for u in units:
                        if u >= 2:
                            unit_used(act_e, l, u - 2)
                        block_in(act_e, l, split_blocks[u // 2])
                        af(w_hi[u % 2][:, :], unit_src(u), ACT.Copy).then_inc(w_hi_ready.sem, 1)

                def h_high(nth):
                    for j in range(NJ):
                        act_e.wait_ge(h_ready.sem, h_ready.at(l, (nth - 1) * NJ + j + 1))
                        af(h_hi[:, j, :], h[:, j, :], ACT.Copy).then_inc(h_hi_ready.sem, 1)

                squares_of_x(x_ready.at(l, 0))
                rows_of_modulation(0)
                split(range(0, 2))
                root_of_mean("ms1")
                split(range(2, 4))
                rows_of_modulation(1)
                split(range(4, 5))
                h_high(1)
                split(range(5, 8))

                def heads_out(stage, dst):
                    for i in range(DH):
                        bk = banks.read(act_e, stage, i)
                        banks.emptied(af(dst[:, i, 0:TOK], bk[:, 0:TOK], ACT.Copy), stage, i)

                heads_out("q", qT)
                rows_of_modulation(2)
                split(range(8, 10))
                heads_out("k", kT)
                split(range(10, 13))
                for t in range(NTILE):
                    bk = banks.read(act_e, "fn", t)
                    banks.emptied(af(u_fn[:, t, :], bk[:, 0:FN], ACT.Copy), "fn", t)
                split(range(13, 14))
                for i in range(2):
                    bk = banks.read(act_e, "hq", i)
                    banks.emptied(af(hqT[:, i, :], bk[:, 0:TOK], ACT.Silu), "hq", i)
                split(range(14, NUNIT))
                for t in range(NTILE):
                    bk = banks.read(act_e, "hif", t)
                    af(hv[:, t, :], bk[:, 0:HW], ACT.Copy)
                    af(logf[:, t, 0:HW], bk[:, HW:2 * HW], ACT.Sigmoid)
                    banks.emptied(af(kk[:, t, 0:HW], bk[:, HW:2 * HW], ACT.Sigmoid, scale=-1.0), "hif", t)
                for t in range(NTILE):
                    bk = banks.read(act_e, "hbg", t)
                    af(logf[:, t, HW:2 * HW], bk[:, 0:HW], ACT.Sigmoid)
                    af(kk[:, t, HW:2 * HW], bk[:, 0:HW], ACT.Sigmoid, scale=-1.0)
                for t in range(NTILE):
                    bk = banks.read(act_e, "hbg", t)
                    banks.emptied(af(gate_o[:, t, :], bk[:, HW:2 * HW], ACT.Silu), "hbg", t)

                bk = banks.read(act_e, "k_rows")
                banks.emptied(af(k_rows[:, :], bk[:, :], ACT.Copy), "k_rows")
                bk = banks.read(act_e, "ckT")
                banks.emptied(af(kT[:, :, TOK:KEYS], bk[:, :].rearrange("p (a t) -> p a t", a=DH), ACT.Copy), "ckT")

                act_e.wait_ge(fgate_ready.sem, fgate_ready.at(l, 1))
                af(logf[:, :, :], logf[:, :, :], ACT.Ln).then_inc(logf_ready.sem, 1)

                for i in range(4):
                    bk = banks.read(act_e, "four1", i)
                    banks.emptied(af(four1[:, i, :], bk[:, 0:TOK], ACT.Copy), "four1", i)
                for c in range(2):
                    bk = banks.read(act_e, "zT", c)
                    banks.emptied(af(zT[:, c, :], bk[:, 0:TOK], ACT.Copy), "zT", c)
                for c in range(2):
                    bk = banks.read(act_e, "fnT", c)
                    banks.emptied(af(mixT[:, c, :], bk[:, 0:TOK], ACT.Copy), "fnT", c)

                for g in range(4):
                    bk = banks.read(act_e, "kkT", g)
                    banks.emptied(af(kkT[:, g, :], bk[:, 0:TOK], ACT.Copy), "kkT", g)
                for g in range(4):
                    bk = banks.read(act_e, "cum", g)
                    banks.emptied(af(cum[:, g, :], bk[:, 0:TOK], ACT.Copy), "cum", g)
                banks.read(act_e, "past", 1)
                for i in range(2):
                    bk = banks.read(act_e, "past", i)
                    banks.emptied(af(kdec[:, 2 * i:2 * i + 2, :], bk[:, :], ACT.Exp), "past", i)
                for g in range(4):
                    banks.wait_emptied(act_e, "cum", g)
                af(qdec[:, :, :], cum[:, :, :], ACT.Exp).then_inc(ecum_ready.sem, 1)
                act_e.wait_ge(lam_sum.sem, lam_sum.at(l, 1))
                af(lam_s[:, :], lam_s[:, :], ACT.Exp).then_inc(lam_exp.sem, 1)

                for n in range(NLEV):
                    if n == 2:
                        rows_of_modulation(3)
                    act_e.wait_ge(diff_ready.sem, diff_ready.at(l, n + 1))
                    if n < CUTS:
                        w = HALVES[n]
                        for d in range(2):
                            dv = flat(diff[:, 2 * d:2 * d + 2, :]).rearrange("p (b w) -> p b w", w=2 * w)
                            early, late = (-1.0, 1.0) if d == 0 else (1.0, -1.0)
                            af(dv[:, :, 0:w], dv[:, :, 0:w], ACT.Exp, scale=early)
                            last = af(dv[:, :, w:2 * w], dv[:, :, w:2 * w], ACT.Exp, scale=late)
                    else:
                        after(af(inverse, diff[:, 0:2, :], ACT.Exp, scale=-1.0))
                        last = af(diff[:, 0:2, :], diff[:, 0:2, :], ACT.Exp)
                    last.then_inc(fac_ready.sem, 1)

                for odd in range(2):
                    bk = banks.read(act_e, "ho", odd)
                    src = bk[:, 0:6 * HK].rearrange("p (i a d) -> p i a d", i=NTILE, a=2)
                    of_heads = lambda ap: ap.rearrange("p i (a b d) -> p i a b d", a=2, b=2)[:, :, :, odd, :]
                    af(of_heads(ho[:, :, :]), src, ACT.Copy)
                    banks.emptied(af(of_heads(ho_sq), src, ACT.Square), "ho", odd)

                for u in range(NU + 3):
                    if u < NU:
                        nk = P if UNITS[u][0] == 0 else KEYS - P
                        act_e.wait_ge(ntop_ready.sem, ntop_ready.at(l, u + 1))
                        for m in range(2):
                            bk = banks.read(act_e, "sc", 2 * u + m)
                            ins = af(prob[:, u % 2, m, 0:nk], bk[:, 0:nk], ACT.Exp, bias=ntop[:, u % 2, m:m + 1],
                                     scale=SCALE, accum_out=den[:, u % 2, m:m + 1])
                            banks.emptied(ins, "sc", 2 * u + m)
                    if 2 <= u < NU + 2:
                        v = u - 2
                        nk = P if UNITS[v][0] == 0 else 3 * P
                        bk = banks.read(act_e, "wT", v)
                        banks.emptied(af(wT[:, v % 2, 0:nk], bk[:, 0:nk], ACT.Copy), "wT", v)
                    if u >= 3 and UNITS[u - 3][1] == DH - 1:
                        t = UNITS[u - 3][0]
                        bk = banks.read(act_e, "o", t)
                        af(att[:, t, :], bk[:, :], ACT.Copy)
                        banks.emptied(af(att_sq[:, t, :], bk[:, :], ACT.Square), "o", t)
                act_e.wait_ge(sums_ready.sem, sums_ready.at(l, 1))
                af(att_r[:, 1, :], att_r[:, 0, :], ACT.Sqrt, bias=eps_t[:, :], scale=1.0 / VD)
                af(ho_r[:, 1, :], ho_r[:, 0, :], ACT.Sqrt, bias=eps_t[:, :], scale=1.0 / HK).then_inc(roots_ready.sem, 1)
                rows_of_modulation(4)
                for t in range(NTILE):
                    bk = banks.read(act_e, "oT", t)
                    banks.emptied(af(mixT[:, 2:6, t * P:(t + 1) * P], bk[:, :].rearrange("p (a t) -> p a t", a=DH), ACT.Copy), "oT", t)
                for c in range(2):
                    bk = banks.read(act_e, "hgT", c)
                    banks.emptied(af(mixT[:, 6 + c, :], bk[:, 0:TOK], ACT.Copy), "hgT", c)

                banks.read(act_e, "hgT", 1)
                act_e.wait_ge(results_out, l * 48 + 48)
                act_e.wait_ge(shared_in, l * 48 + 48)
                af(gu_hi[:, 0, :], w_shared[:, 0:2 * D], ACT.Copy).then_inc(gu_hi_ready.sem, 1)
                af(dn_hi[:, 0, :], w_shared[:, 2 * D:3 * D], ACT.Copy).then_inc(dn_hi_ready.sem, 1)

                for j in range(NJ):
                    banks.wait_emptied(act_e, "out", j)
                    af(squares[:, j, :], x[:, j, :], ACT.Square).then_inc(squared.sem, 1)
                root_of_mean("ms2")
                h_high(2)
                rows_of_modulation(5)
                bk = banks.read(act_e, "router")
                banks.emptied(af(score[:, :, :].rearrange("p i e -> p (i e)"), bk[:, 0:NTILE * E], ACT.Sigmoid), "router")

                def act_step(n, buf, e_mod, turn, has_gu, has_dn):
                    if not (isinstance(n, int) and n < 2):
                        act_e.wait_ge(act_ready.sem, l * VIS + n - 1)
                    bk = banks.read(act_e, "G", 0, n)
                    banks.emptied(af(sil[:, buf, :], bk[:, 0:TOK], ACT.Silu), "G")
                    act_e.wait_ge(act_ready.sem, l * VIS + n + 1)
                    af(act_hi[:, buf, :], act[:, buf, :], ACT.Copy).then_inc(act_hi_ready.sem, 1)
                    if has_gu:
                        banks.read(act_e, "U", 0, n)
                        split_gu(n + 2, buf, (e_mod + 1) % NSLOT, turn + (e_mod + 1) // NSLOT)
                    if has_dn:
                        if not (isinstance(n, int) and n == 0):
                            act_e.wait_ge(applied.sem, l * (VIS - 1) + n)
                        split_dn(1 - buf, ring[:, e_mod % NSLOT, 2 * D:3 * D])

                def split_gu(n, buf, slot, turn):
                    act_e.wait_ge(slot_full[slot], l * slot_layer[slot] + turn * 48 + (fix_sum[slot] + 48))
                    af(gu_hi[:, buf, :], ring[:, slot, 0:2 * D], ACT.Copy).then_inc(gu_hi_ready.sem, 1)

                def split_dn(buf, src):
                    af(dn_hi[:, buf, :], src, ACT.Copy).then_inc(dn_hi_ready.sem, 1)

                split_gu(1, 1, 0, 0)
                act_step(0, 0, 0, 0, True, True)
                with act_e.Fori(0, (E - 8) // 8) as turn:
                    for k in range(8):
                        act_step(turn * 8 + (k + 1), (k + 1) % 2, k + 1, turn * 4, True, True)
                for e in range(E - 8, E):
                    act_step(e + 1, (e + 1) % 2, e + 1 - (E - 8), (E - 8) // 2, e + 2 < E, e + 1 < E)
                for t in range(NTILE):
                    bk = banks.read(act_e, "y", 2 * t)
                    banks.emptied(af(rows[:, t, 0:512], bk[:, :], ACT.Copy), "y", 2 * t)

            banks.enter("final")
            for i in range(2 * NTILE):
                bk = banks.read(act_e, "rows", i)
                last = af(work[:, i * 512:(i + 1) * 512], bk[:, :], ACT.Square, accum_out=mean_sq[:, i // 2, i % 2:i % 2 + 1])
            last.then_inc(token_sums, 1)
            act_e.wait_ge(token_mean, 1)
            af(token_r[:, 0, :], token_r[:, 1, :], ACT.Sqrt, bias=eps_t[:, :], scale=1.0 / D).then_inc(token_root, 1)

        @block.vector
        def _(dve):
            tt, ts, stt = nc.vector.tensor_tensor, nc.vector.tensor_scalar, nc.vector.scalar_tensor_tensor
            copy, red = nc.vector.tensor_copy, nc.vector.tensor_reduce
            order = InOrder(dve, dve_order, 5, LAYER_DVE, DEPTH)
            after = order.after
            order.enter("start")
            banks.enter("start")
            nc.vector.memset(eps_t[:, :], EPS)
            nc.vector.memset(ones[:, :], 1.0).then_inc(ones_ready, 1)
            dve.sem_inc(slots_idle.sem, 1)
            dve.wait_ge(consts_in, 16 * NCONST)
            copy(masks[:, :, :], masks_f)
            dve.wait_ge(scond_hi_ready, 1)
            tt(scond_r[:, :, 2:4], scond[:, :, :], scond_r[:, :, 0:2].bitcast(F32), ALU.subtract).then_inc(scond_split, 1)
            after(tt(kk[:, 0, :], lb_all[:, 0, :], lb_all[:, 1, :], ALU.max))
            tt(kk[:, 1:3, :], lb_all[:, :, :], kk[:, 0, :].unsqueeze(1).broadcast_to([P, 2, 2 * HW]), ALU.subtract).then_inc(lb_diff, 1)
            for t in range(NTILE):
                for half in range(2):
                    bk = banks.read(dve, "xT", 2 * t + half)
                    banks.emptied(copy(x[:, 4 * half:4 * half + 4, t * P:(t + 1) * P],
                                       bk[:, :].rearrange("p (j t) -> p j t", j=4)), "xT", 2 * t + half)
            dve.wait_ge(lb_exp, 1)
            after(tt(kk[:, 0, :], kk[:, 1, :], kk[:, 2, :], ALU.add))
            after(nc.vector.reciprocal(kk[:, 0, :], kk[:, 0, :]))
            after(nc.vector.memset(lb_all[:, 0, :], 0.0))
            after(tt(lb_all[:, 1, :], kk[:, 2, :], kk[:, 0, :], ALU.mult))
            nc.vector.memset(tick[:, :], 0.0).then_inc(x_ready.sem, 1)
            order.leave()

            def modulation(m):
                bk = banks.read(dve, f"modT{m}")
                banks.emptied(tt(mod[:, m, :, :], bk[:, 0:2 * NJ].rearrange("p (j s) -> p j s", s=2),
                                 b_ada[:, m, :].unsqueeze(2).broadcast_to([P, NJ, 2]), ALU.add), f"modT{m}")

            def modulation_of_parts(m):
                bk = banks.read(dve, f"modT{m}")
                parts = bk[:, 0:4 * NJ].rearrange("p (j s) -> p j s", s=4)
                after(tt(mod[:, m, :, :], parts[:, :, 0:2], b_ada[:, m, :].unsqueeze(2).broadcast_to([P, NJ, 2]), ALU.add))
                banks.emptied(tt(mod[:, m, :, :], mod[:, m, :, :], parts[:, :, 2:4], ALU.add), f"modT{m}")

            def scaled_to_one(stage):
                banks.wait_emptied(dve, stage)
                after(nc.vector.reciprocal(rstd[:, :], rms[:, :]))
                after(tt(h[:, :, :], x[:, :, :], rstd[:, :].unsqueeze(1).broadcast_to([P, NJ, TOK]), ALU.mult))

            def modulated(m):
                for j in range(NJ):
                    for s in range(2):
                        last = ts(h[:, j, SPAN[s]], h[:, j, SPAN[s]], gain[:, j, s:s + 1], mod[:, m, j, s:s + 1], ALU.mult, ALU.add)
                    last.then_inc(h_ready.sem, 1)

            def low_units(l, units):
                for u in units:
                    dve.wait_ge(w_hi_ready.sem, w_hi_ready.at(l, u + 1))
                    low_part(w_lo[u % 2][:, :], unit_src(u), w_hi[u % 2][:, :]).then_inc(w_lo_ready.sem, 1)

            def gain_of(m, gi):
                return stt(gain[:, :, :], mod[:, m, :, :], 1.0, norm_g[:, gi, :].unsqueeze(2).broadcast_to([P, NJ, 2]), ALU.add, ALU.mult)

            def low_part(lo, full, hi):
                return tt(lo, full, hi.bitcast(F32), ALU.subtract)

            def gated_residual(stage, m):
                for j in range(NJ):
                    bk = banks.read(dve, stage, j)
                    for s in range(2):
                        last = stt(x[:, j, SPAN[s]], bk[:, SPAN[s]], mod[:, m, j, s:s + 1], x[:, j, SPAN[s]], ALU.mult, ALU.add)
                    banks.emptied(last, stage, j)

            with dve.Fori(0, DEPTH) as l:
                order.enter("layer", l)
                banks.enter("layer", l)
                after(copy(lb[:, :], lb_all[:, l, :]))
                after(ts(om[:, :], lb[:, :], -1.0, 1.0, ALU.mult, ALU.add))
                low_units(l, range(0, 2))
                scaled_to_one("ms1")
                dve.wait_ge(mod_params_in, l * 32 + 32)
                modulation(0)
                low_units(l, range(2, 4))
                modulation_of_parts(1)
                banks.wait_emptied(dve, "modT1")
                after(gain_of(1, 0))
                modulated(0)
                low_units(l, range(4, 5))
                for j in range(NJ):
                    dve.wait_ge(h_hi_ready.sem, h_hi_ready.at(l, j + 1))
                    low_part(h_lo[:, j, :], h[:, j, :], h_hi[:, j, :]).then_inc(h_lo_ready.sem, 1)
                low_units(l, range(5, 8))
                dve.wait_ge(params_in, l * (16 * NPARAM) + 16 * NPARAM)
                after(tt(lam_p[:, :, :], lambdas[:, 0:4:2, :], lambdas[:, 1:4:2, :], ALU.mult))
                red(lam_s[:, :], lam_p[:, :, :], AX.X, ALU.add).then_inc(lam_sum.sem, 1)
                after(ts(attn_g[:, :], attn_g[:, :], lam_init[:, 1:2], None, ALU.mult))
                low_units(l, range(8, 9))
                modulation(2)
                low_units(l, range(9, 12))

                for t in range(NTILE):
                    bk = banks.read(dve, "v", t)
                    banks.emptied(copy(val[:, t, :], bk[:, :]), "v", t)
                low_units(l, range(12, NUNIT))

                for i in range(2):
                    banks.wait_emptied(dve, "hq", i)
                after(ts(hqT[:, :, :], hqT[:, :, :], HK ** -0.5, None, ALU.mult))
                for t in range(NTILE):
                    banks.wait_emptied(dve, "hif", t)
                    banks.wait_emptied(dve, "hbg", t)
                over_tiles = lambda ap: ap.unsqueeze(1).broadcast_to([P, NTILE, 2 * HW])
                after(tt(logf[:, :, :], logf[:, :, :], over_tiles(om[:, :]), ALU.mult))
                after(tt(logf[:, :, :], logf[:, :, :], over_tiles(lb[:, :]), ALU.add))
                ts(logf[:, :, :], logf[:, :, :], LOG_DECAY_FLOOR, None, ALU.max).then_inc(fgate_ready.sem, 1)
                tt(kk[:, :, :], kk[:, :, :], over_tiles(om[:, :]), ALU.mult).then_inc(kk_ready.sem, 1)

                over_heads = lambda ap: ap.unsqueeze(1).broadcast_to([P, 2, TOK - P])
                for stage, dst in (("rotq", qT), ("rotk", kT)):
                    for i in range(2):
                        heads = dst[:, 2 * i:2 * i + 2, P:TOK]
                        bk = banks.read(dve, stage, i)
                        banks.emptied(tt(rot_t[:, :, :], bk[:, :].rearrange("p (a t) -> p a t", a=2), over_heads(const("sin")), ALU.mult), stage, i)
                        after(tt(heads, heads, over_heads(const("cos")), ALU.mult))
                        banks.wait_emptied(dve, stage, i)
                        last = tt(heads, heads, rot_t[:, :, :], ALU.add)
                        if stage == "rotk" and i == 1:
                            last.then_inc(rope_done.sem, 1)
                        else:
                            after(last)

                for i, tiles in enumerate(((0, 0), (1, 2))):
                    banks.wait_emptied(dve, "past", i)
                    for d, t in enumerate(tiles):
                        last = tt(kdec[:, 2 * i + d, :], kdec[:, 2 * i + d, :], kk[:, t, d * HW:(d + 1) * HW], ALU.mult)
                last.then_inc(kdec_ready.sem, 1)
                dve.wait_ge(ecum_ready.sem, ecum_ready.at(l, 1))
                copy(edge[:, 0:2], qdec[:, 0:2, 2 * P - 1])
                after(copy(edge[:, 2:4], qdec[:, 2:4, 2 * P]))
                qd = qdec[:, :, :].rearrange("p (d c) t -> p d (c t)", d=2)
                tt(qd, qd, hqT[:, :, :].rearrange("p c t -> p (c t)").unsqueeze(1).broadcast_to([P, 2, 2 * TOK]), ALU.mult)\
                    .then_inc(qdec_ready.sem, 1)

                def masked(n):
                    d = 1 if n == NLEV - 1 else 0
                    if n > 0:
                        banks.wait_emptied(dve, "lev", 2 * NTILE * n - 1)
                    for t in range(NTILE):
                        for odd in range(2):
                            use = (n * NTILE + t) * 2 + odd
                            bk = banks.read(dve, "lev", use)
                            apart(dve)
                            ins = nc.vector.copy_predicated(aT[:, d, t, :].rearrange("p (a b t) -> p a b t", a=2, b=2)[:, :, odd, :],
                                                            masks[:, n, :].unsqueeze(1).broadcast_to([P, 2, P]),
                                                            bk[:, 0:2 * P].rearrange("p (a t) -> p a t", a=2))
                            banks.emptied(ins, "lev", use)

                def less_middle(n):
                    w = HALVES[n] if n < CUTS else BASE // 2
                    blocks = lambda ap: flat(ap).rearrange("p (b w) -> p b w", w=2 * w)
                    nb = 2 * TOK // (2 * w)
                    for k, d in enumerate(range(2) if n < CUTS else (n - CUTS,)):
                        cd = blocks(cum[:, 2 * d:2 * d + 2, :])
                        at = w - 1 if d == 0 else w
                        last = tt(blocks(diff[:, 2 * k:2 * k + 2, :]), cd, cd[:, :, at:at + 1].broadcast_to([P, nb, 2 * w]), ALU.subtract)
                    last.then_inc(diff_ready.sem, 1)

                less_middle(0)
                for n in range(NLEV):
                    dve.wait_ge(fac_ready.sem, fac_ready.at(l, n + 1))
                    ks, qs = key_side[:, n % 2, :, :], query_side[:, n % 2, :, :]
                    if n < CUTS:
                        w = HALVES[n]
                        half = lambda ap, k, w=w: flat(ap).rearrange("p (b w) -> p b w", w=2 * w)[:, :, k * w:(k + 1) * w]
                        for k in range(2):
                            tt(half(ks, k), half(kkT[:, 2 * k:2 * k + 2, :], k), half(diff[:, 2 * k:2 * k + 2, :], k), ALU.mult)
                            o = 1 - k
                            last = tt(half(qs, k), half(hqT[:, :, :], k), half(diff[:, 2 * o:2 * o + 2, :], k), ALU.mult)
                    else:
                        d = n - CUTS
                        tt(flat(qs), flat(hqT[:, :, :]), flat(diff[:, 0:2, :]), ALU.mult)
                        last = tt(flat(ks), flat(kkT[:, 2 * d:2 * d + 2, :]), flat(inverse), ALU.mult)
                    last.then_inc(pair_ready.sem, 1)
                    if n + 1 < NLEV:
                        dve.wait_ge(pair_ready.sem, pair_ready.at(l, n + 1))
                        less_middle(n + 1)
                    if n == 0:
                        dve.wait_ge(aT_zero.sem, aT_zero.at(l, 1))
                    else:
                        masked(n - 1)
                    if n == 1:
                        modulation(3)
                masked(NLEV - 1)
                banks.wait_emptied(dve, "lev", 2 * NTILE * NLEV - 1)
                tt(aT[:, 0, :, :], aT[:, 0, :, :], aT[:, 1, :, :], ALU.add).then_inc(pairs_summed.sem, 1)

                bk = banks.read(dve, "st", 0)
                sv = bk[:, :].rearrange("p (g n) -> p g n", g=4)
                copy(st_out[0:HK, :, :], sv[0:HK, :, 0:HK])
                banks.emptied(copy(st_out[HK:P, :, :], sv[HK:P, :, HK:P]), "st", 0)
                after(tt(st_mid[:, :, :], state0[:, :, :], edge[:, :].unsqueeze(2).broadcast_to([P, 4, HK]), ALU.mult))
                bk = banks.read(dve, "st", 1)
                sv = bk[:, :].rearrange("p (g n) -> p g n", g=4)
                tt(st_mid[0:HK, :, :], st_mid[0:HK, :, :], sv[0:HK, :, 0:HK], ALU.add)
                banks.emptied(tt(st_mid[HK:P, :, :], st_mid[HK:P, :, :], sv[HK:P, :, HK:P], ALU.add), "st", 1)

                dve.wait_ge(lam_exp.sem, lam_exp.at(l, 1))
                after(stt(neg_lam[:, :], lam_s[:, 1:2], lam_s[:, 0:1], lam_init[:, 0:1], ALU.subtract, ALU.subtract))

                for u in range(NU + 1):
                    if u < NU:
                        nk = P if UNITS[u][0] == 0 else KEYS - P
                        for m in range(2):
                            bk = banks.read(dve, "sc", 2 * u + m)
                            last = red(top[:, u % 2, m:m + 1], bk[:, 0:nk], AX.X, ALU.max)
                        after(last)
                        ts(ntop[:, u % 2, :], top[:, u % 2, :], -SCALE, None, ALU.mult).then_inc(ntop_ready.sem, 1)
                    if u >= 1:
                        v = u - 1
                        nk = P if UNITS[v][0] == 0 else KEYS - P
                        for m in range(2):
                            banks.wait_emptied(dve, "sc", 2 * v + m)
                        after(nc.vector.reciprocal(rden[:, v % 2, :], den[:, v % 2, :]))
                        after(tt(rden[:, v % 2, 1:2], rden[:, v % 2, 1:2], neg_lam[:, :], ALU.mult))
                        if v >= 2:
                            banks.read(dve, "wT", v - 2)
                        after(ts(wts[:, v % 2, 0:nk], prob[:, v % 2, 0, 0:nk], rden[:, v % 2, 0:1], None, ALU.mult))
                        stt(wts[:, v % 2, 0:nk], prob[:, v % 2, 1, 0:nk], rden[:, v % 2, 1:2], wts[:, v % 2, 0:nk], ALU.mult, ALU.add)\
                            .then_inc(wts_ready.sem, 1)

                for t in range(NTILE):
                    banks.wait_emptied(dve, "o", t)
                for odd in range(2):
                    banks.wait_emptied(dve, "ho", odd)
                heads_a = lambda ap: ap.rearrange("p i (a d) -> p (i a) d", a=DH)
                heads_h = lambda ap: ap.rearrange("p i (a d) -> p (i a) d", a=HH)
                red(att_r[:, 0, :], heads_a(att_sq), AX.X, ALU.add)
                red(ho_r[:, 0, :], heads_h(ho_sq[:, :, :]), AX.X, ALU.add).then_inc(sums_ready.sem, 1)
                dve.wait_ge(roots_ready.sem, roots_ready.at(l, 1))
                nc.vector.reciprocal(att_r[:, 0, :], att_r[:, 1, :])
                after(nc.vector.reciprocal(ho_r[:, 0, :], ho_r[:, 1, :]))
                after(tt(heads_a(att[:, :, :]), heads_a(att[:, :, :]), att_r[:, 0, :].unsqueeze(2).broadcast_to([P, NTILE * DH, VD]), ALU.mult))
                tt(heads_a(att[:, :, :]), heads_a(att[:, :, :]), attn_g[:, :].unsqueeze(1).broadcast_to([P, NTILE * DH, VD]), ALU.mult)\
                    .then_inc(anorm_ready.sem, 1)
                after(tt(heads_h(ho[:, :, :]), heads_h(ho[:, :, :]), ho_r[:, 0, :].unsqueeze(2).broadcast_to([P, NTILE * HH, HK]), ALU.mult))
                after(tt(heads_h(ho[:, :, :]), heads_h(ho[:, :, :]), hg_g[:, :].unsqueeze(1).broadcast_to([P, NTILE * HH, HK]), ALU.mult))
                tt(gate_o[:, :, :], gate_o[:, :, :], ho[:, :, :], ALU.mult).then_inc(hnorm_ready.sem, 1)

                dve.wait_ge(gu_hi_ready.sem, gu_hi_ready.at(l, 1))
                low_part(gu_lo[:, 0, :], w_shared[:, 0:2 * D], gu_hi[:, 0, :]).then_inc(gu_lo_ready.sem, 1)
                dve.wait_ge(dn_hi_ready.sem, dn_hi_ready.at(l, 1))
                low_part(dn_lo[:, 0, :], w_shared[:, 2 * D:3 * D], dn_hi[:, 0, :]).then_inc(dn_lo_ready.sem, 1)

                modulation(4)
                banks.wait_emptied(dve, "modT4")
                gated_residual("out", 2)
                gain_of(4, 1).then_inc(x_ready.sem, 1)
                dve.wait_ge(x_ready.sem, x_ready.at(l, 1))
                scaled_to_one("ms2")
                modulated(3)

                dve.wait_ge(h_hi_ready.sem, h_hi_ready.at(l, 2 * NJ))
                low_part(h_lo_late[:, :, :], h[:, :, :], h_hi[:, :, :]).then_inc(h_lo_ready.sem, 1)

                banks.wait_emptied(dve, "router")
                after(tt(biased[:, :, :], score[:, :, :], r_bias[:, :].unsqueeze(1).broadcast_to([P, NTILE, E]), ALU.add))
                apart(dve)
                for t in range(NTILE):
                    for g in range(NG):
                        last = nc.vector.max(tops[:, t * NG + g, :], biased[:, t, g * PG:(g + 1) * PG])
                after(last)
                gs = gsum[:, :, :]
                after(tt(gs.rearrange("p i g -> p (i g)"), tops[:, :, 0], tops[:, :, 1], ALU.add))
                other = gs.unsqueeze(2).broadcast_to([P, NTILE, NG, NG])
                own = gs.unsqueeze(3).broadcast_to([P, NTILE, NG, NG])
                sq4 = lambda ap: ap.rearrange("p i (a b) -> p i a b", a=NG)
                tt(sq4(cmp_a[:, :, :]), other, own, ALU.is_gt)
                after(tt(sq4(cmp_b[:, :, :]), other, own, ALU.is_equal))
                after(tt(cmp_b[:, :, :], cmp_b[:, :, :], const("tie").unsqueeze(1).broadcast_to([P, NTILE, NG * NG]), ALU.mult))
                after(tt(cmp_a[:, :, :], cmp_a[:, :, :], cmp_b[:, :, :], ALU.add))
                after(red(rank[:, :], cmp_a[:, :, :].rearrange("p i (a b) -> p (i a) b", a=NG), AX.X, ALU.add))
                after(ts(rank[:, :], rank[:, :], float(TOPK_GROUPS), None, ALU.is_lt))
                after(ts(gpen[:, :], rank[:, :], NEVER, -NEVER, ALU.mult, ALU.add))
                grouped = biased[:, :, :].rearrange("p i (g k) -> p (i g) k", g=NG)
                wide = lambda ap: ap.unsqueeze(2).broadcast_to([P, NTILE * NG, PG])
                after(tt(grouped, grouped, wide(rank[:, :]), ALU.mult))
                after(tt(grouped, grouped, wide(gpen[:, :]), ALU.add))
                apart(dve)
                for t in range(NTILE):
                    last = nc.vector.max(best[:, t, :], biased[:, t, :])
                after(last)
                apart(dve)
                for t in range(NTILE):
                    last = nc.vector.match_replace(gsel[:, t, :], best[:, t, :], biased[:, t, :], TAKEN)
                after(last)
                after(ts(gsel[:, :, :], gsel[:, :, :], NEVER * 1.05, None, ALU.is_gt))
                after(tt(gsel[:, :, :], gsel[:, :, :], score[:, :, :], ALU.mult))
                after(red(wsum[:, :], gsel[:, :, :], AX.X, ALU.add))
                after(nc.vector.reciprocal(wsum[:, :], wsum[:, :]))
                after(ts(wsum[:, :], wsum[:, :], ROUTED_SCALE, None, ALU.mult))
                tt(gsel[:, :, :], gsel[:, :, :], wsum[:, :].unsqueeze(2).broadcast_to([P, NTILE, E]), ALU.mult).then_inc(gsel_ready.sem, 1)

                dve.wait_ge(gu_hi_ready.sem, gu_hi_ready.at(l, 2))
                low_part(gu_lo[:, 1, :], ring[:, 0, 0:2 * D], gu_hi[:, 1, :]).then_inc(gu_lo_ready.sem, 1)

                def dve_step(n, buf, gates, e_mod, has_gu, has_dn):
                    banks.wait_emptied(dve, "G", 0, n)
                    bk = banks.read(dve, "U", 0, n)
                    banks.emptied(tt(sil[:, buf, :], sil[:, buf, :], bk[:, 0:TOK], ALU.mult), "U")
                    banks.wait_emptied(dve, "U", 0, n)
                    if gates is None:
                        copy(act[:, buf, :], sil[:, buf, :]).then_inc(act_ready.sem, 1)
                    else:
                        tt(act[:, buf, :], sil[:, buf, :], gates, ALU.mult).then_inc(act_ready.sem, 1)
                    dve.wait_ge(act_hi_ready.sem, l * VIS + n + 1)
                    low_part(act_lo[:, buf, :], act[:, buf, :], act_hi[:, buf, :]).then_inc(act_lo_ready.sem, 1)
                    if has_gu:
                        slot = (e_mod + 1) % NSLOT
                        dve.wait_ge(gu_hi_ready.sem, l * VIS + n + 3)
                        low_part(gu_lo[:, buf, :], ring[:, slot, 0:2 * D], gu_hi[:, buf, :]).then_inc(gu_lo_ready.sem, 1)
                    if has_dn:
                        slot = e_mod % NSLOT
                        dve.wait_ge(dn_hi_ready.sem, l * VIS + n + 2)
                        low_part(dn_lo[:, 1 - buf, :], ring[:, slot, 2 * D:3 * D], dn_hi[:, 1 - buf, :]).then_inc(dn_lo_ready.sem, 1)

                modulation(5)
                bk = banks.read(dve, "gT")
                banks.emptied(copy(gatesT[:, :], bk[0:E, 0:TOK]), "gT")
                dve_step(0, 0, None, 0, True, True)

                def eight(turn, last):
                    for i in range(2):
                        dve.wait_ge(gate_in[i], l * (16 * E // (2 * GSLOT)) + turn * 16 + 16)
                        for s in range(GSLOT):
                            k = i * GSLOT + s
                            dve_step(turn * 8 + (k + 1), (k + 1) % 2, gate_b[:, i, s, :], k + 1, not last or k < 6, not last or k < 7)

                with dve.Fori(0, E // 8 - 1) as turn:
                    eight(turn, False)
                eight(E // 8 - 1, True)
                dve.wait_ge(dn_lo_ready.sem, l * VIS + VIS)
                dve.sem_inc(slots_idle.sem, 1)
                for t in range(NTILE):
                    bk = banks.read(dve, "y", 2 * t + 1)
                    banks.emptied(copy(rows[:, t, 512:1024], bk[:, :]), "y", 2 * t + 1)
                gated_residual("yT", 5)
                nc.vector.memset(tick[:, :], 0.0).then_inc(x_ready.sem, 1)
                order.leave()

            order.enter("final")
            banks.enter("final")
            dve.wait_ge(token_sums, 1)
            tt(token_r[:, 1, :], mean_sq[:, :, 0], mean_sq[:, :, 1], ALU.add).then_inc(token_mean, 1)
            dve.wait_ge(token_root, 1)
            after(nc.vector.reciprocal(token_r[:, 1, :], token_r[:, 0, :]))
            dve.wait_ge(final_g_in, 16)
            for t in range(NTILE):
                for half in range(2):
                    bk = banks.read(dve, "rows", 2 * t + half)
                    of_half = lambda ap: ap.rearrange("p (q j) -> p j q", j=NJ)[:, 4 * half:4 * half + 4, :]
                    banks.emptied(stt(of_half(rows[:, t, :]), bk[:, :].rearrange("p (j q) -> p j q", j=4), token_r[:, 1, t:t + 1],
                                      of_half(final_g), ALU.mult, ALU.mult), "rows", 2 * t + half)


_INS = ["x_prompt", "x_sample", "cache_k", "cache_v", "state_hgrn", "c", "c_ctx", "w_ada", "b_ada", "norm_g", "w_in",
        "w_fourier", "lambdas", "attn_norm_g", "lower_bounds", "hg_norm_g", "w_out", "w_router", "router_bias",
        "w_gate", "w_up", "w_down", "ws_gate", "ws_up", "ws_down", "final_g"]


def shape_constants(depth):
    import numpy as np

    i = np.arange(P)
    out = {"ident": np.eye(P), "tri_f": i[:, None] <= i[None, :], "tri_b": i[:, None] >= i[None, :],
           "past_f": i[:, None] > i[None, :], "past_b": i[:, None] < i[None, :]}
    rot = np.zeros((P, P))
    for a in range(0, P, 32):
        for k in range(16):
            rot[a + 16 + k, a + k] = -1.0
            rot[a + k, a + 16 + k] = 1.0
    out["rot"] = rot
    for name, n in (("ctx", 128), ("lat", 256)):
        k = np.arange(n)
        ang = 2 * np.pi * ((k[:, None] * k[None, :]) % n) / n
        for c, m in (("c", np.cos(ang)), ("s", np.sin(ang))):
            out[f"{c}_{name}"] = (m / np.sqrt(n * 64.0)).reshape(n // P, P, n).transpose(1, 0, 2).reshape(P, -1)
    k = np.arange(64)
    ang = 2 * np.pi * ((k[:, None] * k[None, :]) % 64) / 64
    out["c_chan"] = np.kron(np.eye(2), np.cos(ang))
    out["s_chan"] = -np.kron(np.eye(2), np.sin(ang))
    t = np.arange(256)
    inv = (10000.0 ** (-np.arange(0, 32, 2) / 32.0)).astype(np.float32)
    row, col = (t // 64)[None, :] * inv[:, None], (t % 64)[None, :] * inv[:, None]
    ang = np.concatenate([row, row, col, col] * 2, 0)
    out["cos"], out["sin"] = np.cos(ang), np.sin(ang)
    g = np.arange(8)
    out["tie"] = np.broadcast_to((g[None, :] < g[:, None]).reshape(1, 64), (P, 64))
    packed = np.concatenate([np.asarray(out[name], np.float32) for name, _ in CONST_COLS], 1)

    def pair_masks(d):
        s, t = (i[:, None], i[None, :]) if d == 0 else (P - 1 - i[:, None], P - 1 - i[None, :])
        return [(s // (2 * w) == t // (2 * w)) & (s % (2 * w) < w) & (t % (2 * w) >= w) for w in HALVES] + \
               [(s // BASE == t // BASE) & (s <= t)]

    fwd, bwd = pair_masks(0), pair_masks(1)
    masks = [f | b for f, b in zip(fwd[:-1], bwd[:-1])] + [fwd[-1], bwd[-1]]
    init = np.array([0.8 - 0.6 * np.exp(-0.3 * n) for n in range(depth)])
    lam = np.stack([init, 1.0 - init], 1).astype(np.float32)
    return packed, np.stack(masks).astype(np.float32), lam


def kernel(**inputs):
    import numpy as np
    import concourse.bacc as bacc
    from concourse.bass_utils import run_bass_kernel_spmd

    nc = bacc.Bacc("TRN2", target_bir_lowering=False, num_devices=1, dynamic_dma_scratch_size=4096)
    arrays = {name: np.ascontiguousarray(inputs[name]) for name in _INS}
    depth, past, heads, kd = arrays["cache_k"].shape[1:]
    arrays["const_f"], arrays["const_m"], arrays["lam_init"] = shape_constants(depth)
    T = {name: nc.dram_tensor("in_" + name, a.shape, mybir.dt.from_np(a.dtype), kind="ExternalInput").ap()
         for name, a in arrays.items()}
    seq = arrays["x_prompt"].shape[1]
    shapes = {"y_prompt": arrays["x_prompt"].shape, "y_sample": arrays["x_sample"].shape,
              "new_k": (1, depth, seq, heads, kd), "new_v": (1, depth, seq, heads, arrays["cache_v"].shape[4]),
              "new_state": arrays["state_hgrn"].shape}
    outs = {name: nc.dram_tensor("out_" + name, shape, F32, kind="ExternalOutput").ap() for name, shape in shapes.items()}
    trunk_program(nc, T, T["const_f"], T["const_m"], *outs.values())
    r = run_bass_kernel_spmd(nc, [{"in_" + name: a for name, a in arrays.items()}], core_ids=[0])
    return tuple(r.results[0]["out_" + name] for name in shapes)
```
